# Optimizing a Trainium2 kernel written in Bass

```python
import math
import jax, jax.numpy as jnp
from jax import lax
import numpy as np

D_MODEL = 1024
BATCH = 1
SEQ = 1024
DEPTH = 1
DEC_BATCH = 8
DEC_SEQ = 8
PAST_LEN = 8192
PAGE_SIZE = 128

POOL_WINDOWS = (2, 4, 8, 16)
POOL_GROUPS = len(POOL_WINDOWS)
POOL_GROUP_DIM = D_MODEL // 8
POOL_WIDTH = POOL_GROUPS * POOL_GROUP_DIM
POOL_HIST = max(POOL_WINDOWS) - 1
ML_HEADS = 4
ML_WIDTH = D_MODEL
ML_HEAD_DIM = ML_WIDTH // ML_HEADS
ML_CHUNK = 64
M_INIT = -1e30
D_FF = ((8 * D_MODEL + 3 * 256 - 1) // (3 * 256)) * 256
EPS = 1e-6
IN_WIDTHS = (POOL_WIDTH, ML_WIDTH, ML_WIDTH, ML_WIDTH, ML_WIDTH, ML_HEADS, ML_HEADS, D_MODEL, D_MODEL)
N_IN = sum(IN_WIDTHS)
IN_SPLITS = tuple(sum(IN_WIDTHS[:i + 1]) for i in range(len(IN_WIDTHS) - 1))

kernel_name = "hybrid_pool_mlstm_adaln_decode_step"

def rmsnorm(x, g):
    xf = x.astype(jnp.float32)
    y = xf * lax.rsqrt(jnp.mean(xf * xf, axis=-1, keepdims=True) + EPS)
    return (y * g.astype(jnp.float32)).astype(x.dtype)

def pool_mixer(u, hist, pos0, w_pool, s_pool):
    B, T, _ = u.shape
    ext = jnp.concatenate([hist, u], axis=1)
    ef = ext.astype(jnp.float32)
    cs = jnp.concatenate([jnp.zeros_like(ef[:, :1]), jnp.cumsum(ef, axis=1)], axis=1)
    end = cs[:, POOL_HIST + 1:]
    pos = pos0 + jnp.arange(T)
    means = []
    for g, w in enumerate(POOL_WINDOWS):
        sl = slice(g * POOL_GROUP_DIM, (g + 1) * POOL_GROUP_DIM)
        start = cs[:, POOL_HIST + 1 - w: POOL_HIST + 1 - w + T, sl]
        cnt = jnp.minimum(pos + 1, w).astype(jnp.float32)[None, :, None]
        means.append((end[..., sl] - start) / cnt)
    mean = jnp.concatenate(means, axis=-1)
    d = (mean - u.astype(jnp.float32)).astype(u.dtype).reshape(B, T, POOL_GROUPS, POOL_GROUP_DIM)
    y = jnp.einsum('btgc,gcd->btgd', d, w_pool).reshape(B, T, POOL_WIDTH) * s_pool
    return y, ext[:, -POOL_HIST:]

def mlstm_chunk(carry, xs):
    C, n, m = carry
    q, k, v, ig, lf = xs
    L = q.shape[2]
    b = jnp.cumsum(lf, axis=-1)
    causal = jnp.tril(jnp.ones((L, L), dtype=bool))
    logd = jnp.where(causal, b[..., :, None] - b[..., None, :] + ig[..., None, :], -jnp.inf)
    a = b + m[..., None]
    m_t = jnp.maximum(a, jnp.max(logd, axis=-1))
    w_intra = jnp.exp(logd - m_t[..., None])
    w_inter = jnp.exp(a - m_t)
    s = jnp.einsum('bhtd,bhsd->bhts', q, k) * w_intra
    num = w_inter[..., None] * jnp.einsum('bhtd,bhde->bhte', q, C) + jnp.einsum('bhts,bhse->bhte', s, v)
    den = w_inter * jnp.einsum('bhtd,bhd->bht', q, n) + jnp.sum(s, axis=-1)
    h = num / jnp.maximum(jnp.abs(den), jnp.exp(-m_t))[..., None]
    m_new = m_t[..., -1]
    decay = jnp.exp(a[..., -1] - m_new)
    w_end = jnp.exp(b[..., -1:] - b + ig - m_new[..., None])
    C_new = decay[..., None, None] * C + jnp.einsum('bhs,bhsd,bhse->bhde', w_end, k, v)
    n_new = decay[..., None] * n + jnp.einsum('bhs,bhsd->bhd', w_end, k)
    return (C_new, n_new, m_new), h

def mlstm_mixer(q, k, v, ig, lf, C0, n0, m0):
    B, T = q.shape[:2]
    L = math.gcd(T, ML_CHUNK)
    nc = T // L

    def to_chunks(z):
        z = z.reshape((B, nc, L) + z.shape[2:])
        return jnp.transpose(z, (1, 0, 3, 2) + tuple(range(4, z.ndim)))

    xs = (to_chunks(q), to_chunks(k), to_chunks(v), to_chunks(ig), to_chunks(lf))
    (C1, n1, m1), h = lax.scan(mlstm_chunk, (C0, n0, m0), xs)
    h = jnp.transpose(h, (1, 0, 3, 2, 4)).reshape(B, T, ML_HEADS, ML_HEAD_DIM)
    return h, C1, n1, m1

def layer_forward(x, c, pool_hist, C0, n0, m0, pos0, g_mix, g_ffn, w_ada, b_ada, w_in, b_igate, b_fgate,
                  w_pool, s_pool, g_head, w_bp, w_bm, w_out, w_gu, w_down):
    B, T, _ = x.shape
    f32 = jnp.float32
    mod = (jax.nn.silu(c) @ w_ada + b_ada)[:, None, :]
    sh1, sc1, gt1, sh2, sc2, gt2 = jnp.split(mod, 6, axis=-1)
    h = rmsnorm(x, g_mix) * (1 + sc1) + sh1
    z = h @ w_in
    u, q, k, v, o, ig, fg, gp, gm = jnp.split(z, IN_SPLITS, axis=-1)
    y_pool, new_hist = pool_mixer(u, pool_hist, pos0, w_pool, s_pool)
    hd = (B, T, ML_HEADS, ML_HEAD_DIM)
    qf = q.reshape(hd).astype(f32)
    kf = k.reshape(hd).astype(f32) * (ML_HEAD_DIM ** -0.5)
    vf = v.reshape(hd).astype(f32)
    igf = ig.astype(f32) + b_igate.astype(f32)
    lff = jax.nn.log_sigmoid(fg.astype(f32) + b_fgate.astype(f32))
    hm, C1, n1, m1 = mlstm_mixer(qf, kf, vf, igf, lff, C0, n0, m0)
    hm = hm * lax.rsqrt(jnp.mean(hm * hm, axis=-1, keepdims=True) + EPS)
    y_ml = (hm.reshape(B, T, ML_WIDTH) * g_head.astype(f32)).astype(x.dtype) * jax.nn.sigmoid(o)
    merged = jax.nn.sigmoid(gp) * (y_pool @ w_bp) + jax.nn.sigmoid(gm) * (y_ml @ w_bm)
    x = x + gt1 * (merged @ w_out)
    h2 = rmsnorm(x, g_ffn) * (1 + sc2) + sh2
    gate, up = jnp.split(h2 @ w_gu, 2, axis=-1)
    x = x + gt2 * ((jax.nn.silu(gate) * up) @ w_down)
    return x, new_hist, C1, n1, m1

def setup_inputs(seed: int = 0) -> dict:
    key = jax.random.key(seed)
    ks = jax.random.split(key, 32)
    nrm = lambda i, shape, s=1.0: jax.random.normal(ks[i], shape, jnp.float32) * s
    D, H, DK = D_MODEL, ML_HEADS, ML_HEAD_DIM
    return {
        "x_prompt": nrm(0, (BATCH, SEQ, D)),
        "x_sample": nrm(1, (DEC_BATCH, DEC_SEQ, D)),
        "c_prompt": nrm(2, (BATCH, D)),
        "c_sample": nrm(3, (DEC_BATCH, D)),
        "state_pool": nrm(4, (DEPTH, DEC_BATCH, POOL_HIST, POOL_WIDTH)),
        "state_mlstm_c": nrm(5, (DEPTH, DEC_BATCH, H, DK, DK), 0.5),
        "state_mlstm_n": nrm(6, (DEPTH, DEC_BATCH, H, DK), 0.5),
        "state_mlstm_m": nrm(7, (DEPTH, DEC_BATCH, H)),
        "g_mix": 1.0 + nrm(8, (DEPTH, D), 0.02),
        "g_ffn": 1.0 + nrm(9, (DEPTH, D), 0.02),
        "g_final": 1.0 + nrm(10, (D,), 0.02),
        "w_ada": nrm(11, (DEPTH, D, 6 * D), 0.5 * D ** -0.5),
        "b_ada": nrm(12, (DEPTH, 6 * D), 0.02),
        "w_in": nrm(13, (DEPTH, D, N_IN), D ** -0.5),
        "b_igate": nrm(14, (DEPTH, H), 0.1),
        "b_fgate": jnp.linspace(3.0, 6.0, H, dtype=jnp.float32)[None, :] + nrm(15, (DEPTH, H), 0.1),
        "w_pool": nrm(16, (DEPTH, POOL_GROUPS, POOL_GROUP_DIM, POOL_GROUP_DIM), POOL_GROUP_DIM ** -0.5),
        "s_pool": 0.5 + nrm(17, (DEPTH, POOL_WIDTH), 0.1),
        "g_head": 1.0 + nrm(18, (DEPTH, ML_WIDTH), 0.02),
        "w_branch_pool": nrm(19, (DEPTH, POOL_WIDTH, D), POOL_WIDTH ** -0.5),
        "w_branch_mlstm": nrm(20, (DEPTH, ML_WIDTH, D), ML_WIDTH ** -0.5),
        "w_out": nrm(21, (DEPTH, D, D), D ** -0.5),
        "w_gate_up": nrm(22, (DEPTH, D, 2 * D_FF), D ** -0.5),
        "w_down": nrm(23, (DEPTH, D_FF, D), D_FF ** -0.5),
    }

def reference(x_prompt, x_sample, c_prompt, c_sample, state_pool, state_mlstm_c, state_mlstm_n, state_mlstm_m,
              g_mix, g_ffn, g_final, w_ada, b_ada, w_in, b_igate, b_fgate, w_pool, s_pool, g_head,
              w_branch_pool, w_branch_mlstm, w_out, w_gate_up, w_down):
    f32 = jnp.float32
    B = x_prompt.shape[0]
    xp, xs = x_prompt, x_sample
    pool_p, c_p, n_p, m_p = [], [], [], []
    pool_s, c_s, n_s, m_s = [], [], [], []
    for l in range(DEPTH):
        w = (g_mix[l], g_ffn[l], w_ada[l], b_ada[l], w_in[l], b_igate[l], b_fgate[l], w_pool[l], s_pool[l],
             g_head[l], w_branch_pool[l], w_branch_mlstm[l], w_out[l], w_gate_up[l], w_down[l])
        hist0 = jnp.zeros((B, POOL_HIST, POOL_WIDTH), xp.dtype)
        C0 = jnp.zeros((B, ML_HEADS, ML_HEAD_DIM, ML_HEAD_DIM), f32)
        n0 = jnp.zeros((B, ML_HEADS, ML_HEAD_DIM), f32)
        m0 = jnp.full((B, ML_HEADS), M_INIT, f32)
        xp, hp, cp, np_, mp = layer_forward(xp, c_prompt, hist0, C0, n0, m0, 0, *w)
        xs, hs, cs, ns, ms = layer_forward(
            xs, c_sample, state_pool[l], state_mlstm_c[l].astype(f32), state_mlstm_n[l].astype(f32),
            state_mlstm_m[l].astype(f32), PAST_LEN, *w)
        pool_p.append(hp); c_p.append(cp.astype(state_mlstm_c.dtype))
        n_p.append(np_.astype(state_mlstm_n.dtype)); m_p.append(mp.astype(state_mlstm_m.dtype))
        pool_s.append(hs.astype(state_pool.dtype)); c_s.append(cs.astype(state_mlstm_c.dtype))
        n_s.append(ns.astype(state_mlstm_n.dtype)); m_s.append(ms.astype(state_mlstm_m.dtype))
    y_prompt = rmsnorm(xp, g_final)
    y_sample = rmsnorm(xs, g_final)
    return (y_prompt, y_sample,
            jnp.stack(pool_p), jnp.stack(c_p), jnp.stack(n_p), jnp.stack(m_p),
            jnp.stack(pool_s), jnp.stack(c_s), jnp.stack(n_s), jnp.stack(m_s))


_drawn_inputs = setup_inputs


def setup_inputs(seed=0):
    import zlib

    import numpy as np

    out = dict(_drawn_inputs(seed))
    spreads = {}
    factors = {'g_ffn': 8.0, 'g_final': 8.604, 's_pool': 3.757, 'g_head': 27.84}
    for name, (base, spread) in spreads.items():
        noise = np.random.default_rng([zlib.crc32(name.encode()), seed]).standard_normal(out[name].shape)
        drawn = base * np.exp(spread * noise) if base else spread * noise
        out[name] = __import__('jax').numpy.asarray(drawn.astype(out[name].dtype))
    for name, factor in factors.items():
        out[name] = (out[name] * factor).astype(out[name].dtype)
    return out
```

```python
from contextlib import ExitStack

import concourse.bass as bass
from concourse import mybir

F32 = mybir.dt.float32
F32R = mybir.dt.float32r
ALU = mybir.AluOpType
ACT = mybir.ActivationFunctionType
ds = bass.ds

P = 128
D = 1024
KT = D // P
SEQ = 1024
NB, NT = 8, 8
SMP = NB * NT
T = SEQ + SMP
TT = 9
CH = ((0, 384), (384, 768), (768, T))
GRP = 1 + NB
PW = 512
PG = PW // P
HIST = 15
H = 4
HD = 256
CK = 128
NCK = SEQ // CK
HC = H * NCK
GL = CK + NT
E1 = HD + 1
FF = 2816
FT = FF // P
EPS = 1e-6
NEG = -1e30
NA = 6 * KT
V_MIX, V_FFN, V_FIN, V_HEAD, V_POOL, V_ADA = 0, 8, 16, 24, 32, 36
NV = V_ADA + NA
SH1, SC1, GT1, SH2, SC2, GT2 = (KT * j for j in range(6))
Z_U, Z_Q, Z_K, Z_V, Z_O, Z_GP, Z_GM, Z_X, Z_D = 0, 4, 12, 20, 28, 36, 44, 52, 60
GATE_COL = PW + 4 * D
U_L1, U_L2, U_BP, U_BM, U_OUT, U_FFN = 1, 29, 53, 57, 65, 73
T_SS, T_GATE, T_L1, T_L2, T_YP, T_BP, T_BM, T_OUT, T_N2, T_FFN = 8, 9, 10, 38, 62, 66, 74, 82, 90, 91
T_Y = T_FFN + 6 * FT
R_VEC, R_CT, R_ADA = 0, 1, 2
ADA0 = 20
R_L1 = R_ADA + ADA0
L1_CUTS = ((0, 2), (2, 4), (4, 6), (6, 14))
R_SEG = (R_L1, R_L1, R_L1 + 2, R_L1 + 4)
R_GATES = R_L1 + 8
R_COLS = R_L1 + 14
R_L2 = R_L1 + 32
RPC = 23
R_UT = R_L2 + NCK * RPC
R_SMP = R_UT + 2
RPH = 21
R_NOUT = R_SMP + H * RPH
R_Y = R_NOUT + 1


def last_tile(n):
    if n < U_BP:
        return n + T_GATE
    if n < U_BM:
        return T_BP + 2 * (n - U_BP) + 1
    if n < U_FFN:
        return n - U_BM + T_BM
    q, r = divmod(n - U_FFN, 6)
    return T_FFN + 12 * q + (r if r < 4 else 4 * r - 9)


def trunk(nc, x_prompt, x_sample, c_prompt, c_sample, state_pool, state_c, state_n, state_m,
          g_mix, g_ffn, g_final, w_ada, b_ada, w_in, b_igate, b_fgate, w_pool, s_pool, g_head,
          w_bp, w_bm, w_out, w_gu, w_down,
          y_prompt, y_sample, pool_p, c_p, n_p, m_p, pool_s, c_s, n_s, m_s):
    z = nc.dram_tensor("z_scratch", (64, P, T), F32).ap()
    gate_rows_p = nc.dram_tensor("gate_rows_p", (8, SEQ), F32).ap()
    gate_rows_s = nc.dram_tensor("gate_rows_s", (8, SMP), F32).ap()
    negg_dram = nc.dram_tensor("negg_rows", (HC, CK), F32).ap()
    tab_s_dram = nc.dram_tensor("tab_s", (5, HC, NT), F32).ap()
    decay_dram = nc.dram_tensor("decay_rows", (2, HC), F32).ap()

    top = ExitStack()
    with top:
        top.enter_context(nc.allow_non_contiguous_dma(reason="single columns of gates, stabilisers and normalisers"))
        def sem(name):
            return top.enter_context(nc.semaphore(name))

        def sb(stack, name, shape, dt=F32):
            return stack.enter_context(nc.sbuf_tensor(name, shape, dt))

        ident = sb(top, "ident", [P, P])
        ones = sb(top, "ones", [P, P])
        vec = sb(top, "vec", [P, NV])
        mod = sb(top, "mod", [P, NA, GRP])
        amp1 = sb(top, "amp1", [P, KT, GRP])
        amp2 = sb(top, "amp2", [P, KT, GRP])
        epsc = sb(top, "epsc", [P, 1])
        raw = sb(top, "raw", [P, 2, 1024])
        w_hi = sb(top, "w_hi", [P, 2, 1024], F32R)
        w_lo = sb(top, "w_lo", [P, 2, 1024], F32R)
        act_hi = sb(top, "act_hi", [P, KT, T], F32R)
        act_lo = sb(top, "act_lo", [P, KT, T], F32R)
        stage = sb(top, "stage", [P, 2, T])
        dec = sb(top, "dec", [P, 2, HC])
        colp = sb(top, "colp", [P, 4, HC])
        scol = sb(top, "scol", [SMP, 4, H])
        negg_s = sb(top, "negg_s", [SMP, H, SMP])
        gbias = sb(top, "gbias", [8, 1])
        mprev = sb(top, "mprev", [HC, 2])

        early = ExitStack()
        xtok = sb(early, "xtok", [P, TT, D])
        xn = xtok[:, :, :].rearrange("p j d -> p (j d)")[:, 0:KT * T].rearrange("p (k t) -> p k t", t=T)
        xT = sb(early, "xT", [P, KT, T])
        ada_w = sb(early, "ada_w", [P, 2, KT, 256])
        xsq = sb(early, "xsq", [P, T])
        xssq = sb(early, "xssq", [P, T])
        cT = sb(early, "cT", [P, KT, GRP])
        vrow = sb(early, "vrow", [NV, P])
        hrow = sb(early, "hrow", [NB * HIST, PW])
        early.close()
        h32 = stage
        cc, csig = stage[0:GRP, 0, 0:D], stage[0:GRP, 1, 0:D]
        mixer = ExitStack()
        ext_p = sb(mixer, "ext_p", [P, PG, HIST + SEQ])
        ext_s = sb(mixer, "ext_s", [P, PG, NB, HIST + NT])
        win = sb(mixer, "win", [P, 2, HIST + SEQ])
        mixer.close()
        gtab = ExitStack()
        sb(gtab, "over_xtok", [P, TT * D])
        gates = sb(gtab, "gates", [8, T])
        tab = {n: sb(gtab, "tab_" + n, [HC, GL]) for n in
               ("ig", "fg", "abs", "exp", "ln", "lf", "b", "r", "cm", "g", "negg", "mt", "winter", "emt", "wend", "wend16")}
        zeros = sb(gtab, "zeros", [HC, GL])
        ngend = sb(gtab, "ngend", [HC, 2])
        rows2 = sb(gtab, "rows2", [1, 2, HC])
        mnext = sb(gtab, "mnext", [1, HC])
        mprow = sb(gtab, "mprow", [1, HC])
        invcnt = sb(gtab, "invcnt", [P, PG, 16])
        gtab.close()

        hmT = sb(top, "hmT", [P, KT, T])
        mls = ExitStack()
        cst = sb(mls, "cst", [P, H, 2, E1])
        qkv = sb(mls, "qkv", [P, 2, 24, CK])
        neggb = sb(mls, "neggb", [P, 2, H, CK])
        wexp = sb(mls, "wexp", [P, 2, H, CK])
        pT = sb(mls, "pT", [P, H, CK])
        kw = sb(mls, "kw", [P, H, HD])
        vext = sb(mls, "vext", [P, H, E1])
        hs = sb(mls, "hs", [P, H, E1])
        hn = sb(mls, "hn", [P, H, E1])
        hf = sb(mls, "hf", [P, H, HD])
        cur = sb(mls, "cur", [P, 2, 5, H])
        sm = sb(mls, "sm", [P, 8, H])
        mask = sb(mls, "mask", [P, CK])
        mls.close()
        smp = ExitStack()
        cs = sb(smp, "cs", [P, 2, NB, 2, E1])
        qkvs = sb(smp, "qkvs", [P, 2, 6, SMP])
        qm = sb(smp, "qm", [P, 2, NB, 2, SMP])
        argS = sb(smp, "argS", [SMP, 2, SMP])
        wexpS = sb(smp, "wexpS", [SMP, 2, SMP])
        pTS = sb(smp, "pTS", [SMP, SMP])
        ks = sb(smp, "ks", [SMP, HD])
        vs = sb(smp, "vs", [SMP, E1])
        kb = sb(smp, "kb", [SMP, NB, HD])
        hsS = sb(smp, "hsS", [SMP, E1])
        hnS = sb(smp, "hnS", [SMP, E1])
        hfS = sb(smp, "hfS", [SMP, HD])
        junkS = sb(smp, "junkS", [SMP, HD])
        curD = sb(smp, "curD", [P, 2, NB])
        curC = sb(smp, "curC", [SMP, 2, 4])
        wmask = sb(smp, "wmask", [SMP, 2, NB])
        smS = sb(smp, "smS", [SMP, 8])
        maskS = sb(smp, "maskS", [SMP, SMP])
        blk = sb(smp, "blk", [SMP, NB])
        nrow = sb(smp, "nrow", [HC, HD])
        nT = sb(smp, "nT", [P, 2, HC])
        nO = sb(smp, "nO", [P, 2, HC])
        nout = sb(smp, "nout", [HC, HD])
        urows = sb(smp, "urows", [HIST + SMP, PW])
        ulast = sb(smp, "ulast", [P, PG, HIST + SMP])
        smp.close()
        sq = sb(top, "sq", [P, T])
        ssq = sb(top, "ssq", [P, T])
        brn = ExitStack()
        yp_hi = sb(brn, "yp_hi", [P, PG, T], F32R)
        yp_lo = sb(brn, "yp_lo", [P, PG, T], F32R)
        oin = sb(brn, "oin", [P, 2, T])
        wpool = sb(brn, "wpool", [P, PG, P])
        dT = sb(brn, "dT", [P, 2, T])
        brn.close()
        ffn = ExitStack()
        a_hi = sb(ffn, "a_hi", [P, 2, T], F32R)
        a_lo = sb(ffn, "a_lo", [P, 2, T], F32R)
        a32 = sb(ffn, "a32", [P, 2, T])
        sil = sb(ffn, "sil", [P, T])
        gsm = sb(ffn, "gsm", [P, 2, SMP])
        rcol = sb(ffn, "rcol", [P, TT])
        ytok = sb(ffn, "ytok", [P, 2, D])
        ffn.close()

        dense = top.enter_context(nc.psum_tensor("dense", [P, 6, 512], F32))
        misc = top.enter_context(nc.psum_tensor("misc", [P, 2, 512], F32))

        def pair(name):
            return [sem(name + "0"), sem(name + "1")]

        consts_ready = sem("consts_ready")
        small_in, nrow_in, ulast_in, wpool_in = sem("small_in"), sem("nrow_in"), sem("ulast_in"), sem("wpool_in")
        x_in = [sem(f"x_in{j}") for j in range(3)]
        raw_in, raw_free = pair("raw_in"), pair("raw_free")
        ada_in, ada_free = pair("ada_in"), pair("ada_free")
        hi_ready, lo_ready = sem("hi_ready"), sem("lo_ready")
        tile_full, tile_free = pair("tile_full"), pair("tile_free")
        round_full, round_free = pair("round_full"), pair("round_free")
        stage_full, stage_out = sem("stage_full"), pair("stage_out")
        csig_ready, silu_ready = sem("csig_ready"), sem("silu_ready")
        ssq_ready, std_ready, x_spilled = sem("ssq_ready"), sem("std_ready"), sem("x_spilled")
        h32_ready, hhi_ready, h_ready = sem("h32_ready"), sem("hhi_ready"), sem("h_ready")
        dve_step, act_step, pool_step = sem("dve_step"), sem("act_step"), sem("pool_step")
        gates_ready, gates_out, gates_in = sem("gates_ready"), sem("gates_out"), sem("gates_in")
        lnterm_ready, cummax_ready, mprow_ready = sem("lnterm_ready"), sem("cummax_ready"), sem("mprow_ready")
        g_ready, gexp_ready, tables_ready = sem("g_ready"), sem("gexp_ready"), sem("tables_ready")
        tables_out, tables_in = sem("tables_out"), sem("tables_in")
        ext_in, d_out = sem("ext_in"), sem("d_out")
        qkv_in, mls_init, chunk_prep = pair("qkv_in"), sem("mls_init"), sem("chunk_prep")
        weights_exp, inter_ready = sem("weights_exp"), sem("inter_ready")
        msq_ready, hstd_ready, hf_ready = sem("msq_ready"), sem("hstd_ready"), sem("hf_ready")
        outs = sem("outs")
        head_in, cs_out = pair("head_in"), pair("cs_out")
        vs_init, head_prep, head_keys, head_kb = sem("vs_init"), sem("head_prep"), sem("head_keys"), sem("head_kb")
        pe_passed, pool_passed = sem("pe_passed"), sem("pool_passed")
        n_ready, nO_ready = sem("n_ready"), sem("nO_ready")
        d_in = pair("d_in")
        yphi_ready = sem("yphi_ready")
        gin_in, oin_in = pair("gin_in"), pair("oin_in")
        gsig_ready, osig_ready = sem("gsig_ready"), sem("osig_ready")
        yml32_ready, ymlhi_ready, yml_ready = sem("yml32_ready"), sem("ymlhi_ready"), sem("yml_ready")
        m32_ready, mhi_ready, m_ready = sem("m32_ready"), sem("mhi_ready"), sem("m_ready")
        xsum_ready, std2_ready = sem("xsum_ready"), sem("std2_ready")
        h2f_ready, h2hi_ready, h2_ready = sem("h2f_ready"), sem("h2hi_ready"), sem("h2_ready")
        sil_ready, a32_ready, ahi_ready = sem("sil_ready"), sem("a32_ready"), sem("ahi_ready")
        x2_ready, x2sq_ready, x2sum_ready = sem("x2_ready"), sem("x2sq_ready"), sem("x2sum_ready")
        rstd3_ready, rcol_ready, xg_ready = sem("rstd3_ready"), sem("rcol_ready"), sem("xg_ready")
        ytok_act, ytok_dve, y_out = sem("ytok_act"), sem("ytok_dve"), pair("y_out")

        def turn(k, i=0, per=0):
            assert per % 2 == 0
            return k % 2, k // 2 + i * (per // 2)

        def wait_full(eng, sems, k, i=0, per=0, inc=1):
            slot, n = turn(k, i, per)
            eng.wait_ge(sems[slot], n * inc + inc)

        def wait_free(eng, sems, k, i=0, per=0):
            slot, n = turn(k, i, per)
            if per or n:
                eng.wait_ge(sems[slot], n)

        def tile(k, c, lo=0, hi=None):
            return dense[:, 3 * (k % 2) + c, lo:CH[c][1] - CH[c][0] if hi is None else hi]

        def tile_wide(k):
            return dense[:, 3 * (k % 2):3 * (k % 2) + 2, 0:384]

        def wide(ap):
            return ap[:, 0:768].rearrange("p (c t) -> p c t", c=2)

        def bank(r, n=512, rows=P):
            return misc[0:rows, r % 2, 0:n]

        def smp3(ap):
            return ap.rearrange("p (b t) -> p b t", t=NT)

        def per_batch(ap):
            return ap.unsqueeze(2).to_broadcast([P, NB, NT])

        def row(ap3, k):
            return ap3[:, ds(k, 1), :].rearrange("p o t -> p (o t)")

        def zrow(k):
            return z[ds(k, 1)].rearrange("o p t -> (o p) t")

        block = top.enter_context(nc.Block())

        @block.sync
        def _(sp):
            def w_cols(w, col, n=P):
                return w[:, ds(col, n)].rearrange("(k p) n -> p k n", p=P)

            def load(n, src, i=0, per=0, kt=KT):
                wait_free(sp, raw_free, n, i, per)
                sp.dma_start(raw[:, n % 2, :].rearrange("p (k n) -> p k n", k=kt), src).then_inc(raw_in[n % 2], 16)

            def ada_load(a, i=0, per=0):
                wait_free(sp, ada_free, a, i, per)
                sp.dma_start(ada_w[:, a % 2, :, :], w_cols(w_ada[0], i * (256 * per) + 256 * a, 256)
                             ).then_inc(ada_in[a % 2], 16)

            xp = x_prompt[0].rearrange("(j p) d -> p j d", p=P)
            sp.dma_start(xtok[:, 0:8, 0:512], xp[:, :, 0:512]).then_inc(x_in[0], 16)
            sp.dma_start(xtok[0:SMP, 8, :], x_sample.rearrange("b t d -> (b t) d")).then_inc(x_in[2], 16)
            sp.dma_start(xtok[:, 0:8, 512:1024], xp[:, :, 512:1024]).then_inc(x_in[1], 16)
            for a in range(ADA0 // 2):
                ada_load(a)
                if a == 5:
                    load(0, w_cols(w_in[0], GATE_COL))
                if a == 7:
                    load(1, w_cols(w_in[0], 0))
            for s in range(2):
                sp.wait_ge(tile_free[s], KT // 2)
            sp.dma_start(z[Z_X:Z_X + KT].rearrange("k p t -> p k t"), xT[:, :, :]).then_inc(x_spilled, 16)
            load(2, w_cols(w_in[0], P))
            load(3, w_cols(w_in[0], 2 * P))

            sp.wait_ge(gates_ready, 2)
            sp.dma_start(gate_rows_p, gates[:, 0:SEQ]).then_inc(gates_out, 16)
            sp.dma_start(gate_rows_s, gates[:, SEQ:T]).then_inc(gates_out, 16)
            sp.wait_ge(gates_out, 32)
            for n, h0 in (("ig", 0), ("fg", H)):
                sp.dma_start(tab[n][:, 0:CK], gate_rows_p[h0:h0 + H].rearrange("h (c t) -> (h c) t", t=CK)
                             ).then_inc(gates_in, 16)
                sp.dma_start(tab[n][:, CK:GL], gate_rows_s[h0:h0 + H].rearrange("h (c t) -> (h c) t", t=NT)
                             ).then_inc(gates_in, 16)

            def l1_loads(lo, hi):
                with sp.Fori(lo, hi) as i:
                    for j in range(2):
                        ada_load(ADA0 // 2 + j, i, 2)
                        for n in (4 + 2 * j, 5 + 2 * j):
                            load(n, w_cols(w_in[0], i * (4 * P) + P * (n - U_L1)), i, 4)

            l1_loads(0, 4)
            sp.wait_ge(tables_ready, 1)
            sp.dma_start(negg_dram, tab["negg"][:, 0:CK]).then_inc(tables_out, 16)
            for j, n in enumerate(("r", "winter", "emt", "wend16", "negg")):
                sp.dma_start(tab_s_dram[j], tab[n][:, CK:GL]).then_inc(tables_out, 16)
            for j, col in enumerate((CK - 1, GL - 1)):
                sp.dma_start(decay_dram[j].rearrange("(r o) -> r o", o=1), tab["winter"][:, col:col + 1]
                             ).then_inc(tables_out, 16)
            for h in range(H):
                sp.dma_start(m_s[0, :, h:h + 1], tab["mt"][h * NB:(h + 1) * NB, GL - 1:GL]).then_inc(outs, 16)
            sp.dma_start(m_p[0], mnext[:, :].rearrange("p (h c) -> p h c", c=NCK)[:, :, NCK - 1]).then_inc(outs, 16)
            sp.wait_ge(tables_out, 8 * 16)
            sp.dma_start(dec[:, :, :].rearrange("p a r -> p (a r)"),
                         decay_dram.rearrange("a r -> (a r)").partition_broadcast(P)).then_inc(tables_in, 16)
            sp.dma_start(negg_s[:, :, :].rearrange("p h t -> p (h t)"),
                         tab_s_dram[4].rearrange("r t -> (r t)").partition_broadcast(SMP)).then_inc(tables_in, 16)
            for q in range(4):
                for h in range(H):
                    sp.dma_start(scol[:, q, h:h + 1],
                                 tab_s_dram[q, h * NB:(h + 1) * NB].rearrange("b (t o) -> (b t) o", o=1)
                                 ).then_inc(tables_in, 16)
            l1_loads(4, 6)
            for a in (ADA0 // 2 + 12, ADA0 // 2 + 13):
                ada_load(a)
            load(28, w_cols(w_in[0], 27 * P))

            def l2_load(j, i=0, per=0):
                g = j // 2
                col = PW + 3 * D + g * D + (2 * H if g else 0) + P * (j % 2)
                load(U_L2 + j, w_cols(w_in[0], i * 256 + col), i, per)

            def chunk_load(c, ci):
                sp.dma_start(qkv[:, c, :, :], z[Z_Q:Z_O, :, ds(ci * CK, CK)].rearrange("j p t -> p j t")
                             ).then_inc(qkv_in[c], 16)
                src = negg_dram.rearrange("(h c) t -> c h t", h=H)[ds(ci, 1)].rearrange("o h t -> (o h) t")
                sp.dma_start(neggb[:, c, :, :], src.partition_broadcast(P)).then_inc(qkv_in[c], 16)

            for j in range(2):
                l2_load(j)
            sp.wait_ge(x_spilled, 16)
            sp.wait_ge(tables_in, 18 * 16)
            sp.wait_ge(outs, 5 * 16)
            sp.wait_ge(d_out, 2 * PG * 16)
            for s in range(2):
                sp.wait_ge(ada_free[s], NA // 4)
                sp.wait_ge(stage_out[s], 14 * 16)
            for c in range(2):
                chunk_load(c, c)
            for j in range(2, 6):
                l2_load(j)
            with sp.Fori(1, 4) as i:
                for j in range(6):
                    l2_load(j, i, 6)
                    if j % 3 == 1:
                        wait_full(sp, round_full, R_L2 + RPC * (j // 3) + 17, i - 1, 2 * RPC)
                        chunk_load(j // 3, i * 2 + j // 3)

            def bp_src(n):
                return w_bp[0][:, 256 * (n - U_BP):256 * (n - U_BP) + 256].rearrange("(k p) n -> p k n", p=P)

            for n in (U_BP, U_BP + 1):
                load(n, bp_src(n), kt=PG)
            for r in (R_UT - 2, R_UT - 1):
                wait_full(sp, round_free, r)
            for h in range(H):
                sp.dma_start(c_p[0, 0, h].rearrange("(a p) e -> p a e", p=P), cst[:, h, :, 0:HD]).then_inc(outs, 16)
                sp.dma_start(n_p[0, 0, h].rearrange("(a p o) -> p a o", p=P, o=1), cst[:, h, :, HD:E1]).then_inc(outs, 16)
            sp.wait_ge(outs, 13 * 16)
            sp.dma_start(nrow[:, :], state_n[0].rearrange("b h d -> (b h) d")).then_inc(nrow_in, 16)
            sp.dma_start(ulast[:, :, :], z[Z_U:Z_Q, :, SEQ - HIST:T].rearrange("g p t -> p g t")).then_inc(ulast_in, 16)

            def head_load(s, h):
                for g, zr in enumerate((Z_Q, Z_K, Z_V)):
                    sp.dma_start(qkvs[:, s, 2 * g:2 * g + 2, :],
                                 z[2 * h + zr:2 * h + zr + 2, :, SEQ:T].rearrange("j p t -> p j t")
                                 ).then_inc(head_in[s], 16)
                for b in range(NB):
                    sp.dma_start(cs[:, s, b, :, 0:HD], state_c[0, b, h].rearrange("(a p) e -> p a e", p=P)
                                 ).then_inc(head_in[s], 16)

            def head_store(s, h):
                for b in range(NB):
                    for a in range(2):
                        wait_full(sp, round_free, R_SMP + RPH * h + 4 + 2 * b + a)
                    sp.dma_start(c_s[0, b, h].rearrange("(a p) e -> p a e", p=P), cs[:, s, b, :, 0:HD]
                                 ).then_inc(cs_out[s], 16)

            head_load(0, 0)
            head_load(1, 1)
            wait_full(sp, round_free, R_UT + 1)
            sp.dma_start(pool_p[0, 0], urows[0:HIST, :]).then_inc(outs, 16)
            for b in range(NB):
                sp.dma_start(pool_s[0, b, HIST - NT:HIST], urows[HIST + b * NT:HIST + (b + 1) * NT, :]).then_inc(outs, 16)
            sp.dma_start(pool_s[0, :, 0:HIST - NT], state_pool[0, :, NT:HIST]).then_inc(outs, 16)
            for h in range(H):
                head_store(h % 2, h)
                if h + 2 < H:
                    sp.wait_ge(cs_out[h % 2], NB * 16)
                    wait_full(sp, round_free, R_SMP + RPH * h + 20)
                    head_load(h % 2, h + 2)
            wait_full(sp, round_free, R_NOUT)
            sp.dma_start(n_s[0].rearrange("b h d -> (b h) d"), nout[:, :]).then_inc(outs, 16)
            sp.wait_ge(outs, 24 * 16)
            for s in range(2):
                sp.wait_ge(cs_out[s], 2 * NB * 16)
            sp.dma_start(wpool[:, :, :], w_pool[0].rearrange("g c d -> c g d")).then_inc(wpool_in, 16)
            for g in range(PG):
                if g >= 2:
                    wait_full(sp, tile_full, T_YP + g - 2)
                sp.dma_start(dT[:, g % 2, :], z[Z_D + g]).then_inc(d_in[g % 2], 16)
            for s in range(2):
                sp.wait_ge(stage_out[s], 26 * 16)

            def rows_in(k, src, i=0, per=0):
                wait_free(sp, tile_free, k, i, per)
                sp.dma_start(stage[:, k % 2, :], src).then_inc(gin_in[k % 2], 16)

            for j in range(8):
                rows_in(T_BP + j, z[Z_GP + j])
                sp.dma_start(oin[:, j % 2, :], z[Z_O + j]).then_inc(oin_in[j % 2], 16)
                if j % 2:
                    if j < 4:
                        load(U_BP + 2 + j // 2, bp_src(U_BP + 2 + j // 2), kt=PG)
                    else:
                        load(U_BM + j // 2 - 2, w_cols(w_bm[0], P * (j // 2 - 2)))
            for t0, zr, u0, w, w_next in ((T_BM, Z_GM, U_BM, w_bm, w_out), (T_OUT, Z_X, U_OUT, w_out, None)):
                with sp.Fori(0, 3) as i:
                    for j in range(2):
                        rows_in(t0 + j, zrow(i * 2 + (zr + j)), i, 2)
                        load(u0 + 2 + j, w_cols(w[0], i * 256 + P * (2 + j)), i, 2)
                for j in range(6, 8):
                    rows_in(t0 + j, z[zr + j])
                    if w_next is not None:
                        load(u0 + 2 + j, w_cols(w_next[0], P * (j - 6)))

            def ffn_load(j, i=0, per=0):
                if j < 4:
                    load(U_FFN + j, w_cols(w_gu[0], i * 256 + P * (j // 2) + FF * (j % 2)), i, per)
                else:
                    src = w_down[0][ds(i * 256, 256), 512 * (j - 4):512 * (j - 3)].rearrange("(f p) n -> p f n", p=P)
                    load(U_FFN + j, src, i, per, kt=2)

            for j in range(6):
                ffn_load(j)
            with sp.Fori(1, FT // 2) as i:
                for j in range(6):
                    ffn_load(j, i, 6)

            for tt in range(TT):
                sp.wait_ge(ytok_act, tt + 1)
                sp.wait_ge(ytok_dve, tt + 1)
                dst = y_prompt[0, tt * P:(tt + 1) * P] if tt < 8 else y_sample.rearrange("b t d -> (b t) d")
                sp.dma_start(dst, ytok[0:P if tt < 8 else SMP, tt % 2, :]).then_inc(y_out[tt % 2], 16)
            sp.wait_ge(y_out[0], 5 * 16)
            sp.wait_ge(y_out[1], 4 * 16)

        @block.gpsimd
        def _(pool):
            step = [0]

            def link(ins):
                step[0] += 1
                ins.then_inc(pool_step, 1)
                pool.wait_ge(pool_step, step[0])

            pool.memset(ones[:, :], 1.0).then_inc(consts_ready, 1)
            pool.memset(epsc[:, :], EPS).then_inc(consts_ready, 1)
            link(pool.memset(ident[:, :], 0.0))
            pool.affine_select(out=ident[:, :], in_=ident[:, :], compare_op=ALU.not_equal, fill=1.0,
                               base=0, pattern=[[-1, P]], channel_multiplier=1).then_inc(consts_ready, 1)

            pool.wait_ge(h_ready, KT)
            pool.wait_ge(x_spilled, 16)
            pool.memset(zeros[:, :], 0.0).then_inc(consts_ready, 1)
            for g in range(PG):
                for t in range(16):
                    last = pool.memset(invcnt[:, g, t:t + 1], 1.0 / min(t + 1, 2 << g))
            link(last)
            link(pool.memset(ext_p[:, :, 0:HIST], 0.0))
            for s in range(2):
                pool.wait_ge(stage_out[s], 2 * 16)
            for g in range(PG):
                pool.dma_start(ext_p[:, g, HIST:HIST + SEQ], z[Z_U + g, :, 0:SEQ]).then_inc(ext_in, 16)
                pool.dma_start(ext_s[:, g, :, HIST:HIST + NT], smp3(z[Z_U + g, :, SEQ:T])).then_inc(ext_in, 16)
            pool.wait_ge(ext_in, 2 * PG * 16)
            wait_full(pool, round_free, R_COLS + 1)
            for g in range(PG):
                for smp_part in (False, True):
                    n = HIST + (NT if smp_part else SEQ)
                    ext = ext_s[:, g, :, :] if smp_part else ext_p[:, g, :]
                    bufs = [win[:, s, 0:NB * n].rearrange("p (b t) -> p b t", b=NB) if smp_part else win[:, s, :]
                            for s in range(2)]

                    def cut(v, lo, hi):
                        return v[:, :, lo:hi] if smp_part else v[:, lo:hi]

                    src, span, turn_ = ext, 1, 0
                    while span < 2 << g:
                        dst, turn_ = bufs[turn_], 1 - turn_
                        link(pool.tensor_tensor(cut(dst, 2 * span - 1, n), cut(src, 2 * span - 1, n),
                                                cut(src, span - 1, n - span), ALU.add))
                        src, span = dst, 2 * span
                    dst = bufs[turn_]
                    if smp_part:
                        link(pool.tensor_scalar(cut(dst, HIST, n), cut(src, HIST, n), 1.0 / (2 << g), None, ALU.mult))
                    else:
                        pool.tensor_tensor(dst[:, HIST:HIST + 16], src[:, HIST:HIST + 16], invcnt[:, g, :], ALU.mult)
                        link(pool.tensor_scalar(dst[:, HIST + 16:n], src[:, HIST + 16:n], 1.0 / (2 << g), None, ALU.mult))
                    link(pool.tensor_tensor(cut(ext, HIST, n), cut(dst, HIST, n), cut(ext, HIST, n), ALU.subtract))
                pool.dma_start(z[Z_D + g, :, 0:SEQ], ext_p[:, g, HIST:HIST + SEQ]).then_inc(d_out, 16)
                pool.dma_start(smp3(z[Z_D + g, :, SEQ:T]), ext_s[:, g, :, HIST:HIST + NT]).then_inc(d_out, 16)
            pool.wait_ge(d_out, 2 * PG * 16)

            pool.wait_ge(tables_in, 18 * 16)
            pool.wait_ge(outs, 5 * 16)
            for s in range(2):
                pool.wait_ge(ada_free[s], NA // 4)
            link(pool.memset(mask[:, :], 0.0))
            link(pool.affine_select(out=mask[:, :], in_=mask[:, :], compare_op=ALU.is_ge, fill=NEG,
                                    base=0, pattern=[[1, CK]], channel_multiplier=-1))
            pool.memset(vext[:, :, HD:E1], 1.0).then_inc(mls_init, 1)
            pool.memset(cst[:, :, :, :], 0.0).then_inc(mls_init, 1)
            with pool.Fori(0, NCK // 2) as i:
                for c in range(2):
                    ci = i * 2 + c
                    for r in (21, 22):
                        wait_full(pool, round_free, R_L2 + RPC * c + r, i - 1, 2 * RPC)
                    pool.wait_ge(qkv_in[c], i * 32 + 32)
                    pool.tensor_tensor(neggb[:, c, :, :], neggb[:, c, :, :],
                                       mask[:, :].unsqueeze(1).to_broadcast([P, H, CK]), ALU.add).then_inc(chunk_prep, 1)
                    pool.tensor_copy(cur[:, c, 0:4, :], colp[:, :, :].rearrange("p q (h c) -> p q h c", h=H)
                                     [:, :, :, ds(ci, 1)].rearrange("p q h o -> p q (h o)")).then_inc(chunk_prep, 1)
                    pool.tensor_copy(cur[:, c, 4, :], dec[:, 0, :].rearrange("p (h c) -> p h c", h=H)
                                     [:, :, ds(ci, 1)].rearrange("p h o -> p (h o)")).then_inc(chunk_prep, 1)

            pool.wait_ge(outs, 13 * 16)
            pool.memset(vs[:, HD:E1], 1.0).then_inc(vs_init, 1)
            link(pool.memset(maskS[:, :], 0.0))
            m3 = smp3(maskS[:, :])
            link(pool.affine_select(out=m3, in_=m3, compare_op=ALU.is_ge, fill=NEG,
                                    base=0, pattern=[[NT, NB], [1, NT]], channel_multiplier=-1))
            link(pool.affine_select(out=m3, in_=m3, compare_op=ALU.is_ge, fill=NEG,
                                    base=0, pattern=[[-NT, NB], [0, NT]], channel_multiplier=1))
            link(pool.memset(blk[:, :], 1.0))
            link(pool.affine_select(out=blk[:, :], in_=blk[:, :], compare_op=ALU.is_ge, fill=0.0,
                                    base=0, pattern=[[-NT, NB]], channel_multiplier=1))
            link(pool.affine_select(out=blk[:, :], in_=blk[:, :], compare_op=ALU.is_ge, fill=0.0,
                                    base=NT - 1, pattern=[[NT, NB]], channel_multiplier=-1))
            link(pool.memset(qm[:, :, :, :, :], 0.0))
            base = step[0]
            with pool.Fori(0, H // 2) as i:
                for s in range(2):
                    h = i * 2 + s
                    pool.wait_ge(head_in[s], i * (11 * 16) + 11 * 16)
                    pool.tensor_tensor(argS[:, s, :], row(negg_s, h), maskS[:, :], ALU.add).then_inc(head_prep, 1)
                    pool.tensor_copy(curD[:, s, :], dec[:, 1, ds(h * NB, NB)]).then_inc(head_prep, 1)
                    pool.tensor_copy(curC[:, s, :], scol[:, :, ds(h, 1)].rearrange("p q o -> p (q o)")
                                     ).then_inc(pool_step, 1)
                    pool.wait_ge(pool_step, h + (base + 1))
                    pool.sem_inc(pool_passed, 1)
                    pool.tensor_scalar(wmask[:, s, :], blk[:, :], curC[:, s, 3:4], None, ALU.mult
                                       ).then_inc(head_prep, 1)
                    for b in range(NB):
                        pool.tensor_copy(qm[:, s, b, :, NT * b:NT * b + NT], qkvs[:, s, 0:2, NT * b:NT * b + NT]
                                         ).then_inc(head_prep, 1)
                    pool.wait_ge(head_keys, h + 1)
                    pool.wait_ge(head_prep, h * 11 + 11)
                    pool.sem_inc(pool_passed, 1)
                    for b in range(NB):
                        pool.tensor_scalar(kb[:, b, :], ks[:, :], wmask[:, s, b:b + 1], None, ALU.mult
                                           ).then_inc(head_kb, 1)

        @block.scalar
        def _(act):
            def copy2(k, dst, func=ACT.Copy, scale=1.0, bias=None):
                kw_ = {} if bias is None else {"bias": bias}
                act.activation(wide(dst), tile_wide(k), func, scale=scale, **kw_)
                return act.activation(dst[:, 768:T], tile(k, 2), func, scale=scale, **kw_)

            def split_hi(n, i=0, per=0):
                wait_full(act, raw_in, n, i, per, inc=16)
                act.activation(w_hi[:, n % 2, :], raw[:, n % 2, :], ACT.Copy).then_inc(hi_ready, 1)

            def modulation(r, m, a=None, i=0, per=0, mdyn=None):
                wait_full(act, round_full, r, i, per)
                if a is not None:
                    act.sem_inc(ada_free[a % 2], 1)
                if mdyn is None:
                    out, b = mod[:, m, :], vec[:, V_ADA + m:V_ADA + m + 1]
                else:
                    out, b = mod[:, ds(mdyn, 1), :].rearrange("p o g -> p (o g)"), vec[:, ds(mdyn + V_ADA, 1)]
                act.activation(out, bank(r, GRP), ACT.Identity, bias=b).then_inc(round_free[r % 2], 1)

            vecs = ((V_MIX, g_mix[0]), (V_FFN, g_ffn[0]), (V_FIN, g_final), (V_HEAD, g_head[0]), (V_POOL, s_pool[0]),
                    (V_ADA, b_ada[0]))
            act.dma_start(cc[0:1, :], c_prompt).then_inc(small_in, 16)
            act.dma_start(cc[1:GRP, :], c_sample).then_inc(small_in, 16)
            for r, v in vecs:
                n = v.shape[0] // P
                act.dma_start(vrow[r:r + n, :], v.rearrange("(k p) -> k p", p=P)).then_inc(small_in, 16)
            act.dma_start(hrow[:, :], state_pool[0].rearrange("b t c -> (b t) c")).then_inc(small_in, 16)
            act.dma_start(gbias[0:H, :], b_igate[0].rearrange("(h o) -> h o", o=1)).then_inc(small_in, 16)
            act.dma_start(gbias[H:2 * H, :], b_fgate[0].rearrange("(h o) -> h o", o=1)).then_inc(small_in, 16)
            for h in range(H):
                act.dma_start(mprev[h * NB:(h + 1) * NB, 1:2], state_m[0, :, h:h + 1]).then_inc(small_in, 16)
            act.wait_ge(small_in, 15 * 16)
            act.activation(csig, cc, ACT.Sigmoid).then_inc(csig_ready, 1)

            for k in range(KT):
                wait_full(act, tile_full, k)
                copy2(k, xT[:, k, :])
                if k >= 1:
                    act.wait_ge(ssq_ready, k)
                copy2(k, xsq[:, :], ACT.Square).then_inc(tile_free[k % 2], 1)
            act.wait_ge(ssq_ready, KT)
            act.wait_ge(consts_ready, 3)
            wait_full(act, tile_full, T_SS)
            copy2(T_SS, xsq[:, :], ACT.Sqrt, 1.0 / D, epsc[:, 0:1]).then_inc(std_ready, 1)
            wait_full(act, round_free, R_VEC)
            for m in range(ADA0):
                modulation(R_ADA + m, m, m // 2 if m % 2 else None)
            split_hi(0)
            split_hi(1)
            for k in range(KT):
                act.wait_ge(h32_ready, k + 1)
                act.activation(act_hi[:, k, :], h32[:, k % 2, :], ACT.Copy).then_inc(hhi_ready, 1)
            wait_full(act, tile_full, T_GATE)
            act.wait_ge(x_spilled, 16)
            s = 3 * (T_GATE % 2)
            act.activation(wide(gates[:, :]), dense[0:8, s:s + 2, 0:384], ACT.Identity, bias=gbias[:, 0:1]
                           ).then_inc(gates_ready, 1)
            act.activation(gates[:, 768:T], dense[0:8, s + 2, 0:320], ACT.Identity, bias=gbias[:, 0:1]
                           ).then_inc(gates_ready, 1)
            act.wait_ge(gates_ready, 2)
            act.sem_inc(tile_free[T_GATE % 2], 1)
            split_hi(2)

            def evac(k, part, i=0, per=0):
                if part == 0:
                    wait_full(act, tile_full, k, i, per)
                    slot, m = turn(k - T_L1, i, per)
                    if per or m:
                        act.wait_ge(stage_out[slot], m * 16)
                    act.activation(wide(stage[:, k % 2, :]), tile_wide(k), ACT.Copy)
                else:
                    act.activation(stage[:, k % 2, 768:T], tile(k, 2), ACT.Copy).then_inc(tile_free[k % 2], 1)

            def store(k, dst, i=0, per=0):
                wait_full(act, tile_free, k, i, per)
                act.dma_start(dst, stage[:, k % 2, :]).then_inc(stage_out[k % 2], 16)

            def l1_part(part):
                lo, hi = L1_CUTS[part]
                rb = R_SEG[part]

                def body(j, i, per):
                    k = T_L1 + j
                    evac(k, 0, i, per)
                    evac(k, 1, i, per)
                    split_hi(U_L1 + j + 2, i, per)
                    store(k, zrow(i * 4 + j) if per else z[j], i, per)
                    a = j // 2 if j % 2 else None
                    modulation(rb + j, ADA0 + j, a, i, per, i * 4 + (ADA0 + j) if per else None)

                if lo == 0:
                    act.wait_ge(h_ready, KT)
                    for j in range(4):
                        body(j, 0, 0)
                    return
                with act.Fori(lo // 2, hi // 2) as i:
                    for j in range(4):
                        body(j, i, 4)

            l1_part(0)
            act.wait_ge(gates_in, 4 * 16)
            act.activation(tab["abs"][:, :], tab["fg"][:, :], ACT.Abs).then_inc(act_step, 1)
            act.wait_ge(act_step, 1)
            act.activation(tab["exp"][:, :], tab["abs"][:, :], ACT.Exp, scale=-1.0).then_inc(act_step, 1)
            act.wait_ge(act_step, 2)
            act.activation(tab["ln"][:, :], tab["exp"][:, :], ACT.Ln, bias=1.0).then_inc(lnterm_ready, 1)
            l1_part(1)
            act.wait_ge(g_ready, 1)
            for a, cols in enumerate((slice(0, CK), slice(CK, GL))):
                act.activation(tab["winter"][:, cols], tab["g"][:, cols], ACT.Exp, scale=-1.0, bias=mprev[:, a:a + 1]
                               ).then_inc(gexp_ready, 1)
                act.activation(tab["wend"][:, cols], tab["r"][:, cols], ACT.Exp, bias=ngend[:, a:a + 1]
                               ).then_inc(gexp_ready, 1)
            act.activation(tab["emt"][:, :], tab["mt"][:, :], ACT.Exp, scale=-1.0).then_inc(gexp_ready, 1)
            l1_part(2)
            l1_part(3)

            def l2_step(j, i, part):
                k = T_L2 + j
                if part < 2:
                    evac(k, part, i, 6)
                if part == 2:
                    split_hi(U_L2 + j + 2, i, 6)
                if part == 3:
                    store(k, zrow(i * 2 + (Z_O + KT * (j // 2) + j % 2)), i, 6)

            def chunk_act(c, i, slot):
                ci = i * 2 + c
                rb = R_L2 + RPC * c
                if slot == 0:
                    act.wait_ge(chunk_prep, ci * 3 + 3)
                    for h in range(H):
                        ins = act.activation(wexp[:, c, h, :], neggb[:, c, h, :], ACT.Exp, bias=cur[:, c, 0, h:h + 1])
                    ins.then_inc(weights_exp, 1)
                if slot in (0, 1):
                    r = rb + 1 + slot
                    wait_full(act, round_full, r, i, 2 * RPC)
                    for a in range(2):
                        h = 2 * slot + a
                        ins = act.activation(kw[:, h, :], bank(r)[:, HD * a:HD * a + HD], ACT.Copy,
                                             scale=cur[:, c, 3, h:h + 1])
                    ins.then_inc(round_free[r % 2], 1)
                if 4 <= slot < 20 and slot % 4 == 0:
                    h = slot // 4 - 1
                    r = rb + 5 + 4 * h
                    wait_full(act, round_full, r, i, 2 * RPC)
                    act.activation(hs[:, h, :], bank(r, E1), ACT.Copy, scale=cur[:, c, 1, h:h + 1]
                                   ).then_inc(round_free[r % 2], 1)
                if slot == 20:
                    act.wait_ge(msq_ready, ci + 1)
                    act.activation(sm[:, 4, :], sm[:, 3, :], ACT.Sqrt, scale=1.0 / HD, bias=epsc[:, 0:1]
                                   ).then_inc(hstd_ready, 1)
                if slot == 23:
                    for a in range(2):
                        r = rb + 21 + a
                        wait_full(act, round_full, r, i, 2 * RPC)
                        act.activation(hmT[:, 4 * a:4 * a + 4, ds(ci * CK, CK)],
                                       bank(r).rearrange("p (j t) -> p j t", t=CK), ACT.Copy
                                       ).then_inc(round_free[r % 2], 1)

            with act.Fori(0, 4) as i:
                for j in range(6):
                    for s in range(8):
                        chunk_act(j // 3, i, (j % 3) * 8 + s)
                        if j:
                            l2_step(j - 1, i, s)
                for s in range(4):
                    l2_step(5, i, s)

            with act.Fori(0, H // 2) as i:
                for s in range(2):
                    h = i * 2 + s
                    rb = R_SMP + RPH * s
                    act.wait_ge(head_prep, h * 11 + 11)
                    act.activation(wexpS[:, s, :], argS[:, s, :], ACT.Exp, bias=curC[:, s, 0:1]).then_inc(weights_exp, 1)
                    wait_full(act, round_full, rb + 2, i, 2 * RPH)
                    act.activation(hsS[:, :], bank(rb + 2, E1, SMP), ACT.Copy, scale=curC[:, s, 1:2]
                                   ).then_inc(round_free[(rb + 2) % 2], 1)
                    act.wait_ge(msq_ready, h + (NCK + 1))
                    act.activation(smS[:, 4:5], smS[:, 3:4], ACT.Sqrt, scale=1.0 / HD, bias=epsc[0:SMP, 0:1]
                                   ).then_inc(hstd_ready, 1)
                    wait_full(act, round_full, rb + 20, i, 2 * RPH)
                    act.activation(hmT[:, ds(h * 2, 2), SEQ:T], bank(rb + 20, 128).rearrange("p (j t) -> p j t", t=SMP),
                                   ACT.Copy).then_inc(round_free[(rb + 20) % 2], 1)

            act.wait_ge(outs, 24 * 16)
            for s in range(2):
                act.wait_ge(cs_out[s], 2 * NB * 16)
            for g in range(PG):
                k = T_YP + g
                sc = vec[:, V_POOL + g:V_POOL + g + 1]
                wait_full(act, tile_full, k)
                if g:
                    wait_full(act, tile_free, k - 1)
                copy2(k, sq[:, :], scale=sc)
                copy2(k, yp_hi[:, g, :], scale=sc).then_inc(yphi_ready, 1)

            with act.Fori(0, 2) as i:
                for j in range(4):
                    k = T_BP + j
                    kt = i * 4 + j
                    wait_full(act, oin_in, j, i, 4, 16)
                    act.activation(oin[:, j % 2, :], oin[:, j % 2, :], ACT.Sigmoid).then_inc(osig_ready, 1)
                    wait_full(act, gin_in, j, i, 4, 16)
                    act.activation(stage[:, k % 2, :], stage[:, k % 2, :], ACT.Sigmoid).then_inc(gsig_ready, 1)
                    act.wait_ge(yml32_ready, kt + 1)
                    act.activation(row(act_hi, kt), row(hmT, kt), ACT.Copy).then_inc(ymlhi_ready, 1)
                    if j % 2:
                        wait_full(act, tile_full, k, i, 4)
                        split_hi(U_BP + 2 + j // 2, i, 2)
            with act.Fori(0, 4) as i:
                for j in range(2):
                    k = T_BM + j
                    wait_full(act, gin_in, 8 + j, i, 2, 16)
                    act.activation(stage[:, k % 2, :], stage[:, k % 2, :], ACT.Sigmoid).then_inc(gsig_ready, 1)
                    wait_full(act, tile_full, k, i, 2)
                    split_hi(U_BM + 2 + j, i, 2)
            for k in range(KT):
                act.wait_ge(m32_ready, k + 1)
                act.activation(act_hi[:, k, :], hmT[:, k, :], ACT.Copy).then_inc(mhi_ready, 1)
            with act.Fori(0, 4) as i:
                for j in range(2):
                    wait_full(act, tile_full, T_OUT + j, i, 2)
                    split_hi(U_OUT + 2 + j, i, 2)
            wait_full(act, tile_full, T_N2)
            copy2(T_N2, sq[:, :], ACT.Sqrt, 1.0 / D, epsc[:, 0:1]).then_inc(std2_ready, 1)
            for k in range(KT):
                act.wait_ge(h2f_ready, k + 1)
                act.activation(act_hi[:, k, :], h32[:, k % 2, :], ACT.Copy).then_inc(h2hi_ready, 1)

            def ffn_act(i, last=False):
                for j in range(6):
                    n = U_FFN + j
                    wait_full(act, tile_full, last_tile(n), i, 12)
                    if j in (0, 2):
                        act.wait_ge(a32_ready, i * 2 + (j // 2 + 1))
                        copy2(T_FFN + j, sil[:, :], ACT.Silu).then_inc(sil_ready, 1)
                    if j in (1, 3):
                        act.wait_ge(a32_ready, i * 2 + (j // 2 + 2))
                        act.activation(a_hi[:, j // 2, :], a32[:, j // 2, :], ACT.Copy).then_inc(ahi_ready, 1)
                    if not last or j < 4:
                        split_hi(n + 2, i, 6)

            with act.Fori(0, FT // 2 - 1) as i:
                ffn_act(i)
            ffn_act(FT // 2 - 1, last=True)

            for k in range(KT):
                act.wait_ge(x2_ready, 8 * (FT // 2 - 1) + k + 1)
                if k >= 2:
                    act.wait_ge(x2sum_ready, k - 1)
                act.activation((sq, sil)[k % 2][:, :], hmT[:, k, :], ACT.Square).then_inc(x2sq_ready, 1)
            wait_full(act, round_full, R_Y)
            act.activation(rcol[:, 0:8], bank(R_Y, 8), ACT.Sqrt, scale=1.0 / D, bias=epsc[:, 0:1]).then_inc(rstd3_ready, 1)
            act.activation(rcol[0:SMP, 8:9], bank(R_Y, 9, SMP)[:, 8:9], ACT.Sqrt, scale=1.0 / D,
                           bias=epsc[0:SMP, 0:1]).then_inc(rstd3_ready, 1)
            act.wait_ge(rcol_ready, 2)
            for tt in range(TT):
                k, rows = T_Y + tt, P if tt < 8 else SMP
                wait_full(act, tile_full, k)
                if tt >= 2:
                    act.wait_ge(y_out[tt % 2], 16 * (tt // 2))
                act.activation(ytok[0:rows, tt % 2, 0:512], dense[0:rows, 3 * (k % 2), :], ACT.Copy,
                               scale=rcol[0:rows, tt:tt + 1]).then_inc(ytok_act, 1)

        @block.vector
        def _(dve):
            steps = [0, 0, None]

            def now():
                return steps[0] if steps[2] is None else steps[2] + steps[0]

            def link(ins):
                steps[0] += 1
                ins.then_inc(dve_step, 1)
                dve.wait_ge(dve_step, now())

            def enter(i, per):
                steps[1], steps[2] = steps[0], i * per

            def leave(n, per):
                assert steps[0] - steps[1] == per, (steps[0] - steps[1], per)
                steps[0], steps[2] = steps[1] + n * per, None

            def split_lo(n, i=0, per=0):
                dve.wait_ge(hi_ready, i * per + (n + 1))
                dve.tensor_tensor(w_lo[:, n % 2, :], raw[:, n % 2, :], w_hi[:, n % 2, :].bitcast(F32), ALU.subtract
                                  ).then_inc(raw_free[n % 2], 1)

            def norm_rows(k, xrows, amp, sh, done, used):
                o = h32[:, k % 2, :]
                if k >= 2:
                    dve.wait_ge(used, k - 1)
                link(dve.tensor_tensor(smp3(o[:, SEQ:T]), smp3(xrows[:, SEQ:T]), per_batch(amp[:, k, 1:GRP]), ALU.mult))
                dve.tensor_scalar(o[:, 0:SEQ], xrows[:, 0:SEQ], amp[:, k, 0:1], mod[:, sh + k, 0:1], ALU.mult, ALU.add)
                dve.tensor_tensor(smp3(o[:, SEQ:T]), smp3(o[:, SEQ:T]), per_batch(mod[:, sh + k, 1:GRP]), ALU.add
                                  ).then_inc(done, 1)

            def low_rows(k, src, hi_sem, out_sem):
                dve.wait_ge(hi_sem, k + 1)
                dve.tensor_tensor(act_lo[:, k, :], src, act_hi[:, k, :].bitcast(F32), ALU.subtract).then_inc(out_sem, 1)

            dve.sem_inc(a32_ready, 1)
            dve.wait_ge(csig_ready, 1)
            dve.tensor_tensor(cc, cc, csig, ALU.mult).then_inc(silu_ready, 1)
            wait_full(dve, round_full, R_VEC)
            dve.tensor_copy(vec[:, :], bank(R_VEC, NV)).then_inc(round_free[R_VEC % 2], 1)
            wait_full(dve, round_full, R_CT)
            dve.tensor_copy(cT[:, :, :].rearrange("p k g -> p (k g)"), bank(R_CT, KT * GRP)).then_inc(round_free[R_CT % 2], 1)
            for k in range(KT):
                wait_full(dve, tile_free, k)
                if k == 0:
                    dve.tensor_copy(xssq[:, :], xsq[:, :]).then_inc(ssq_ready, 1)
                else:
                    dve.wait_ge(ssq_ready, k)
                    dve.tensor_tensor(xssq[:, :], xssq[:, :], xsq[:, :], ALU.add).then_inc(ssq_ready, 1)
            dve.wait_ge(std_ready, 1)
            dve.reciprocal(xsq[:, :], xsq[:, :]).then_inc(tile_free[T_SS % 2], 1)
            wait_full(dve, tile_free, T_SS)
            for k in range(KT):
                ins = dve.tensor_tensor(xn[:, k, :], xT[:, k, :], xsq[:, :], ALU.mult)
            link(ins)
            for m in (2 * KT - 2, 2 * KT - 1):
                wait_full(dve, round_free, R_ADA + m)
            link(dve.scalar_tensor_tensor(out=amp1[:, :, :], in0=mod[:, SC1:SC1 + KT, :], scalar=1.0,
                                          in1=vec[:, V_MIX:V_MIX + KT].unsqueeze(2).to_broadcast([P, KT, GRP]),
                                          op0=ALU.add, op1=ALU.mult))
            split_lo(0)
            split_lo(1)
            for k in range(KT):
                norm_rows(k, xn[:, k, :], amp1, SH1, h32_ready, h_ready)
                if k:
                    low_rows(k - 1, h32[:, (k - 1) % 2, :], hhi_ready, h_ready)
            low_rows(KT - 1, h32[:, (KT - 1) % 2, :], hhi_ready, h_ready)
            split_lo(2)

            def l1_part(part):
                with dve.Fori(*L1_CUTS[part]) as i:
                    for j in range(2):
                        split_lo(U_L1 + j + 2, i, 2)

            l1_part(0)
            parts = (slice(0, CK), slice(CK, GL))
            dve.wait_ge(lnterm_ready, 1)
            link(dve.scalar_tensor_tensor(out=tab["lf"][:, :], in0=tab["fg"][:, :], scalar=0.0, in1=tab["ln"][:, :],
                                          op0=ALU.min, op1=ALU.subtract))
            for cols in parts:
                link(dve.tensor_tensor_scan(tab["b"][:, cols], ones[0:HC, 0:cols.stop - cols.start], tab["lf"][:, cols],
                                            0.0, ALU.mult, ALU.add))
            link(dve.tensor_tensor(tab["r"][:, :], tab["ig"][:, :], tab["b"][:, :], ALU.subtract))
            dve.wait_ge(consts_ready, 4)
            for cols in parts:
                dve.tensor_tensor_scan(tab["cm"][:, cols], tab["r"][:, cols], zeros[:, cols], -3e38, ALU.max, ALU.add
                                       ).then_inc(cummax_ready, 1)
            l1_part(1)
            wait_full(dve, round_full, R_GATES)
            dve.tensor_copy(rows2[:, :, :].rearrange("p a r -> p (a r)"), bank(R_GATES, 2 * HC, 1)
                            ).then_inc(round_free[R_GATES % 2], 1)
            wait_full(dve, round_free, R_GATES)
            link(dve.memset(mprow[:, :], NEG))
            for h in range(H):
                c = slice(h * NCK, (h + 1) * NCK)
                link(dve.tensor_tensor_scan(mnext[:, c], rows2[:, 1, c], rows2[:, 0, c], NEG, ALU.max, ALU.add))
            dve.tensor_copy(mprow[:, :].rearrange("p (h c) -> p h c", h=H)[:, :, 1:NCK],
                            mnext[:, :].rearrange("p (h c) -> p h c", h=H)[:, :, 0:NCK - 1]).then_inc(mprow_ready, 1)
            wait_full(dve, round_full, R_GATES + 1)
            dve.tensor_copy(mprev[:, 0:1], bank(R_GATES + 1, 1, HC)).then_inc(round_free[(R_GATES + 1) % 2], 1)
            wait_full(dve, round_free, R_GATES + 1)
            dve.wait_ge(small_in, 15 * 16)
            dve.wait_ge(cummax_ready, 2)
            for a, cols in enumerate(parts):
                link(dve.tensor_scalar(tab["g"][:, cols], tab["cm"][:, cols], mprev[:, a:a + 1], None, ALU.max))
            link(dve.tensor_scalar(tab["negg"][:, :], tab["g"][:, :], -1.0, None, ALU.mult))
            for a, cols in enumerate(parts):
                link(dve.tensor_copy(ngend[:, a:a + 1], tab["negg"][:, cols.stop - 1:cols.stop]))
            dve.tensor_tensor(tab["mt"][:, :], tab["b"][:, :], tab["g"][:, :], ALU.add).then_inc(g_ready, 1)
            dve.wait_ge(gexp_ready, 5)
            dve.tensor_scalar(tab["wend16"][:, :], tab["wend"][:, :], HD ** -0.5, None, ALU.mult).then_inc(tables_ready, 1)
            l1_part(2)
            wait_full(dve, round_full, R_COLS)
            dve.tensor_copy(colp[:, :, :].rearrange("p q r -> p (q r)"), bank(R_COLS, 4 * HC)
                            ).then_inc(round_free[R_COLS % 2], 1)
            wait_full(dve, round_full, R_COLS + 1)
            dve.tensor_copy(ext_s[:, :, :, 0:HIST], bank(R_COLS + 1, PG * NB * HIST).rearrange(
                "p (g b t) -> p g b t", g=PG, b=NB)).then_inc(round_free[(R_COLS + 1) % 2], 1)
            l1_part(3)

            def chunk_dve(c, i, slot):
                ci = i * 2 + c
                rb = R_L2 + RPC * c
                per = 2 * RPC
                if slot == 0:
                    dve.wait_ge(weights_exp, ci + 1)
                    wait_full(dve, round_full, rb, i, per)
                    dve.scalar_tensor_tensor(out=pT[:, :, :].rearrange("p h t -> p (h t)"), in0=bank(rb),
                                             scalar=HD ** -0.5,
                                             in1=wexp[:, c, :, :].rearrange("p h t -> p (h t)"),
                                             op0=ALU.mult, op1=ALU.mult).then_inc(round_free[rb % 2], 1)
                if slot in (2, 3):
                    r = rb + 1 + slot
                    wait_full(dve, round_full, r, i, per)
                    dve.tensor_copy(vext[:, 2 * slot - 4:2 * slot - 2, 0:HD], bank(r).rearrange("p (h e) -> p h e", e=HD)
                                    ).then_inc(round_free[r % 2], 1)
                if 4 <= slot < 20:
                    h, q = slot // 4 - 1, slot % 4
                    r = rb + 5 + 4 * h + q
                    if q == 1:
                        wait_full(dve, round_free, r - 1, i, per)
                        wait_full(dve, round_full, r, i, per)
                        dve.tensor_tensor(hn[:, h, :], bank(r, E1), hs[:, h, :], ALU.add).then_inc(round_free[r % 2], 1)
                        wait_full(dve, round_free, r, i, per)
                        link(dve.tensor_tensor_reduce(out=hf[:, h, :], in0=hn[:, h, 0:HD], in1=hn[:, h, 0:HD], scale=1.0,
                                                      scalar=0.0, op0=ALU.mult, op1=ALU.add, accum_out=sm[:, 0, h:h + 1]))
                    if q >= 2:
                        wait_full(dve, round_full, r, i, per)
                        a = q - 2
                        dve.scalar_tensor_tensor(out=cst[:, h, a, :], in0=cst[:, h, a, :], scalar=cur[:, c, 4, h:h + 1],
                                                 in1=bank(r, E1), op0=ALU.mult, op1=ALU.add
                                                 ).then_inc(round_free[r % 2], 1)
                if slot == 20:
                    den = hn[:, :, HD]
                    link(dve.scalar_tensor_tensor(out=sm[:, 1, :], in0=den, scalar=-1.0, in1=den, op0=ALU.mult, op1=ALU.max))
                    link(dve.tensor_tensor(sm[:, 1, :], sm[:, 1, :], cur[:, c, 2, :], ALU.max))
                    link(dve.reciprocal(sm[:, 2, :], sm[:, 1, :]))
                    link(dve.tensor_tensor(sm[:, 3, :], sm[:, 0, :], sm[:, 2, :], ALU.mult))
                    dve.tensor_tensor(sm[:, 3, :], sm[:, 3, :], sm[:, 2, :], ALU.mult).then_inc(msq_ready, 1)
                    dve.wait_ge(hstd_ready, ci + 1)
                    link(dve.reciprocal(sm[:, 5, :], sm[:, 4, :]))
                    link(dve.tensor_tensor(sm[:, 6, :], sm[:, 5, :], sm[:, 2, :], ALU.mult))
                    for h in range(H):
                        ins = dve.tensor_scalar(hf[:, h, :], hn[:, h, 0:HD], sm[:, 6, h:h + 1], None, ALU.mult)
                    ins.then_inc(hf_ready, 1)

            chunk_steps = 2 * (H + 6)
            with dve.Fori(0, NCK // 2) as i:
                enter(i, chunk_steps)
                for j in range(6):
                    for s in range(8):
                        chunk_dve(j // 3, i, (j % 3) * 8 + s)
                        if j and s == 3:
                            split_lo(U_L2 + j + 1, i, 6)
                split_lo(U_L2 + 7, i, 6)
                leave(NCK // 2, chunk_steps)

            wait_full(dve, round_full, R_UT)
            dve.tensor_copy(nT[:, :, :].rearrange("p a r -> p (a r)"), bank(R_UT, 2 * HC)).then_inc(round_free[R_UT % 2], 1)
            wait_full(dve, round_full, R_UT + 1)
            dve.tensor_copy(urows[:, :], bank(R_UT + 1, PW, HIST + SMP)).then_inc(round_free[(R_UT + 1) % 2], 1)
            wait_full(dve, round_free, R_UT)
            with dve.Fori(0, H // 2) as i:
                enter(i, 14)
                for s in range(2):
                    h = i * 2 + s
                    rb, per = R_SMP + RPH * s, 2 * RPH

                    def full(r):
                        wait_full(dve, round_full, rb + r, i, per)

                    def by_head(ap):
                        return ap[:, :, :].rearrange("p a (b h) -> p b a h", h=H)[:, :, :, ds(h, 1)].rearrange(
                            "p b a o -> p b (a o)")

                    dve.wait_ge(head_in[s], i * (11 * 16) + 11 * 16)
                    dve.tensor_copy(cs[:, s, :, :, HD], by_head(nT)).then_inc(n_ready, 1)
                    full(0)
                    dve.wait_ge(weights_exp, h + (NCK + 1))
                    dve.scalar_tensor_tensor(out=pTS[:, :], in0=bank(rb, SMP, SMP), scalar=HD ** -0.5,
                                             in1=wexpS[:, s, :], op0=ALU.mult, op1=ALU.mult
                                             ).then_inc(round_free[rb % 2], 1)
                    full(1)
                    dve.tensor_copy(ks[:, :], bank(rb + 1, HD, SMP)).then_inc(head_keys, 1)
                    dve.tensor_copy(vs[:, 0:HD], bank(rb + 1, 512, SMP)[:, HD:512]).then_inc(round_free[(rb + 1) % 2], 1)
                    wait_full(dve, round_free, rb + 2, i, per)
                    full(3)
                    dve.tensor_tensor(hnS[:, :], bank(rb + 3, E1, SMP), hsS[:, :], ALU.add
                                      ).then_inc(round_free[(rb + 3) % 2], 1)
                    wait_full(dve, round_free, rb + 3, i, per)
                    link(dve.tensor_tensor_reduce(out=hfS[:, :], in0=hnS[:, 0:HD], in1=hnS[:, 0:HD], scale=1.0,
                                                  scalar=0.0, op0=ALU.mult, op1=ALU.add, accum_out=smS[:, 0:1]))
                    den = hnS[:, HD:E1]
                    link(dve.scalar_tensor_tensor(out=smS[:, 1:2], in0=den, scalar=-1.0, in1=den, op0=ALU.mult, op1=ALU.max))
                    link(dve.tensor_tensor(smS[:, 1:2], smS[:, 1:2], curC[:, s, 2:3], ALU.max))
                    link(dve.reciprocal(smS[:, 2:3], smS[:, 1:2]))
                    link(dve.tensor_tensor(smS[:, 3:4], smS[:, 0:1], smS[:, 2:3], ALU.mult))
                    dve.tensor_tensor(smS[:, 3:4], smS[:, 3:4], smS[:, 2:3], ALU.mult).then_inc(msq_ready, 1)
                    for b in range(NB):
                        for a in range(2):
                            r = 4 + 2 * b + a
                            full(r)
                            dve.scalar_tensor_tensor(out=cs[:, s, b, a, :], in0=cs[:, s, b, a, :],
                                                     scalar=curD[:, s, b:b + 1], in1=bank(rb + r, E1),
                                                     op0=ALU.mult, op1=ALU.add).then_inc(round_free[(rb + r) % 2], 1)
                        if b == 1:
                            dve.wait_ge(hstd_ready, h + (NCK + 1))
                            link(dve.reciprocal(smS[:, 5:6], smS[:, 4:5]))
                            link(dve.tensor_tensor(smS[:, 6:7], smS[:, 5:6], smS[:, 2:3], ALU.mult))
                            dve.tensor_scalar(hfS[:, :], hnS[:, 0:HD], smS[:, 6:7], None, ALU.mult).then_inc(hf_ready, 1)
                    for r in (18, 19):
                        wait_full(dve, round_free, rb + r, i, per)
                    dve.tensor_copy(by_head(nO), cs[:, s, :, :, HD]).then_inc(nO_ready, 1)
                leave(H // 2, 14)
            wait_full(dve, round_full, R_NOUT)
            dve.tensor_copy(nout[:, :], bank(R_NOUT, HD, HC)).then_inc(round_free[R_NOUT % 2], 1)

            for g in range(PG):
                k = T_YP + g
                dve.wait_ge(yphi_ready, g + 1)
                dve.tensor_tensor(yp_lo[:, g, :], sq[:, :], yp_hi[:, g, :].bitcast(F32), ALU.subtract
                                  ).then_inc(tile_free[k % 2], 1)
            def gated(k, dst, i, per):
                sg = stage[:, k % 2, :]
                wait_full(dve, tile_full, k, i, per)
                dve.tensor_tensor(wide(dst), tile_wide(k), wide(sg), ALU.mult)
                dve.tensor_tensor(dst[:, 768:T], tile(k, 2), sg[:, 768:T], ALU.mult).then_inc(tile_free[k % 2], 1)

            with dve.Fori(0, 2) as i:
                for j in range(4):
                    kt = i * 4 + j
                    y = row(hmT, kt)
                    dve.wait_ge(osig_ready, kt + 1)
                    dve.scalar_tensor_tensor(out=y, in0=y, scalar=vec[:, ds(kt + V_HEAD, 1)], in1=oin[:, j % 2, :],
                                             op0=ALU.mult, op1=ALU.mult).then_inc(yml32_ready, 1)
                    dve.wait_ge(ymlhi_ready, kt + 1)
                    dve.tensor_tensor(row(act_lo, kt), y, row(act_hi, kt).bitcast(F32), ALU.subtract
                                      ).then_inc(yml_ready, 1)
                    dve.wait_ge(gsig_ready, kt + 1)
                    dve.wait_ge(yml_ready, kt + 1)
                    gated(T_BP + j, y, i, 4)
                    if j % 2:
                        split_lo(U_BP + 2 + j // 2, i, 2)
            with dve.Fori(0, 4) as i:
                for j in range(2):
                    k = T_BM + j
                    kt = i * 2 + j
                    m = row(hmT, kt)
                    dve.wait_ge(gsig_ready, kt + (KT + 1))
                    wait_full(dve, raw_free, U_BM + 1 + j, i, 2)
                    gated(k, sq[:, :], i, 2)
                    wait_full(dve, tile_free, k, i, 2)
                    dve.tensor_tensor(m, m, sq[:, :], ALU.add).then_inc(m32_ready, 1)
                    split_lo(U_BM + 2 + j, i, 2)
            for k in range(KT):
                low_rows(k, hmT[:, k, :], mhi_ready, m_ready)

            link(dve.memset(ssq[:, :], 0.0))
            with dve.Fori(0, 4) as i:
                enter(i, 6)
                for j in range(2):
                    k = T_OUT + j
                    kt = i * 2 + j
                    x1, xin = row(hmT, kt), stage[:, k % 2, :]
                    gt = mod[:, ds(kt + GT1, 1), :].rearrange("p o g -> p (o g)")
                    wait_full(dve, tile_full, k, i, 2)
                    wait_full(dve, gin_in, 16 + j, i, 2, 16)
                    link(dve.tensor_tensor(smp3(gsm[:, 0, :]), smp3(tile(k, 2, 256, 320)), per_batch(gt[:, 1:GRP]), ALU.mult))
                    dve.scalar_tensor_tensor(out=wide(x1), in0=tile_wide(k), scalar=gt[:, 0:1], in1=wide(xin),
                                             op0=ALU.mult, op1=ALU.add)
                    dve.scalar_tensor_tensor(out=x1[:, 768:SEQ], in0=tile(k, 2, 0, 256), scalar=gt[:, 0:1],
                                             in1=xin[:, 768:SEQ], op0=ALU.mult, op1=ALU.add)
                    dve.tensor_tensor(x1[:, SEQ:T], gsm[:, 0, :], xin[:, SEQ:T], ALU.add).then_inc(tile_free[k % 2], 1)
                    wait_full(dve, tile_free, k, i, 2)
                    link(dve.tensor_tensor(sq[:, :], x1, x1, ALU.mult))
                    link(dve.tensor_tensor(ssq[:, :], ssq[:, :], sq[:, :], ALU.add))
                    split_lo(U_OUT + 2 + j, i, 2)
                leave(4, 6)
            dve.sem_inc(xsum_ready, 1)
            link(dve.scalar_tensor_tensor(out=amp2[:, :, :], in0=mod[:, SC2:SC2 + KT, :], scalar=1.0,
                                          in1=vec[:, V_FFN:V_FFN + KT].unsqueeze(2).to_broadcast([P, KT, GRP]),
                                          op0=ALU.add, op1=ALU.mult))
            dve.wait_ge(std2_ready, 1)
            dve.reciprocal(sq[:, :], sq[:, :]).then_inc(tile_free[T_N2 % 2], 1)
            wait_full(dve, tile_free, T_N2)
            for k in range(KT):
                s = (sil, a32[:, 0, :])[k % 2]
                s = s[:, :]
                link(dve.tensor_tensor(s, hmT[:, k, :], sq[:, :], ALU.mult))
                norm_rows(k, s, amp2, SH2, h2f_ready, h2_ready)
                if k:
                    low_rows(k - 1, h32[:, (k - 1) % 2, :], h2hi_ready, h2_ready)
            low_rows(KT - 1, h32[:, (KT - 1) % 2, :], h2hi_ready, h2_ready)

            dve.wait_ge(h2_ready, KT)

            def ffn_dve(i, last=False):
                for j in range(4):
                    k, f = T_FFN + j, j // 2
                    if j % 2 == 0:
                        dve.wait_ge(sil_ready, i * 2 + (f + 1))
                        dve.sem_inc(tile_free[k % 2], 1)
                    else:
                        wait_full(dve, tile_full, k, i, 12)
                        dve.tensor_tensor(wide(a32[:, f, :]), tile_wide(k), wide(sil[:, :]), ALU.mult)
                        dve.tensor_tensor(a32[:, f, 768:T], tile(k, 2), sil[:, 768:T], ALU.mult).then_inc(a32_ready, 1)
                        dve.wait_ge(ahi_ready, i * 2 + (f + 1))
                        dve.tensor_tensor(a_lo[:, f, :], a32[:, f, :], a_hi[:, f, :].bitcast(F32), ALU.subtract
                                          ).then_inc(tile_free[k % 2], 1)
                    split_lo(U_FFN + j + 2, i, 6)
                for o in range(KT):
                    k = T_FFN + 4 + o
                    x1 = hmT[:, o, :]
                    gt = mod[:, GT2 + o, :]
                    wait_full(dve, tile_full, k, i, 12)
                    dve.scalar_tensor_tensor(out=wide(x1), in0=tile_wide(k), scalar=gt[:, 0:1], in1=wide(x1),
                                             op0=ALU.mult, op1=ALU.add)
                    dve.scalar_tensor_tensor(out=x1[:, 768:SEQ], in0=tile(k, 2, 0, 256), scalar=gt[:, 0:1],
                                             in1=x1[:, 768:SEQ], op0=ALU.mult, op1=ALU.add)
                    g = gsm[:, o % 2, :]
                    dve.tensor_tensor(smp3(g), smp3(tile(k, 2, 256, 320)), per_batch(gt[:, 1:GRP]), ALU.mult
                                      ).then_inc(tile_free[k % 2], 1)
                    wait_full(dve, tile_free, k, i, 12)
                    dve.tensor_tensor(x1[:, SEQ:T], g, x1[:, SEQ:T], ALU.add).then_inc(x2_ready, 1)
                    if o % 4 == 3 and not last:
                        split_lo(U_FFN + 6 + o // 4, i, 6)

            with dve.Fori(0, FT // 2 - 1) as i:
                ffn_dve(i)
            ffn_dve(FT // 2 - 1, last=True)

            for k in range(KT):
                dve.wait_ge(x2sq_ready, k + 1)
                s = (sq, sil)[k % 2][:, :]
                if k == 0:
                    dve.tensor_copy(ssq[:, :], s).then_inc(x2sum_ready, 1)
                else:
                    dve.wait_ge(x2sum_ready, k)
                    dve.tensor_tensor(ssq[:, :], ssq[:, :], s, ALU.add).then_inc(x2sum_ready, 1)
                dve.tensor_scalar(hmT[:, k, :], hmT[:, k, :], vec[:, V_FIN + k:V_FIN + k + 1], None, ALU.mult
                                  ).then_inc(xg_ready, 1)
            dve.wait_ge(rstd3_ready, 2)
            dve.reciprocal(rcol[:, 0:8], rcol[:, 0:8]).then_inc(rcol_ready, 1)
            dve.reciprocal(rcol[0:SMP, 8:9], rcol[0:SMP, 8:9]).then_inc(rcol_ready, 1)
            dve.wait_ge(rcol_ready, 2)
            for tt in range(TT):
                k, rows = T_Y + tt, P if tt < 8 else SMP
                wait_full(dve, tile_full, k)
                if tt >= 2:
                    dve.wait_ge(y_out[tt % 2], 16 * (tt // 2))
                dve.tensor_scalar(ytok[0:rows, tt % 2, 512:1024], dense[0:rows, 3 * (k % 2) + 1, :],
                                  rcol[0:rows, tt:tt + 1], None, ALU.mult).then_inc(ytok_dve, 1)

        @block.tensor
        def _(pe):
            def products(k, n, off, kk, last, x_hi, x_lo):
                hi, lo = w_hi[:, n % 2, off:off + P], w_lo[:, n % 2, off:off + P]
                for w, x in ((hi, x_hi), (hi, x_lo), (lo, x_hi)):
                    for c, (t0, t1) in enumerate(CH):
                        ins = pe.matmul(tile(k, c), w, x[:, kk, t0:t1], start=(kk == 0 and x is x_hi and w is hi),
                                        stop=(last and w is lo))
                if last:
                    ins.then_inc(tile_full[k % 2], 1)

            def halves(n, i=0, per=0):
                wait_full(pe, raw_free, n, i, per)

            def free_tile(k, i=0, per=0):
                wait_free(pe, tile_free, k, i, per)

            def take(r, i=0, per=0):
                wait_free(pe, round_free, r, i, per)

            def give(ins, r):
                ins.then_inc(round_full[r % 2], 1)

            def unit(n, k, i=0, per=0, between=None, ready=None):
                halves(n, i, per)
                free_tile(k, i, per)
                for kk in range(KT):
                    if ready is not None:
                        pe.wait_ge(ready, kk + 1)
                    products(k, n, P * kk, kk, kk == KT - 1, act_hi, act_lo)
                    if between is not None:
                        between(kk)

            pe.wait_ge(consts_ready, 3)
            pe.wait_ge(small_in, 15 * 16)
            give(pe.transpose(bank(R_VEC, NV), vrow[:, :], ident[0:NV, 0:NV]), R_VEC)
            pe.wait_ge(silu_ready, 1)
            for k in range(KT):
                ins = pe.transpose(misc[:, R_CT % 2, GRP * k:GRP * k + GRP], stage[0:GRP, 0, P * k:P * k + P],
                                   ident[0:GRP, 0:GRP])
            give(ins, R_CT)
            pe.wait_ge(x_in[2], 16)
            for k in range(KT):
                if k % 4 == 0:
                    pe.wait_ge(x_in[k // 4], 16)
                free_tile(k)
                for j in range(TT):
                    rows = P if j < 8 else SMP
                    c = j // 3
                    ins = pe.transpose(tile(k, c, P * (j - 3 * c), P * (j - 3 * c) + rows),
                                       xtok[0:rows, j, P * k:P * k + P], ident[0:rows, 0:rows])
                ins.then_inc(tile_full[k % 2], 1)

            def sum_partitions(k, src):
                free_tile(k)
                for c, (t0, t1) in enumerate(CH):
                    ins = pe.matmul(tile(k, c), ones[:, :], src[:, t0:t1], start=True, stop=True)
                ins.then_inc(tile_full[k % 2], 1)

            pe.wait_ge(ssq_ready, KT)
            sum_partitions(T_SS, xssq)

            def ada(r, a, col, i=0, per=0, aper=0):
                if col == 0:
                    wait_full(pe, ada_in, a, i, aper, 16)
                take(r, i, per)
                for kk in range(KT):
                    ins = pe.matmul(bank(r, GRP), ada_w[:, a % 2, kk, P * col:P * col + P], cT[:, kk, :],
                                    start=(kk == 0), stop=(kk == KT - 1))
                give(ins, r)

            wait_full(pe, round_free, R_CT)
            for a in range(ADA0 // 2):
                for col in range(2):
                    ada(R_ADA + 2 * a + col, a, col)
            unit(0, T_GATE, ready=h_ready)

            def l1_part(part):
                lo, hi = L1_CUTS[part]
                rb = R_SEG[part]
                with pe.Fori(lo // 2, hi // 2) as i:
                    for jj in range(2):
                        a = ADA0 // 2 + jj
                        for j in range(2):
                            jt = 2 * jj + j
                            unit(U_L1 + jt, T_L1 + jt, i, 4)
                            ada(rb + jt, a, j, i, 4, 2)

            l1_part(0)
            l1_part(1)
            pe.wait_ge(cummax_ready, 2)
            take(R_GATES)
            for a, n in enumerate(("b", "cm")):
                ins = pe.matmul(misc[0:1, R_GATES % 2, HC * a:HC * a + HC], tab[n][:, CK - 1:CK], ident[0:HC, 0:HC],
                                start=True, stop=True)
            give(ins, R_GATES)
            pe.wait_ge(mprow_ready, 1)
            take(R_GATES + 1)
            give(pe.matmul(bank(R_GATES + 1, 1, HC), mprow[0:1, :], ones[0:1, 0:1], start=True, stop=True), R_GATES + 1)
            l1_part(2)
            pe.wait_ge(tables_ready, 1)
            take(R_COLS)
            for q, n in enumerate(("r", "winter", "emt", "wend16")):
                ins = pe.transpose(misc[:, R_COLS % 2, HC * q:HC * q + HC], tab[n][:, 0:CK], ident[0:HC, 0:HC])
            give(ins, R_COLS)
            take(R_COLS + 1)
            rows = NB * HIST
            for g in range(PG):
                ins = pe.transpose(misc[:, (R_COLS + 1) % 2, rows * g:rows * g + rows], hrow[:, P * g:P * g + P],
                                   ident[0:rows, 0:rows])
            give(ins, R_COLS + 1)
            l1_part(3)

            def chunk_pe(c, i, slot):
                rb, per = R_L2 + RPC * c, 2 * RPC
                q, k, v = (qkv[:, c, 8 * g:8 * g + 8, :] for g in range(3))

                def turned(src, r):
                    take(r, i, per)
                    for a in range(4):
                        ins = pe.transpose(bank(r)[:, P * a:P * a + P], src[:, a, :], ident[:, :])
                    give(ins, r)

                if slot == 0:
                    pe.wait_ge(qkv_in[c], i * 32 + 32)
                    take(rb, i, per)
                    for h in range(H):
                        for a in range(2):
                            ins = pe.matmul(bank(rb)[:, CK * h:CK * h + CK], k[:, 2 * h + a, :], q[:, 2 * h + a, :],
                                            start=(a == 0), stop=(a == 1))
                    give(ins, rb)
                    turned(k[:, 0:4, :], rb + 1)
                if slot == 1:
                    turned(k[:, 4:8, :], rb + 2)
                if slot in (2, 3):
                    turned(v[:, 4 * slot - 8:4 * slot - 4, :], rb + 1 + slot)
                if 4 <= slot < 20:
                    h, p = slot // 4 - 1, slot % 4
                    r = rb + 5 + 4 * h + p
                    take(r, i, per)
                    if p == 0:
                        if h == 0:
                            pe.wait_ge(mls_init, 2)
                        for a in range(2):
                            ins = pe.matmul(bank(r, E1), q[:, 2 * h + a, :], cst[:, h, a, :], start=(a == 0), stop=(a == 1))
                    elif p == 1:
                        ins = pe.matmul(bank(r, E1), pT[:, h, :], vext[:, h, :], start=True, stop=True)
                    else:
                        ins = pe.matmul(bank(r, E1), kw[:, h, P * (p - 2):P * (p - 1)], vext[:, h, :], start=True, stop=True)
                    give(ins, r)
                if slot == 23:
                    pe.wait_ge(hf_ready, i * 2 + (c + 1))
                    for a in range(2):
                        turned(hf[:, 2 * a:2 * a + 2, :].rearrange("p h (a t) -> p (h a) t", a=2), rb + 21 + a)

            with pe.Fori(0, NCK // 2) as i:
                for j in range(6):
                    def between(kk, j=j):
                        chunk_pe(j // 3, i, (j % 3) * 8 + kk)
                    unit(U_L2 + j, T_L2 + j, i, 6, between)

            pe.wait_ge(nrow_in, 16)
            take(R_UT)
            for a in range(2):
                ins = pe.transpose(misc[:, R_UT % 2, HC * a:HC * a + HC], nrow[:, P * a:P * a + P], ident[0:HC, 0:HC])
            give(ins, R_UT)
            pe.wait_ge(ulast_in, 16)
            take(R_UT + 1)
            for g in range(PG):
                ins = pe.transpose(misc[0:HIST + SMP, (R_UT + 1) % 2, P * g:P * g + P], ulast[:, g, :], ident[:, :])
            give(ins, R_UT + 1)
            pe.wait_ge(vs_init, 1)
            with pe.Fori(0, H // 2) as i:
                for s in range(2):
                    rb, per = R_SMP + RPH * s, 2 * RPH
                    h = i * 2 + s

                    def take_s(r):
                        take(r, i, per)
                        pe.sem_inc(pe_passed, 1)

                    qs, kks, vvs = (qkvs[:, s, 2 * g:2 * g + 2, :] for g in range(3))
                    pe.wait_ge(head_in[s], i * (11 * 16) + 11 * 16)
                    take_s(rb)
                    for a in range(2):
                        ins = pe.matmul(bank(rb, SMP, SMP), kks[:, a, :], qs[:, a, :], start=(a == 0), stop=(a == 1))
                    give(ins, rb)
                    take_s(rb + 1)
                    for g, src in enumerate((kks, vvs)):
                        for a in range(2):
                            c0 = HD * g + P * a
                            ins = pe.transpose(misc[0:SMP, (rb + 1) % 2, c0:c0 + P], src[:, a, :], ident[:, :])
                    give(ins, rb + 1)
                    pe.wait_ge(n_ready, h + 1)
                    pe.wait_ge(head_prep, h * 11 + 11)
                    take_s(rb + 2)
                    for b in range(NB):
                        for a in range(2):
                            ins = pe.matmul(bank(rb + 2, E1, SMP), qm[:, s, b, a, :], cs[:, s, b, a, :],
                                            start=(b == 0 and a == 0), stop=(b == NB - 1 and a == 1))
                    give(ins, rb + 2)
                    take_s(rb + 3)
                    give(pe.matmul(bank(rb + 3, E1, SMP), pTS[:, :], vs[:, :], start=True, stop=True), rb + 3)
                    for b in range(NB):
                        for a in range(2):
                            r = rb + 4 + 2 * b + a
                            if a == 0:
                                pe.wait_ge(head_kb, h * NB + (b + 1))
                            take_s(r)
                            give(pe.matmul(bank(r, E1), kb[:, b, P * a:P * a + P], vs[:, :], start=True, stop=True), r)
                    pe.wait_ge(hf_ready, h + (NCK + 1))
                    take_s(rb + 20)
                    for a in range(2):
                        ins = pe.transpose(misc[:, (rb + 20) % 2, SMP * a:SMP * a + SMP], hfS[:, P * a:P * a + P],
                                           ident[0:SMP, 0:SMP])
                    give(ins, rb + 20)
            pe.wait_ge(nO_ready, H)
            take(R_NOUT)
            for a in range(2):
                ins = pe.transpose(misc[0:HC, R_NOUT % 2, P * a:P * a + P], nO[:, a, :], ident[:, :])
            give(ins, R_NOUT)

            pe.wait_ge(wpool_in, 16)
            for g in range(PG):
                k = T_YP + g
                free_tile(k)
                wait_full(pe, d_in, g, inc=16)
                for c, (t0, t1) in enumerate(CH):
                    ins = pe.matmul(tile(k, c), wpool[:, g, :], dT[:, g % 2, t0:t1], start=True, stop=True)
                ins.then_inc(tile_full[k % 2], 1)
            for g in (PG - 2, PG - 1):
                wait_full(pe, tile_free, T_YP + g)
            with pe.Fori(0, 2) as i:
                for u in range(2):
                    halves(U_BP + u, i, 2)
                    for o in range(2):
                        k = T_BP + 2 * u + o
                        free_tile(k, i, 4)
                        for kk in range(PG):
                            products(k, U_BP + u, 256 * kk + P * o, kk, kk == PG - 1, yp_hi, yp_lo)
            pe.wait_ge(yml_ready, KT)
            with pe.Fori(0, 4) as i:
                for j in range(2):
                    unit(U_BM + j, T_BM + j, i, 2)
            unit(U_OUT, T_OUT, ready=m_ready)
            unit(U_OUT + 1, T_OUT + 1)
            with pe.Fori(1, 4) as i:
                for j in range(2):
                    unit(U_OUT + j, T_OUT + j, i, 2)
            pe.wait_ge(xsum_ready, 1)
            sum_partitions(T_N2, ssq)

            def ffn_pe(i, ready=None):
                for j in range(4):
                    ffn_up(i, j, ready)
                wait_full(pe, tile_free, T_FFN + 3, i, 12)
                for j in range(2):
                    n = U_FFN + 4 + j
                    halves(n, i, 6)
                    for o in range(4):
                        k = T_FFN + 4 + 4 * j + o
                        free_tile(k, i, 12)
                        for f in range(2):
                            products(k, n, 512 * f + P * o, f, f == 1, a_hi, a_lo)

            def ffn_up(i, j, ready):
                n, k = U_FFN + j, T_FFN + j
                halves(n, i, 6)
                free_tile(k, i, 12)
                for kk in range(KT):
                    if ready is not None and j == 0:
                        pe.wait_ge(ready, kk + 1)
                    products(k, n, P * kk, kk, kk == KT - 1, act_hi, act_lo)

            ffn_pe(0, h2_ready)
            with pe.Fori(1, FT // 2) as i:
                ffn_pe(i)

            pe.wait_ge(x2sum_ready, KT)
            take(R_Y)
            for tt in range(TT):
                rows = P if tt < 8 else SMP
                ins = pe.matmul(misc[0:rows, R_Y % 2, tt:tt + 1], ssq[:, P * tt:P * tt + rows], ones[:, 0:1],
                                start=True, stop=True)
            give(ins, R_Y)
            pe.wait_ge(xg_ready, KT)
            for tt in range(TT):
                k, rows = T_Y + tt, P if tt < 8 else SMP
                if tt < 2:
                    free_tile(k)
                else:
                    pe.wait_ge(ytok_act, tt - 1)
                    pe.wait_ge(ytok_dve, tt - 1)
                for kk in range(KT):
                    ins = pe.transpose(dense[0:rows, 3 * (k % 2) + kk // 4, P * (kk % 4):P * (kk % 4) + P],
                                       hmT[:, kk, P * tt:P * tt + rows], ident[:, :])
                ins.then_inc(tile_full[k % 2], 1)


_INS = ['x_prompt', 'x_sample', 'c_prompt', 'c_sample', 'state_pool', 'state_mlstm_c', 'state_mlstm_n',
        'state_mlstm_m', 'g_mix', 'g_ffn', 'g_final', 'w_ada', 'b_ada', 'w_in', 'b_igate', 'b_fgate', 'w_pool',
        's_pool', 'g_head', 'w_branch_pool', 'w_branch_mlstm', 'w_out', 'w_gate_up', 'w_down']
_OUTS = [(1, SEQ, D), (NB, NT, D),
         (1, 1, HIST, PW), (1, 1, H, HD, HD), (1, 1, H, HD), (1, 1, H),
         (1, NB, HIST, PW), (1, NB, H, HD, HD), (1, NB, H, HD), (1, NB, H)]


def kernel(**inputs):
    import numpy as _np
    import concourse.bacc as _bacc
    from concourse import mybir as _mybir
    from concourse.bass_utils import run_bass_kernel_spmd as _run

    nc = _bacc.Bacc("TRN2", target_bir_lowering=False, num_devices=1)
    arrays, args = {}, []
    for name in _INS:
        a = _np.ascontiguousarray(inputs[name])
        arrays[f"in_{name}_dram"] = a
        args.append(nc.dram_tensor(f"in_{name}_dram", a.shape, _mybir.dt.from_np(a.dtype), kind="ExternalInput").ap())
    for i, shape in enumerate(_OUTS):
        args.append(nc.dram_tensor(f"out_{i}_dram", shape, _mybir.dt.float32, kind="ExternalOutput").ap())
    trunk(nc, *args)
    r = _run(nc, [arrays], core_ids=[0])
    return tuple(r.results[0][f"out_{i}_dram"] for i in range(len(_OUTS)))
```

```python
from contextlib import ExitStack

import concourse.bass as bass
from concourse import mybir

F32 = mybir.dt.float32
F32R = mybir.dt.float32r
ALU = mybir.AluOpType
ACT = mybir.ActivationFunctionType
ds = bass.ds

P = 128
D = 1024
KT = D // P
SEQ = 1024
NB, NT = 8, 8
SMP = NB * NT
T = SEQ + SMP
TT = 9
CH = ((0, 384), (384, 768), (768, T))
GRP = 1 + NB
PW = 512
PG = PW // P
HIST = 15
H = 4
HD = 256
CK = 128
NCK = SEQ // CK
HC = H * NCK
GL = CK + NT
E1 = HD + 1
FF = 2816
FT = FF // P
FI = FT // 2
EPS = 1e-6
NEG = -1e30
NA = 6 * KT
V_MIX, V_FFN, V_FIN, V_HEAD, V_POOL, V_ADA = 0, 8, 16, 24, 32, 36
NV = V_ADA + NA
SH1, SC1, GT1, SH2, SC2, GT2 = (KT * j for j in range(6))
Z_U, Z_Q, Z_K, Z_V, Z_O, Z_GP, Z_GM, Z_X, Z_D = 0, 4, 12, 20, 28, 36, 44, 52, 60
GATE_COL = PW + 4 * D
U_L1, U_L2, U_BP, U_BM, U_OUT, U_FFN = 1, 29, 53, 57, 65, 73
T_SS, T_GATE, T_L1, T_L2, T_YP, T_BP, T_BM, T_OUT, T_N2, T_FFN = 8, 9, 10, 38, 62, 66, 74, 82, 90, 91
T_Y = T_FFN + 6 * FT
R_CT, R_VEC, R_ADA = 0, 1, 2
ADA0 = 20
A_NORM = KT
R_SS = R_ADA + 2 * (A_NORM - 1)
R_L1 = R_ADA + ADA0 + 1
L1_CUTS = ((0, 2), (2, 4), (4, 6), (6, 14))
R_SEG = (R_L1, R_L1, R_L1 + 2, R_L1 + 4)
R_GATES = R_L1 + 8
R_COLS = R_L1 + 14
R_L2 = R_L1 + 32
RPC = 23
R_UT = R_L2 + NCK * RPC
R_SMP = R_UT + 2
RPH = 21
R_NOUT = R_SMP + H * RPH
R_N2 = R_NOUT + 1
R_Y = R_N2 + 1


def ada_rounds(a):
    r = R_ADA + 2 * a + (a >= A_NORM - 1)
    return r, r + 1


def last_tile(n):
    if n < U_BP:
        return n + T_GATE
    if n < U_BM:
        return T_BP + 2 * (n - U_BP) + 1
    if n < U_FFN:
        return n - U_BM + T_BM
    if n == U_FFN:
        return T_FFN
    q, r = divmod(n - U_FFN - 1, 6)
    ups = 4 if q < FI - 1 else 3
    return T_FFN + 1 + 12 * q + (r if r < ups else 4 * r - 3 * ups + 3)


def trunk(nc, x_prompt, x_sample, c_prompt, c_sample, state_pool, state_c, state_n, state_m,
          g_mix, g_ffn, g_final, w_ada, b_ada, w_in, b_igate, b_fgate, w_pool, s_pool, g_head,
          w_bp, w_bm, w_out, w_gu, w_down,
          y_prompt, y_sample, pool_p, c_p, n_p, m_p, pool_s, c_s, n_s, m_s):
    z = nc.dram_tensor("z_scratch", (64, P, T), F32).ap()
    gate_rows_p = nc.dram_tensor("gate_rows_p", (8, SEQ), F32).ap()
    gate_rows_s = nc.dram_tensor("gate_rows_s", (8, SMP), F32).ap()
    negg_dram = nc.dram_tensor("negg_rows", (HC, CK), F32).ap()
    tab_s_dram = nc.dram_tensor("tab_s", (5, HC, NT), F32).ap()
    decay_dram = nc.dram_tensor("decay_rows", (2, HC), F32).ap()

    top = ExitStack()
    with top:
        top.enter_context(nc.allow_non_contiguous_dma(reason="single columns of gates, stabilisers and normalisers"))
        def sem(name):
            return top.enter_context(nc.semaphore(name))

        def sb(stack, name, shape, dt=F32):
            return stack.enter_context(nc.sbuf_tensor(name, shape, dt))

        ident = sb(top, "ident", [P, P])
        ones = sb(top, "ones", [P, P])
        vec = sb(top, "vec", [P, NV])
        mod = sb(top, "mod", [P, NA, GRP])
        amp1 = sb(top, "amp1", [P, KT, GRP])
        amp2 = sb(top, "amp2", [P, KT, GRP])
        epsc = sb(top, "epsc", [P, 1])
        raw = sb(top, "raw", [P, 2, 1024])
        w_hi = sb(top, "w_hi", [P, 2, 1024], F32R)
        w_lo = sb(top, "w_lo", [P, 2, 1024], F32R)
        act_hi = sb(top, "act_hi", [P, KT, T], F32R)
        act_lo = sb(top, "act_lo", [P, KT, T], F32R)
        stage = sb(top, "stage", [P, 2, T])
        dec = sb(top, "dec", [P, 2, HC])
        colp = sb(top, "colp", [P, 4, HC])
        scol = sb(top, "scol", [SMP, 4, H])
        negg_s = sb(top, "negg_s", [SMP, H, SMP])
        gbias = sb(top, "gbias", [8, 1])
        mprev = sb(top, "mprev", [HC, 2])
        rcol = sb(top, "rcol", [P, TT])

        early = ExitStack()
        xtok = sb(early, "xtok", [P, TT, D])
        xn = xtok[:, :, :].rearrange("p j d -> p (j d)")[:, 0:KT * T].rearrange("p (k t) -> p k t", t=T)
        xT = sb(early, "xT", [P, KT, T])
        ada_w = sb(early, "ada_w", [P, 2, KT, 256])
        xsq = sb(early, "xsq", [P, 2, T])
        xssq = sb(early, "xssq", [P, T])
        cT = sb(early, "cT", [P, KT, GRP])
        vrow = sb(early, "vrow", [NV, P])
        hrow = sb(early, "hrow", [NB * HIST, PW])
        early.close()
        h32 = stage
        cc, csig = stage[0:GRP, 0, 0:D], stage[0:GRP, 1, 0:D]
        mod_rows = negg_s[0:GRP, :, :].rearrange("p h t -> p (h t)")
        mixer = ExitStack()
        ext_p = sb(mixer, "ext_p", [P, PG, HIST + SEQ])
        ext_s = sb(mixer, "ext_s", [P, PG, NB, HIST + NT])
        win = sb(mixer, "win", [P, 2, HIST + SEQ])
        mixer.close()
        gtab = ExitStack()
        sb(gtab, "over_xtok", [P, TT * D])
        gates = sb(gtab, "gates", [8, T])
        tab = {n: sb(gtab, "tab_" + n, [HC, GL]) for n in
               ("ig", "fg", "abs", "exp", "ln", "lf", "b", "r", "cm", "g", "negg", "mt", "winter", "emt", "wend", "wend16")}
        zeros = sb(gtab, "zeros", [HC, GL])
        ngend = sb(gtab, "ngend", [HC, 2])
        rows2 = sb(gtab, "rows2", [1, 2, HC])
        mnext = sb(gtab, "mnext", [1, HC])
        mprow = sb(gtab, "mprow", [1, HC])
        invcnt = sb(gtab, "invcnt", [P, PG, 16])
        gtab.close()

        hmT = sb(top, "hmT", [P, KT, T])
        mls = ExitStack()
        cst = sb(mls, "cst", [P, H, 2, E1])
        qkv = sb(mls, "qkv", [P, 2, 24, CK])
        neggb = sb(mls, "neggb", [P, 2, H, CK])
        wexp = sb(mls, "wexp", [P, 2, H, CK])
        pT = sb(mls, "pT", [P, H, CK])
        kw = sb(mls, "kw", [P, H, HD])
        vext = sb(mls, "vext", [P, H, E1])
        hs = sb(mls, "hs", [P, H, E1])
        hn = sb(mls, "hn", [P, H, E1])
        hf = sb(mls, "hf", [P, H, HD])
        cur = sb(mls, "cur", [P, 2, 5, H])
        sm = sb(mls, "sm", [P, 8, H])
        mask = sb(mls, "mask", [P, CK])
        mls.close()
        smp = ExitStack()
        cs = sb(smp, "cs", [P, 2, NB, 2, E1])
        qkvs = sb(smp, "qkvs", [P, 2, 6, SMP])
        qm = sb(smp, "qm", [P, 2, NB, 2, SMP])
        argS = sb(smp, "argS", [SMP, 2, SMP])
        wexpS = sb(smp, "wexpS", [SMP, 2, SMP])
        pTS = sb(smp, "pTS", [SMP, SMP])
        ks = sb(smp, "ks", [SMP, HD])
        vs = sb(smp, "vs", [SMP, E1])
        kb = sb(smp, "kb", [SMP, NB, HD])
        hsS = sb(smp, "hsS", [SMP, E1])
        hnS = sb(smp, "hnS", [SMP, E1])
        hfS = sb(smp, "hfS", [SMP, HD])
        junkS = sb(smp, "junkS", [SMP, HD])
        curD = sb(smp, "curD", [P, 2, NB])
        curC = sb(smp, "curC", [SMP, 2, 4])
        wmask = sb(smp, "wmask", [SMP, 2, NB])
        smS = sb(smp, "smS", [SMP, 8])
        maskS = sb(smp, "maskS", [SMP, SMP])
        blk = sb(smp, "blk", [SMP, NB])
        nrow = sb(smp, "nrow", [HC, HD])
        nT = sb(smp, "nT", [P, 2, HC])
        nO = sb(smp, "nO", [P, 2, HC])
        nout = sb(smp, "nout", [HC, HD])
        urows = sb(smp, "urows", [HIST + SMP, PW])
        ulast = sb(smp, "ulast", [P, PG, HIST + SMP])
        smp.close()
        sq = sb(top, "sq", [P, T])
        ssq = sb(top, "ssq", [P, T])
        brn = ExitStack()
        yp_hi = sb(brn, "yp_hi", [P, PG, T], F32R)
        yp_lo = sb(brn, "yp_lo", [P, PG, T], F32R)
        oin = sb(brn, "oin", [P, 2, T])
        wpool = sb(brn, "wpool", [P, PG, P])
        dT = sb(brn, "dT", [P, 2, T])
        brn.close()
        ffn = ExitStack()
        a_hi = sb(ffn, "a_hi", [P, 2, T], F32R)
        a_lo = sb(ffn, "a_lo", [P, 2, T], F32R)
        a32 = sb(ffn, "a32", [P, 2, T])
        sil = sb(ffn, "sil", [P, T])
        gsm = sb(ffn, "gsm", [P, 2, SMP])
        ytok = sb(ffn, "ytok", [P, 2, D])
        ffn.close()

        dense = top.enter_context(nc.psum_tensor("dense", [P, 6, 512], F32))
        misc = top.enter_context(nc.psum_tensor("misc", [P, 2, 512], F32))

        def pair(name):
            return [sem(name + "0"), sem(name + "1")]

        consts_ready = sem("consts_ready")
        c_in = sem("c_in")
        small_in, nrow_in, ulast_in, wpool_in = sem("small_in"), sem("nrow_in"), sem("ulast_in"), sem("wpool_in")
        x_in = [sem(f"x_in{j}") for j in range(3)]
        raw_in, raw_free = pair("raw_in"), pair("raw_free")
        ada_in, ada_free = pair("ada_in"), pair("ada_free")
        hi_ready = sem("hi_ready")
        tile_full, tile_free = pair("tile_full"), pair("tile_free")
        round_full, round_free = pair("round_full"), pair("round_free")
        stage_out = pair("stage_out")
        csig_ready, silu_ready = sem("csig_ready"), sem("silu_ready")
        xsq_ready, ssq_ready, xn_ready = sem("xsq_ready"), sem("ssq_ready"), sem("xn_ready")
        std_ready, diag_ready, x_spilled = sem("std_ready"), sem("diag_ready"), sem("x_spilled")
        h32_ready, hhi_ready, h_ready = sem("h32_ready"), sem("hhi_ready"), sem("h_ready")
        dve_step, act_step, pool_step = sem("dve_step"), sem("act_step"), sem("pool_step")
        gates_ready, gates_out, gates_in = sem("gates_ready"), sem("gates_out"), sem("gates_in")
        lnterm_ready, cummax_ready, mprow_ready = sem("lnterm_ready"), sem("cummax_ready"), sem("mprow_ready")
        g_ready, gexp_ready, tables_ready = sem("g_ready"), sem("gexp_ready"), sem("tables_ready")
        tables_out, tables_in = sem("tables_out"), sem("tables_in")
        ext_in, d_out = sem("ext_in"), sem("d_out")
        qkv_in, mls_init, chunk_prep = pair("qkv_in"), sem("mls_init"), sem("chunk_prep")
        weights_exp, inter_ready = sem("weights_exp"), sem("inter_ready")
        msq_ready, hstd_ready, hf_ready = sem("msq_ready"), sem("hstd_ready"), sem("hf_ready")
        outs = sem("outs")
        head_in, cs_out = pair("head_in"), pair("cs_out")
        vs_init, head_prep, head_keys, head_kb = sem("vs_init"), sem("head_prep"), sem("head_keys"), sem("head_kb")
        pe_passed, pool_passed = sem("pe_passed"), sem("pool_passed")
        n_ready, nO_ready = sem("n_ready"), sem("nO_ready")
        d_in = pair("d_in")
        yphi_ready = sem("yphi_ready")
        gin_in, oin_in = pair("gin_in"), pair("oin_in")
        gsig_ready, osig_ready = sem("gsig_ready"), sem("osig_ready")
        yml32_ready, ymlhi_ready, yml_ready = sem("yml32_ready"), sem("ymlhi_ready"), sem("yml_ready")
        m32_ready, mhi_ready, m_ready = sem("m32_ready"), sem("mhi_ready"), sem("m_ready")
        xsum_ready, x1n_ready = sem("xsum_ready"), sem("x1n_ready")
        h2f_ready, h2hi_ready, h2_ready = sem("h2f_ready"), sem("h2hi_ready"), sem("h2_ready")
        sil_ready, a32_ready, ahi_ready = sem("sil_ready"), sem("a32_ready"), sem("ahi_ready")
        x2_ready, x2sq_ready, x2sum_ready = sem("x2_ready"), sem("x2sq_ready"), sem("x2sum_ready")
        rcol_ready, xg_ready = sem("rcol_ready"), sem("xg_ready")
        ytok_act, ytok_dve, y_out = sem("ytok_act"), sem("ytok_dve"), pair("y_out")

        def turn(k, i=0, per=0):
            assert per % 2 == 0
            return k % 2, k // 2 + i * (per // 2)

        def wait_full(eng, sems, k, i=0, per=0, inc=1):
            slot, n = turn(k, i, per)
            eng.wait_ge(sems[slot], n * inc + inc)

        def wait_free(eng, sems, k, i=0, per=0):
            slot, n = turn(k, i, per)
            if per or n:
                eng.wait_ge(sems[slot], n)

        def tile(k, c, lo=0, hi=None):
            return dense[:, 3 * (k % 2) + c, lo:CH[c][1] - CH[c][0] if hi is None else hi]

        def tile_wide(k):
            return dense[:, 3 * (k % 2):3 * (k % 2) + 2, 0:384]

        def wide(ap):
            return ap[:, 0:768].rearrange("p (c t) -> p c t", c=2)

        def bank(r, n=512, rows=P):
            return misc[0:rows, r % 2, 0:n]

        def smp3(ap):
            return ap.rearrange("p (b t) -> p b t", t=NT)

        def per_batch(ap):
            return ap.unsqueeze(2).to_broadcast([P, NB, NT])

        def row(ap3, k):
            return ap3[:, ds(k, 1), :].rearrange("p o t -> p (o t)")

        def zrow(k):
            return z[ds(k, 1)].rearrange("o p t -> (o p) t")

        vecs = ((V_MIX, g_mix[0]), (V_FFN, g_ffn[0]), (V_FIN, g_final), (V_HEAD, g_head[0]), (V_POOL, s_pool[0]),
                (V_ADA, b_ada[0]))
        small = 13 * 16

        block = top.enter_context(nc.Block())

        @block.sync
        def _(sp):
            def w_cols(w, col, n=P):
                return w[:, ds(col, n)].rearrange("(k p) n -> p k n", p=P)

            def load(n, src, i=0, per=0, kt=KT):
                wait_free(sp, raw_free, n, i, per)
                sp.dma_start(raw[:, n % 2, :].rearrange("p (k n) -> p k n", k=kt), src).then_inc(raw_in[n % 2], 16)

            def ada_load(a, i=0, per=0):
                wait_free(sp, ada_free, a, i, per)
                sp.dma_start(ada_w[:, a % 2, :, :], w_cols(w_ada[0], i * (256 * per) + 256 * a, 256)
                             ).then_inc(ada_in[a % 2], 16)

            xp = x_prompt[0].rearrange("(j p) d -> p j d", p=P)
            sp.dma_start(xtok[:, 0:8, 0:512], xp[:, :, 0:512]).then_inc(x_in[0], 16)
            for r, v in vecs:
                n = v.shape[0] // P
                sp.dma_start(vrow[r:r + n, :], v.rearrange("(k p) -> k p", p=P)).then_inc(small_in, 16)
            sp.dma_start(xtok[0:SMP, 8, :], x_sample.rearrange("b t d -> (b t) d")).then_inc(x_in[2], 16)
            ada_load(0)
            sp.dma_start(xtok[:, 0:8, 512:1024], xp[:, :, 512:1024]).then_inc(x_in[1], 16)
            for a in range(1, ADA0 // 2):
                ada_load(a)
                if a in (5, 6):
                    load(a - 5, w_cols(w_in[0], GATE_COL if a == 5 else 0))
            for j in range(2):
                ada_load(ADA0 // 2 + j)
                load(2 + j, w_cols(w_in[0], P * (1 + j)))
            for s in range(2):
                sp.wait_ge(tile_free[s], KT // 2)
            sp.dma_start(z[Z_X:Z_X + KT].rearrange("k p t -> p k t"), xT[:, :, :]).then_inc(x_spilled, 16)

            sp.wait_ge(gates_ready, 2)
            sp.dma_start(gate_rows_p, gates[:, 0:SEQ]).then_inc(gates_out, 16)
            sp.dma_start(gate_rows_s, gates[:, SEQ:T]).then_inc(gates_out, 16)
            sp.wait_ge(gates_out, 32)
            for n, h0 in (("ig", 0), ("fg", H)):
                sp.dma_start(tab[n][:, 0:CK], gate_rows_p[h0:h0 + H].rearrange("h (c t) -> (h c) t", t=CK)
                             ).then_inc(gates_in, 16)
                sp.dma_start(tab[n][:, CK:GL], gate_rows_s[h0:h0 + H].rearrange("h (c t) -> (h c) t", t=NT)
                             ).then_inc(gates_in, 16)

            def l1_loads(lo, hi):
                with sp.Fori(lo, hi) as i:
                    for j in range(2):
                        for n in (4 + 2 * j, 5 + 2 * j):
                            load(n, w_cols(w_in[0], i * (4 * P) + P * (n - U_L1)), i, 4)
                        ada_load(ADA0 // 2 + 2 + j, i, 2)

            l1_loads(0, 4)
            sp.wait_ge(tables_ready, 1)
            sp.dma_start(negg_dram, tab["negg"][:, 0:CK]).then_inc(tables_out, 16)
            for j, n in enumerate(("r", "winter", "emt", "wend16", "negg")):
                sp.dma_start(tab_s_dram[j], tab[n][:, CK:GL]).then_inc(tables_out, 16)
            for j, col in enumerate((CK - 1, GL - 1)):
                sp.dma_start(decay_dram[j].rearrange("(r o) -> r o", o=1), tab["winter"][:, col:col + 1]
                             ).then_inc(tables_out, 16)
            for h in range(H):
                sp.dma_start(m_s[0, :, h:h + 1], tab["mt"][h * NB:(h + 1) * NB, GL - 1:GL]).then_inc(outs, 16)
            sp.dma_start(m_p[0], mnext[:, :].rearrange("p (h c) -> p h c", c=NCK)[:, :, NCK - 1]).then_inc(outs, 16)
            sp.wait_ge(tables_out, 8 * 16)
            sp.dma_start(dec[:, :, :].rearrange("p a r -> p (a r)"),
                         decay_dram.rearrange("a r -> (a r)").partition_broadcast(P)).then_inc(tables_in, 16)
            sp.dma_start(negg_s[:, :, :].rearrange("p h t -> p (h t)"),
                         tab_s_dram[4].rearrange("r t -> (r t)").partition_broadcast(SMP)).then_inc(tables_in, 16)
            for q in range(4):
                for h in range(H):
                    sp.dma_start(scol[:, q, h:h + 1],
                                 tab_s_dram[q, h * NB:(h + 1) * NB].rearrange("b (t o) -> (b t) o", o=1)
                                 ).then_inc(tables_in, 16)
            l1_loads(4, 6)
            load(28, w_cols(w_in[0], 27 * P))

            def l2_load(j, i=0, per=0):
                g = j // 2
                col = PW + 3 * D + g * D + (2 * H if g else 0) + P * (j % 2)
                load(U_L2 + j, w_cols(w_in[0], i * 256 + col), i, per)

            def chunk_load(c, ci):
                sp.dma_start(qkv[:, c, :, :], z[Z_Q:Z_O, :, ds(ci * CK, CK)].rearrange("j p t -> p j t")
                             ).then_inc(qkv_in[c], 16)
                src = negg_dram.rearrange("(h c) t -> c h t", h=H)[ds(ci, 1)].rearrange("o h t -> (o h) t")
                sp.dma_start(neggb[:, c, :, :], src.partition_broadcast(P)).then_inc(qkv_in[c], 16)

            for j in range(2):
                l2_load(j)
            sp.wait_ge(x_spilled, 16)
            sp.wait_ge(tables_in, 18 * 16)
            sp.wait_ge(outs, 5 * 16)
            sp.wait_ge(d_out, 2 * PG * 16)
            for s in range(2):
                sp.wait_ge(ada_free[s], NA // 4)
                sp.wait_ge(stage_out[s], 14 * 16)
            for c in range(2):
                chunk_load(c, c)
            for j in range(2, 6):
                l2_load(j)
            with sp.Fori(1, 4) as i:
                for j in range(6):
                    l2_load(j, i, 6)
                    if j % 3 == 1:
                        wait_full(sp, round_full, R_L2 + RPC * (j // 3) + 17, i - 1, 2 * RPC)
                        chunk_load(j // 3, i * 2 + j // 3)

            def bp_src(n):
                return w_bp[0][:, 256 * (n - U_BP):256 * (n - U_BP) + 256].rearrange("(k p) n -> p k n", p=P)

            for n in (U_BP, U_BP + 1):
                load(n, bp_src(n), kt=PG)
            for r in (R_UT - 2, R_UT - 1):
                wait_full(sp, round_free, r)
            for h in range(H):
                sp.dma_start(c_p[0, 0, h].rearrange("(a p) e -> p a e", p=P), cst[:, h, :, 0:HD]).then_inc(outs, 16)
                sp.dma_start(n_p[0, 0, h].rearrange("(a p o) -> p a o", p=P, o=1), cst[:, h, :, HD:E1]).then_inc(outs, 16)
            sp.wait_ge(outs, 13 * 16)
            sp.dma_start(nrow[:, :], state_n[0].rearrange("b h d -> (b h) d")).then_inc(nrow_in, 16)
            sp.dma_start(ulast[:, :, :], z[Z_U:Z_Q, :, SEQ - HIST:T].rearrange("g p t -> p g t")).then_inc(ulast_in, 16)

            def head_load(s, h):
                for g, zr in enumerate((Z_Q, Z_K, Z_V)):
                    sp.dma_start(qkvs[:, s, 2 * g:2 * g + 2, :],
                                 z[2 * h + zr:2 * h + zr + 2, :, SEQ:T].rearrange("j p t -> p j t")
                                 ).then_inc(head_in[s], 16)
                for b in range(NB):
                    sp.dma_start(cs[:, s, b, :, 0:HD], state_c[0, b, h].rearrange("(a p) e -> p a e", p=P)
                                 ).then_inc(head_in[s], 16)

            def head_store(s, h):
                for b in range(NB):
                    for a in range(2):
                        wait_full(sp, round_free, R_SMP + RPH * h + 4 + 2 * b + a)
                    sp.dma_start(c_s[0, b, h].rearrange("(a p) e -> p a e", p=P), cs[:, s, b, :, 0:HD]
                                 ).then_inc(cs_out[s], 16)

            head_load(0, 0)
            head_load(1, 1)
            wait_full(sp, round_free, R_UT + 1)
            sp.dma_start(pool_p[0, 0], urows[0:HIST, :]).then_inc(outs, 16)
            for b in range(NB):
                sp.dma_start(pool_s[0, b, HIST - NT:HIST], urows[HIST + b * NT:HIST + (b + 1) * NT, :]).then_inc(outs, 16)
            sp.dma_start(pool_s[0, :, 0:HIST - NT], state_pool[0, :, NT:HIST]).then_inc(outs, 16)
            for h in range(H):
                head_store(h % 2, h)
                if h + 2 < H:
                    sp.wait_ge(cs_out[h % 2], NB * 16)
                    wait_full(sp, round_free, R_SMP + RPH * h + 20)
                    head_load(h % 2, h + 2)
            wait_full(sp, round_free, R_NOUT)
            sp.dma_start(n_s[0].rearrange("b h d -> (b h) d"), nout[:, :]).then_inc(outs, 16)
            sp.wait_ge(outs, 24 * 16)
            for s in range(2):
                sp.wait_ge(cs_out[s], 2 * NB * 16)
            sp.dma_start(wpool[:, :, :], w_pool[0].rearrange("g c d -> c g d")).then_inc(wpool_in, 16)
            for g in range(PG):
                if g >= 2:
                    wait_full(sp, tile_full, T_YP + g - 2)
                sp.dma_start(dT[:, g % 2, :], z[Z_D + g]).then_inc(d_in[g % 2], 16)
            for s in range(2):
                sp.wait_ge(stage_out[s], 26 * 16)

            def rows_in(k, src, i=0, per=0):
                wait_free(sp, tile_free, k, i, per)
                sp.dma_start(stage[:, k % 2, :], src).then_inc(gin_in[k % 2], 16)

            for j in range(8):
                rows_in(T_BP + j, z[Z_GP + j])
                sp.dma_start(oin[:, j % 2, :], z[Z_O + j]).then_inc(oin_in[j % 2], 16)
                if j % 2:
                    if j < 4:
                        load(U_BP + 2 + j // 2, bp_src(U_BP + 2 + j // 2), kt=PG)
                    else:
                        load(U_BM + j // 2 - 2, w_cols(w_bm[0], P * (j // 2 - 2)))
            for t0, zr, u0, w, w_next in ((T_BM, Z_GM, U_BM, w_bm, w_out), (T_OUT, Z_X, U_OUT, w_out, None)):
                with sp.Fori(0, 3) as i:
                    for j in range(2):
                        rows_in(t0 + j, zrow(i * 2 + (zr + j)), i, 2)
                        load(u0 + 2 + j, w_cols(w[0], i * 256 + P * (2 + j)), i, 2)
                for j in range(6, 8):
                    rows_in(t0 + j, z[zr + j])
                    if w_next is not None:
                        load(u0 + 2 + j, w_cols(w_next[0], P * (j - 6)))

            def up_load(n, f, up, i, i_w, per):
                load(n, w_cols(w_gu[0], i_w * 256 + (P * f + FF * up)), i, per)

            def ffn_loads(i, last=False):
                n = U_FFN + 1
                for f, up in ((0, 1), (1, 0), (1, 1)):
                    up_load(n, f, up, i, i, 6)
                    n += 1
                if not last:
                    up_load(n, 0, 0, i, i + 1, 6)
                    n += 1
                for half in range(2):
                    load(n + half, w_down[0][ds(i * 256, 256), 512 * half:512 * half + 512].rearrange(
                        "(f p) n -> p f n", p=P), i, 6, kt=2)

            up_load(U_FFN, 0, 0, 0, 0, 0)
            with sp.Fori(0, FI - 1) as i:
                ffn_loads(i)
            ffn_loads(FI - 1, last=True)

            for tt in range(TT):
                sp.wait_ge(ytok_act, tt + 1)
                sp.wait_ge(ytok_dve, tt + 1)
                dst = y_prompt[0, tt * P:(tt + 1) * P] if tt < 8 else y_sample.rearrange("b t d -> (b t) d")
                sp.dma_start(dst, ytok[0:P if tt < 8 else SMP, tt % 2, :]).then_inc(y_out[tt % 2], 16)
            sp.wait_ge(y_out[0], 5 * 16)
            sp.wait_ge(y_out[1], 4 * 16)

        @block.gpsimd
        def _(pool):
            step = [0]

            def link(ins):
                step[0] += 1
                ins.then_inc(pool_step, 1)
                pool.wait_ge(pool_step, step[0])

            pool.memset(ones[:, :], 1.0).then_inc(consts_ready, 1)
            pool.memset(epsc[:, :], EPS).then_inc(consts_ready, 1)
            link(pool.memset(ident[:, :], 0.0))
            pool.affine_select(out=ident[:, :], in_=ident[:, :], compare_op=ALU.not_equal, fill=1.0,
                               base=0, pattern=[[-1, P]], channel_multiplier=1).then_inc(consts_ready, 1)

            for k in range(KT):
                pool.wait_ge(xsq_ready, k + 1)
                if k == 0:
                    pool.tensor_copy(xssq[:, :], xsq[:, 0, :]).then_inc(ssq_ready, 1)
                else:
                    pool.wait_ge(ssq_ready, k)
                    pool.tensor_tensor(xssq[:, :], xssq[:, :], xsq[:, k % 2, :], ALU.add).then_inc(ssq_ready, 1)
            wait_full(pool, tile_free, T_SS)
            for k in range(KT):
                pool.tensor_tensor(xn[:, k, :], xT[:, k, :], xssq[:, :], ALU.mult).then_inc(xn_ready, 1)

            pool.wait_ge(h_ready, KT)
            pool.wait_ge(x_spilled, 16)
            pool.memset(zeros[:, :], 0.0).then_inc(consts_ready, 1)
            for g in range(PG):
                for t in range(16):
                    last = pool.memset(invcnt[:, g, t:t + 1], 1.0 / min(t + 1, 2 << g))
            link(last)
            link(pool.memset(ext_p[:, :, 0:HIST], 0.0))
            for s in range(2):
                pool.wait_ge(stage_out[s], 2 * 16)
            for g in range(PG):
                pool.dma_start(ext_p[:, g, HIST:HIST + SEQ], z[Z_U + g, :, 0:SEQ]).then_inc(ext_in, 16)
                pool.dma_start(ext_s[:, g, :, HIST:HIST + NT], smp3(z[Z_U + g, :, SEQ:T])).then_inc(ext_in, 16)
            pool.wait_ge(ext_in, 2 * PG * 16)
            wait_full(pool, round_free, R_COLS + 1)
            for g in range(PG):
                for smp_part in (False, True):
                    n = HIST + (NT if smp_part else SEQ)
                    ext = ext_s[:, g, :, :] if smp_part else ext_p[:, g, :]
                    bufs = [win[:, s, 0:NB * n].rearrange("p (b t) -> p b t", b=NB) if smp_part else win[:, s, :]
                            for s in range(2)]

                    def cut(v, lo, hi):
                        return v[:, :, lo:hi] if smp_part else v[:, lo:hi]

                    src, span, turn_ = ext, 1, 0
                    while span < 2 << g:
                        dst, turn_ = bufs[turn_], 1 - turn_
                        link(pool.tensor_tensor(cut(dst, 2 * span - 1, n), cut(src, 2 * span - 1, n),
                                                cut(src, span - 1, n - span), ALU.add))
                        src, span = dst, 2 * span
                    dst = bufs[turn_]
                    if smp_part:
                        link(pool.tensor_scalar(cut(dst, HIST, n), cut(src, HIST, n), 1.0 / (2 << g), None, ALU.mult))
                    else:
                        pool.tensor_tensor(dst[:, HIST:HIST + 16], src[:, HIST:HIST + 16], invcnt[:, g, :], ALU.mult)
                        link(pool.tensor_scalar(dst[:, HIST + 16:n], src[:, HIST + 16:n], 1.0 / (2 << g), None, ALU.mult))
                    link(pool.tensor_tensor(cut(ext, HIST, n), cut(dst, HIST, n), cut(ext, HIST, n), ALU.subtract))
                pool.dma_start(z[Z_D + g, :, 0:SEQ], ext_p[:, g, HIST:HIST + SEQ]).then_inc(d_out, 16)
                pool.dma_start(smp3(z[Z_D + g, :, SEQ:T]), ext_s[:, g, :, HIST:HIST + NT]).then_inc(d_out, 16)
            pool.wait_ge(d_out, 2 * PG * 16)

            pool.wait_ge(tables_in, 18 * 16)
            pool.wait_ge(outs, 5 * 16)
            for s in range(2):
                pool.wait_ge(ada_free[s], NA // 4)
            link(pool.memset(mask[:, :], 0.0))
            link(pool.affine_select(out=mask[:, :], in_=mask[:, :], compare_op=ALU.is_ge, fill=NEG,
                                    base=0, pattern=[[1, CK]], channel_multiplier=-1))
            pool.memset(vext[:, :, HD:E1], 1.0).then_inc(mls_init, 1)
            pool.memset(cst[:, :, :, :], 0.0).then_inc(mls_init, 1)
            with pool.Fori(0, NCK // 2) as i:
                for c in range(2):
                    ci = i * 2 + c
                    for r in (21, 22):
                        wait_full(pool, round_free, R_L2 + RPC * c + r, i - 1, 2 * RPC)
                    pool.wait_ge(qkv_in[c], i * 32 + 32)
                    pool.tensor_tensor(neggb[:, c, :, :], neggb[:, c, :, :],
                                       mask[:, :].unsqueeze(1).to_broadcast([P, H, CK]), ALU.add).then_inc(chunk_prep, 1)
                    pool.tensor_copy(cur[:, c, 0:4, :], colp[:, :, :].rearrange("p q (h c) -> p q h c", h=H)
                                     [:, :, :, ds(ci, 1)].rearrange("p q h o -> p q (h o)")).then_inc(chunk_prep, 1)
                    pool.tensor_copy(cur[:, c, 4, :], dec[:, 0, :].rearrange("p (h c) -> p h c", h=H)
                                     [:, :, ds(ci, 1)].rearrange("p h o -> p (h o)")).then_inc(chunk_prep, 1)

            pool.wait_ge(outs, 13 * 16)
            pool.memset(vs[:, HD:E1], 1.0).then_inc(vs_init, 1)
            link(pool.memset(maskS[:, :], 0.0))
            m3 = smp3(maskS[:, :])
            link(pool.affine_select(out=m3, in_=m3, compare_op=ALU.is_ge, fill=NEG,
                                    base=0, pattern=[[NT, NB], [1, NT]], channel_multiplier=-1))
            link(pool.affine_select(out=m3, in_=m3, compare_op=ALU.is_ge, fill=NEG,
                                    base=0, pattern=[[-NT, NB], [0, NT]], channel_multiplier=1))
            link(pool.memset(blk[:, :], 1.0))
            link(pool.affine_select(out=blk[:, :], in_=blk[:, :], compare_op=ALU.is_ge, fill=0.0,
                                    base=0, pattern=[[-NT, NB]], channel_multiplier=1))
            link(pool.affine_select(out=blk[:, :], in_=blk[:, :], compare_op=ALU.is_ge, fill=0.0,
                                    base=NT - 1, pattern=[[NT, NB]], channel_multiplier=-1))
            link(pool.memset(qm[:, :, :, :, :], 0.0))
            base = step[0]
            with pool.Fori(0, H // 2) as i:
                for s in range(2):
                    h = i * 2 + s
                    pool.wait_ge(head_in[s], i * (11 * 16) + 11 * 16)
                    pool.tensor_tensor(argS[:, s, :], row(negg_s, h), maskS[:, :], ALU.add).then_inc(head_prep, 1)
                    pool.tensor_copy(curD[:, s, :], dec[:, 1, ds(h * NB, NB)]).then_inc(head_prep, 1)
                    pool.tensor_copy(curC[:, s, :], scol[:, :, ds(h, 1)].rearrange("p q o -> p (q o)")
                                     ).then_inc(pool_step, 1)
                    pool.wait_ge(pool_step, h + (base + 1))
                    pool.sem_inc(pool_passed, 1)
                    pool.tensor_scalar(wmask[:, s, :], blk[:, :], curC[:, s, 3:4], None, ALU.mult
                                       ).then_inc(head_prep, 1)
                    for b in range(NB):
                        pool.tensor_copy(qm[:, s, b, :, NT * b:NT * b + NT], qkvs[:, s, 0:2, NT * b:NT * b + NT]
                                         ).then_inc(head_prep, 1)
                    pool.wait_ge(head_keys, h + 1)
                    pool.wait_ge(head_prep, h * 11 + 11)
                    pool.sem_inc(pool_passed, 1)
                    for b in range(NB):
                        pool.tensor_scalar(kb[:, b, :], ks[:, :], wmask[:, s, b:b + 1], None, ALU.mult
                                           ).then_inc(head_kb, 1)

            wait_full(pool, tile_free, T_N2)
            for k in range(KT):
                if k >= 2:
                    pool.wait_ge(h2f_ready, k - 1)
                pool.tensor_tensor((sil[:, :], a32[:, 0, :])[k % 2], hmT[:, k, :], ssq[:, :], ALU.mult
                                   ).then_inc(x1n_ready, 1)

            for k in range(KT):
                pool.wait_ge(x2sq_ready, k + 1)
                s = (sq, sil)[k % 2][:, :]
                if k == 0:
                    pool.tensor_copy(ssq[:, :], s).then_inc(x2sum_ready, 1)
                else:
                    pool.wait_ge(x2sum_ready, k)
                    pool.tensor_tensor(ssq[:, :], ssq[:, :], s, ALU.add).then_inc(x2sum_ready, 1)

        @block.scalar
        def _(act):
            def copy2(k, dst, func=ACT.Copy, scale=1.0, bias=None):
                kw_ = {} if bias is None else {"bias": bias}
                act.activation(wide(dst), tile_wide(k), func, scale=scale, **kw_)
                return act.activation(dst[:, 768:T], tile(k, 2), func, scale=scale, **kw_)

            def split_hi(n, i=0, per=0):
                wait_full(act, raw_in, n, i, per, inc=16)
                act.activation(w_hi[:, n % 2, :], raw[:, n % 2, :], ACT.Copy).then_inc(hi_ready, 1)

            def modulation(r, m, a=None, i=0, per=0, mdyn=None):
                wait_full(act, round_full, r, i, per)
                if a is not None:
                    act.sem_inc(ada_free[a % 2], 1)
                if mdyn is None:
                    out, b = mod[:, m, :], vec[:, V_ADA + m:V_ADA + m + 1]
                else:
                    out, b = mod[:, ds(mdyn, 1), :].rearrange("p o g -> p (o g)"), vec[:, ds(mdyn + V_ADA, 1)]
                act.activation(out, bank(r, GRP), ACT.Identity, bias=b).then_inc(round_free[r % 2], 1)

            def col_std(r):
                wait_full(act, round_full, r)
                act.activation(rcol[:, 0:8], bank(r, 8), ACT.Sqrt, scale=1.0 / D, bias=epsc[:, 0:1]).then_inc(std_ready, 1)
                act.activation(rcol[0:SMP, 8:9], bank(r, 9, SMP)[:, 8:9], ACT.Sqrt, scale=1.0 / D,
                               bias=epsc[0:SMP, 0:1]).then_inc(std_ready, 1)
                act.wait_ge(std_ready, 2 * (1 + (R_SS, R_N2, R_Y).index(r)))
                act.sem_inc(round_free[r % 2], 1)

            act.dma_start(cc[0:1, :], c_prompt).then_inc(c_in, 16)
            act.dma_start(cc[1:GRP, :], c_sample).then_inc(c_in, 16)
            act.dma_start(hrow[:, :], state_pool[0].rearrange("b t c -> (b t) c")).then_inc(small_in, 16)
            act.dma_start(gbias[0:H, :], b_igate[0].rearrange("(h o) -> h o", o=1)).then_inc(small_in, 16)
            act.dma_start(gbias[H:2 * H, :], b_fgate[0].rearrange("(h o) -> h o", o=1)).then_inc(small_in, 16)
            for h in range(H):
                act.dma_start(mprev[h * NB:(h + 1) * NB, 1:2], state_m[0, :, h:h + 1]).then_inc(small_in, 16)
            act.wait_ge(c_in, 2 * 16)
            act.activation(csig, cc, ACT.Sigmoid).then_inc(csig_ready, 1)

            def squares(k):
                wait_full(act, tile_full, k)
                if k >= 2:
                    act.wait_ge(ssq_ready, k - 1)
                copy2(k, xsq[:, k % 2, :], ACT.Square).then_inc(xsq_ready, 1)

            def h_high(k):
                act.wait_ge(h32_ready, k + 1)
                act.activation(act_hi[:, k, :], h32[:, k % 2, :], ACT.Copy).then_inc(hhi_ready, 1)

            squares(0)
            squares(1)
            act.wait_ge(consts_ready, 3)
            for a in range(ADA0 // 2):
                r0, r1 = ada_rounds(a)
                wait_full(act, round_full, r0)
                act.sem_inc(ada_free[a % 2], 1)
                if a == 0:
                    act.wait_ge(silu_ready, 1)
                act.activation(mod_rows, bank(r0, 256, GRP), ACT.Copy).then_inc(round_free[r0 % 2], 1)
                if a + 2 < KT:
                    squares(a + 2)
                if a == 0:
                    wait_full(act, round_free, R_VEC)
                wait_full(act, round_full, r1)
                for m in (2 * a, 2 * a + 1):
                    ins = act.activation(mod[:, m, :], bank(r1, 2 * GRP)[:, GRP * (m % 2):GRP * (m % 2) + GRP],
                                         ACT.Identity, bias=vec[:, V_ADA + m:V_ADA + m + 1])
                ins.then_inc(round_free[r1 % 2], 1)
                if a == A_NORM - 2:
                    col_std(R_SS)
                if a == A_NORM - 1:
                    wait_full(act, tile_full, T_SS)
                    copy2(T_SS, xssq[:, :]).then_inc(tile_free[T_SS % 2], 1)
                    split_hi(0)
                    split_hi(1)
                if a == A_NORM:
                    h_high(0)
            for k in range(1, KT):
                h_high(k)
            act.wait_ge(small_in, small)
            wait_full(act, tile_full, T_GATE)
            act.wait_ge(x_spilled, 16)
            s = 3 * (T_GATE % 2)
            act.activation(wide(gates[:, :]), dense[0:8, s:s + 2, 0:384], ACT.Identity, bias=gbias[:, 0:1]
                           ).then_inc(gates_ready, 1)
            act.activation(gates[:, 768:T], dense[0:8, s + 2, 0:320], ACT.Identity, bias=gbias[:, 0:1]
                           ).then_inc(gates_ready, 1)
            act.wait_ge(gates_ready, 2)
            act.sem_inc(tile_free[T_GATE % 2], 1)
            split_hi(2)

            def evac(k, part, i=0, per=0):
                if part == 0:
                    wait_full(act, tile_full, k, i, per)
                    slot, m = turn(k - T_L1, i, per)
                    if per or m:
                        act.wait_ge(stage_out[slot], m * 16)
                    act.activation(wide(stage[:, k % 2, :]), tile_wide(k), ACT.Copy)
                else:
                    act.activation(stage[:, k % 2, 768:T], tile(k, 2), ACT.Copy).then_inc(tile_free[k % 2], 1)

            def store(k, dst, i=0, per=0):
                wait_full(act, tile_free, k, i, per)
                act.dma_start(dst, stage[:, k % 2, :]).then_inc(stage_out[k % 2], 16)

            def l1_part(part):
                lo, hi = L1_CUTS[part]
                rb = R_SEG[part]

                def body(j, i, per):
                    k = T_L1 + j
                    evac(k, 0, i, per)
                    evac(k, 1, i, per)
                    split_hi(U_L1 + j + 2, i, per)
                    store(k, zrow(i * 4 + j) if per else z[j], i, per)
                    a = j // 2 if j % 2 else None
                    modulation(rb + j, ADA0 + j, a, i, per, i * 4 + (ADA0 + j) if per else None)

                if lo == 0:
                    act.wait_ge(h_ready, KT)
                    for j in range(4):
                        body(j, 0, 0)
                    return
                with act.Fori(lo // 2, hi // 2) as i:
                    for j in range(4):
                        body(j, i, 4)

            l1_part(0)
            act.wait_ge(gates_in, 4 * 16)
            act.activation(tab["abs"][:, :], tab["fg"][:, :], ACT.Abs).then_inc(act_step, 1)
            act.wait_ge(act_step, 1)
            act.activation(tab["exp"][:, :], tab["abs"][:, :], ACT.Exp, scale=-1.0).then_inc(act_step, 1)
            act.wait_ge(act_step, 2)
            act.activation(tab["ln"][:, :], tab["exp"][:, :], ACT.Ln, bias=1.0).then_inc(lnterm_ready, 1)
            l1_part(1)
            act.wait_ge(g_ready, 1)
            for a, cols in enumerate((slice(0, CK), slice(CK, GL))):
                act.activation(tab["winter"][:, cols], tab["g"][:, cols], ACT.Exp, scale=-1.0, bias=mprev[:, a:a + 1]
                               ).then_inc(gexp_ready, 1)
                act.activation(tab["wend"][:, cols], tab["r"][:, cols], ACT.Exp, bias=ngend[:, a:a + 1]
                               ).then_inc(gexp_ready, 1)
            act.activation(tab["emt"][:, :], tab["mt"][:, :], ACT.Exp, scale=-1.0).then_inc(gexp_ready, 1)
            l1_part(2)
            l1_part(3)

            def l2_step(j, i, part):
                k = T_L2 + j
                if part < 2:
                    evac(k, part, i, 6)
                if part == 2:
                    split_hi(U_L2 + j + 2, i, 6)
                if part == 3:
                    store(k, zrow(i * 2 + (Z_O + KT * (j // 2) + j % 2)), i, 6)

            def chunk_act(c, i, slot):
                ci = i * 2 + c
                rb = R_L2 + RPC * c
                if slot == 0:
                    act.wait_ge(chunk_prep, ci * 3 + 3)
                    for h in range(H):
                        ins = act.activation(wexp[:, c, h, :], neggb[:, c, h, :], ACT.Exp, bias=cur[:, c, 0, h:h + 1])
                    ins.then_inc(weights_exp, 1)
                if slot in (0, 1):
                    r = rb + 1 + slot
                    wait_full(act, round_full, r, i, 2 * RPC)
                    for a in range(2):
                        h = 2 * slot + a
                        ins = act.activation(kw[:, h, :], bank(r)[:, HD * a:HD * a + HD], ACT.Copy,
                                             scale=cur[:, c, 3, h:h + 1])
                    ins.then_inc(round_free[r % 2], 1)
                if 4 <= slot < 20 and slot % 4 == 0:
                    h = slot // 4 - 1
                    r = rb + 5 + 4 * h
                    wait_full(act, round_full, r, i, 2 * RPC)
                    act.activation(hs[:, h, :], bank(r, E1), ACT.Copy, scale=cur[:, c, 1, h:h + 1]
                                   ).then_inc(round_free[r % 2], 1)
                if slot == 20:
                    act.wait_ge(msq_ready, ci + 1)
                    act.activation(sm[:, 4, :], sm[:, 3, :], ACT.Sqrt, scale=1.0 / HD, bias=epsc[:, 0:1]
                                   ).then_inc(hstd_ready, 1)
                if slot == 23:
                    for a in range(2):
                        r = rb + 21 + a
                        wait_full(act, round_full, r, i, 2 * RPC)
                        act.activation(hmT[:, 4 * a:4 * a + 4, ds(ci * CK, CK)],
                                       bank(r).rearrange("p (j t) -> p j t", t=CK), ACT.Copy
                                       ).then_inc(round_free[r % 2], 1)

            with act.Fori(0, 4) as i:
                for j in range(6):
                    for s in range(8):
                        chunk_act(j // 3, i, (j % 3) * 8 + s)
                        if j:
                            l2_step(j - 1, i, s)
                for s in range(4):
                    l2_step(5, i, s)

            with act.Fori(0, H // 2) as i:
                for s in range(2):
                    h = i * 2 + s
                    rb = R_SMP + RPH * s
                    act.wait_ge(head_prep, h * 11 + 11)
                    act.activation(wexpS[:, s, :], argS[:, s, :], ACT.Exp, bias=curC[:, s, 0:1]).then_inc(weights_exp, 1)
                    wait_full(act, round_full, rb + 2, i, 2 * RPH)
                    act.activation(hsS[:, :], bank(rb + 2, E1, SMP), ACT.Copy, scale=curC[:, s, 1:2]
                                   ).then_inc(round_free[(rb + 2) % 2], 1)
                    act.wait_ge(msq_ready, h + (NCK + 1))
                    act.activation(smS[:, 4:5], smS[:, 3:4], ACT.Sqrt, scale=1.0 / HD, bias=epsc[0:SMP, 0:1]
                                   ).then_inc(hstd_ready, 1)
                    wait_full(act, round_full, rb + 20, i, 2 * RPH)
                    act.activation(hmT[:, ds(h * 2, 2), SEQ:T], bank(rb + 20, 128).rearrange("p (j t) -> p j t", t=SMP),
                                   ACT.Copy).then_inc(round_free[(rb + 20) % 2], 1)

            act.wait_ge(outs, 24 * 16)
            for s in range(2):
                act.wait_ge(cs_out[s], 2 * NB * 16)
            for g in range(PG):
                k = T_YP + g
                sc = vec[:, V_POOL + g:V_POOL + g + 1]
                wait_full(act, tile_full, k)
                if g:
                    wait_full(act, tile_free, k - 1)
                copy2(k, sq[:, :], scale=sc)
                copy2(k, yp_hi[:, g, :], scale=sc).then_inc(yphi_ready, 1)

            with act.Fori(0, 2) as i:
                for j in range(4):
                    k = T_BP + j
                    kt = i * 4 + j
                    wait_full(act, oin_in, j, i, 4, 16)
                    act.activation(oin[:, j % 2, :], oin[:, j % 2, :], ACT.Sigmoid).then_inc(osig_ready, 1)
                    wait_full(act, gin_in, j, i, 4, 16)
                    act.activation(stage[:, k % 2, :], stage[:, k % 2, :], ACT.Sigmoid).then_inc(gsig_ready, 1)
                    act.wait_ge(yml32_ready, kt + 1)
                    act.activation(row(act_hi, kt), row(hmT, kt), ACT.Copy).then_inc(ymlhi_ready, 1)
                    if j % 2:
                        wait_full(act, tile_full, k, i, 4)
                        split_hi(U_BP + 2 + j // 2, i, 2)
            with act.Fori(0, 4) as i:
                for j in range(2):
                    k = T_BM + j
                    wait_full(act, gin_in, 8 + j, i, 2, 16)
                    act.activation(stage[:, k % 2, :], stage[:, k % 2, :], ACT.Sigmoid).then_inc(gsig_ready, 1)
                    wait_full(act, tile_full, k, i, 2)
                    split_hi(U_BM + 2 + j, i, 2)
            for k in range(KT):
                act.wait_ge(m32_ready, k + 1)
                act.activation(act_hi[:, k, :], hmT[:, k, :], ACT.Copy).then_inc(mhi_ready, 1)
            with act.Fori(0, 4) as i:
                for j in range(2):
                    wait_full(act, tile_full, T_OUT + j, i, 2)
                    split_hi(U_OUT + 2 + j, i, 2)
            col_std(R_N2)
            wait_full(act, tile_full, T_N2)
            copy2(T_N2, ssq[:, :]).then_inc(tile_free[T_N2 % 2], 1)
            for k in range(KT):
                act.wait_ge(h2f_ready, k + 1)
                act.activation(act_hi[:, k, :], h32[:, k % 2, :], ACT.Copy).then_inc(h2hi_ready, 1)

            def silu(k, f, i, per=12):
                wait_full(act, tile_full, k, i, per)
                act.wait_ge(a32_ready, i * 2 + (f + 1))
                copy2(k, sil[:, :], ACT.Silu).then_inc(sil_ready, 1)

            def ffn_act(i, last=False):
                n, k = U_FFN + 1, T_FFN + 1
                for f in range(2):
                    if f:
                        silu(k + 1, 1, i)
                        split_hi(n + 3, i, 6)
                    wait_full(act, tile_full, k + 2 * f, i, 12)
                    act.wait_ge(a32_ready, i * 2 + (f + 2))
                    act.activation(a_hi[:, f, :], a32[:, f, :], ACT.Copy).then_inc(ahi_ready, 1)
                    split_hi(n + 2 * f + 2, i, 6)
                if last:
                    return
                wait_full(act, tile_full, k + 3, i, 12)
                act.wait_ge(a32_ready, i * 2 + 3)
                copy2(k + 3, sil[:, :], ACT.Silu).then_inc(sil_ready, 1)
                split_hi(n + 5, i, 6)
                for j in (4, 5):
                    wait_full(act, tile_full, last_tile(n + j), i, 12)
                    split_hi(n + j + 2, i, 6)

            silu(T_FFN, 0, 0, 0)
            split_hi(U_FFN + 2)
            with act.Fori(0, FI - 1) as i:
                ffn_act(i)
            ffn_act(FI - 1, last=True)

            for k in range(KT):
                act.wait_ge(x2_ready, KT * (FI - 1) + k + 1)
                if k >= 2:
                    act.wait_ge(x2sum_ready, k - 1)
                act.activation((sq, sil)[k % 2][:, :], hmT[:, k, :], ACT.Square).then_inc(x2sq_ready, 1)
                act.wait_ge(x2sq_ready, k + 1)
                act.activation(hmT[:, k, :], hmT[:, k, :], ACT.Copy, scale=vec[:, V_FIN + k:V_FIN + k + 1]
                               ).then_inc(xg_ready, 1)
            col_std(R_Y)
            act.wait_ge(rcol_ready, 3 * 2)
            for tt in range(TT):
                k, rows = T_Y + tt, P if tt < 8 else SMP
                wait_full(act, tile_full, k)
                if tt >= 2:
                    act.wait_ge(y_out[tt % 2], 16 * (tt // 2))
                act.activation(ytok[0:rows, tt % 2, 0:512], dense[0:rows, 3 * (k % 2), :], ACT.Copy,
                               scale=rcol[0:rows, tt:tt + 1]).then_inc(ytok_act, 1)

        @block.vector
        def _(dve):
            steps = [0, 0, None]

            def now():
                return steps[0] if steps[2] is None else steps[2] + steps[0]

            def link(ins):
                steps[0] += 1
                ins.then_inc(dve_step, 1)
                dve.wait_ge(dve_step, now())

            def enter(i, per):
                steps[1], steps[2] = steps[0], i * per

            def leave(n, per):
                assert steps[0] - steps[1] == per, (steps[0] - steps[1], per)
                steps[0], steps[2] = steps[1] + n * per, None

            def split_lo(n, i=0, per=0):
                dve.wait_ge(hi_ready, i * per + (n + 1))
                dve.tensor_tensor(w_lo[:, n % 2, :], raw[:, n % 2, :], w_hi[:, n % 2, :].bitcast(F32), ALU.subtract
                                  ).then_inc(raw_free[n % 2], 1)

            def norm_rows(k, xrows, amp, sh, done, used):
                o = h32[:, k % 2, :]
                if k >= 2:
                    dve.wait_ge(used, k - 1)
                link(dve.tensor_tensor(smp3(o[:, SEQ:T]), smp3(xrows[:, SEQ:T]), per_batch(amp[:, k, 1:GRP]), ALU.mult))
                dve.tensor_scalar(o[:, 0:SEQ], xrows[:, 0:SEQ], amp[:, k, 0:1], mod[:, sh + k, 0:1], ALU.mult, ALU.add)
                dve.tensor_tensor(smp3(o[:, SEQ:T]), smp3(o[:, SEQ:T]), per_batch(mod[:, sh + k, 1:GRP]), ALU.add
                                  ).then_inc(done, 1)

            def low_rows(k, src, hi_sem, out_sem):
                dve.wait_ge(hi_sem, k + 1)
                dve.tensor_tensor(act_lo[:, k, :], src, act_hi[:, k, :].bitcast(F32), ALU.subtract).then_inc(out_sem, 1)

            dve.sem_inc(a32_ready, 1)
            dve.wait_ge(csig_ready, 1)
            dve.tensor_tensor(cc, cc, csig, ALU.mult).then_inc(silu_ready, 1)

            def recip_cols(use):
                dve.wait_ge(std_ready, 2 * use)
                dve.reciprocal(rcol[:, 0:8], rcol[:, 0:8]).then_inc(rcol_ready, 1)
                dve.reciprocal(rcol[0:SMP, 8:9], rcol[0:SMP, 8:9]).then_inc(rcol_ready, 1)
                dve.wait_ge(rcol_ready, 2 * use)

            def diagonals(dst):
                for tt in range(TT):
                    n = P if tt < 8 else SMP
                    ins = dve.tensor_scalar(dst[:, P * tt:P * tt + n], ident[:, 0:n], rcol[:, tt:tt + 1], None, ALU.mult)
                ins.then_inc(diag_ready, 1)

            def take_x(k):
                wait_full(dve, tile_full, k)
                dve.wait_ge(xsq_ready, k + 1)
                dve.tensor_copy(wide(xT[:, k, :]), tile_wide(k))
                dve.tensor_copy(xT[:, k, 768:T], tile(k, 2)).then_inc(tile_free[k % 2], 1)

            link(dve.memset(rcol[:, :], 0.0))
            take_x(0)
            take_x(1)
            wait_full(dve, round_full, R_CT)
            dve.tensor_copy(cT[:, :, :].rearrange("p k g -> p (k g)"), bank(R_CT, KT * GRP)).then_inc(round_free[R_CT % 2], 1)
            wait_full(dve, round_full, R_VEC)
            dve.tensor_copy(vec[:, :], bank(R_VEC, NV)).then_inc(round_free[R_VEC % 2], 1)
            for k in range(2, KT):
                take_x(k)
            dve.wait_ge(consts_ready, 3)
            recip_cols(1)
            dve.wait_ge(ssq_ready, KT)
            diagonals(xsq[:, 0, :])
            for r in ada_rounds(A_NORM - 1):
                wait_full(dve, round_free, r)
            wait_full(dve, round_free, R_VEC)
            link(dve.scalar_tensor_tensor(out=amp1[:, :, :], in0=mod[:, SC1:SC1 + KT, :], scalar=1.0,
                                          in1=vec[:, V_MIX:V_MIX + KT].unsqueeze(2).to_broadcast([P, KT, GRP]),
                                          op0=ALU.add, op1=ALU.mult))
            split_lo(0)
            split_lo(1)
            for k in range(KT):
                dve.wait_ge(xn_ready, k + 1)
                norm_rows(k, xn[:, k, :], amp1, SH1, h32_ready, h_ready)
                if k:
                    low_rows(k - 1, h32[:, (k - 1) % 2, :], hhi_ready, h_ready)
            low_rows(KT - 1, h32[:, (KT - 1) % 2, :], hhi_ready, h_ready)
            split_lo(2)

            def l1_part(part):
                with dve.Fori(*L1_CUTS[part]) as i:
                    for j in range(2):
                        split_lo(U_L1 + j + 2, i, 2)

            l1_part(0)
            parts = (slice(0, CK), slice(CK, GL))
            dve.wait_ge(lnterm_ready, 1)
            link(dve.scalar_tensor_tensor(out=tab["lf"][:, :], in0=tab["fg"][:, :], scalar=0.0, in1=tab["ln"][:, :],
                                          op0=ALU.min, op1=ALU.subtract))
            for cols in parts:
                link(dve.tensor_tensor_scan(tab["b"][:, cols], ones[0:HC, 0:cols.stop - cols.start], tab["lf"][:, cols],
                                            0.0, ALU.mult, ALU.add))
            link(dve.tensor_tensor(tab["r"][:, :], tab["ig"][:, :], tab["b"][:, :], ALU.subtract))
            dve.wait_ge(consts_ready, 4)
            for cols in parts:
                dve.tensor_tensor_scan(tab["cm"][:, cols], tab["r"][:, cols], zeros[:, cols], -3e38, ALU.max, ALU.add
                                       ).then_inc(cummax_ready, 1)
            l1_part(1)
            wait_full(dve, round_full, R_GATES)
            dve.tensor_copy(rows2[:, :, :].rearrange("p a r -> p (a r)"), bank(R_GATES, 2 * HC, 1)
                            ).then_inc(round_free[R_GATES % 2], 1)
            wait_full(dve, round_free, R_GATES)
            link(dve.memset(mprow[:, :], NEG))
            for h in range(H):
                c = slice(h * NCK, (h + 1) * NCK)
                link(dve.tensor_tensor_scan(mnext[:, c], rows2[:, 1, c], rows2[:, 0, c], NEG, ALU.max, ALU.add))
            dve.tensor_copy(mprow[:, :].rearrange("p (h c) -> p h c", h=H)[:, :, 1:NCK],
                            mnext[:, :].rearrange("p (h c) -> p h c", h=H)[:, :, 0:NCK - 1]).then_inc(mprow_ready, 1)
            wait_full(dve, round_full, R_GATES + 1)
            dve.tensor_copy(mprev[:, 0:1], bank(R_GATES + 1, 1, HC)).then_inc(round_free[(R_GATES + 1) % 2], 1)
            wait_full(dve, round_free, R_GATES + 1)
            dve.wait_ge(small_in, small)
            dve.wait_ge(cummax_ready, 2)
            for a, cols in enumerate(parts):
                link(dve.tensor_scalar(tab["g"][:, cols], tab["cm"][:, cols], mprev[:, a:a + 1], None, ALU.max))
            link(dve.tensor_scalar(tab["negg"][:, :], tab["g"][:, :], -1.0, None, ALU.mult))
            for a, cols in enumerate(parts):
                link(dve.tensor_copy(ngend[:, a:a + 1], tab["negg"][:, cols.stop - 1:cols.stop]))
            dve.tensor_tensor(tab["mt"][:, :], tab["b"][:, :], tab["g"][:, :], ALU.add).then_inc(g_ready, 1)
            dve.wait_ge(gexp_ready, 5)
            dve.tensor_scalar(tab["wend16"][:, :], tab["wend"][:, :], HD ** -0.5, None, ALU.mult).then_inc(tables_ready, 1)
            l1_part(2)
            wait_full(dve, round_full, R_COLS)
            dve.tensor_copy(colp[:, :, :].rearrange("p q r -> p (q r)"), bank(R_COLS, 4 * HC)
                            ).then_inc(round_free[R_COLS % 2], 1)
            wait_full(dve, round_full, R_COLS + 1)
            dve.tensor_copy(ext_s[:, :, :, 0:HIST], bank(R_COLS + 1, PG * NB * HIST).rearrange(
                "p (g b t) -> p g b t", g=PG, b=NB)).then_inc(round_free[(R_COLS + 1) % 2], 1)
            l1_part(3)

            def chunk_dve(c, i, slot):
                ci = i * 2 + c
                rb = R_L2 + RPC * c
                per = 2 * RPC
                if slot == 0:
                    dve.wait_ge(weights_exp, ci + 1)
                    wait_full(dve, round_full, rb, i, per)
                    dve.scalar_tensor_tensor(out=pT[:, :, :].rearrange("p h t -> p (h t)"), in0=bank(rb),
                                             scalar=HD ** -0.5,
                                             in1=wexp[:, c, :, :].rearrange("p h t -> p (h t)"),
                                             op0=ALU.mult, op1=ALU.mult).then_inc(round_free[rb % 2], 1)
                if slot in (2, 3):
                    r = rb + 1 + slot
                    wait_full(dve, round_full, r, i, per)
                    dve.tensor_copy(vext[:, 2 * slot - 4:2 * slot - 2, 0:HD], bank(r).rearrange("p (h e) -> p h e", e=HD)
                                    ).then_inc(round_free[r % 2], 1)
                if 4 <= slot < 20:
                    h, q = slot // 4 - 1, slot % 4
                    r = rb + 5 + 4 * h + q
                    if q == 1:
                        wait_full(dve, round_free, r - 1, i, per)
                        wait_full(dve, round_full, r, i, per)
                        dve.tensor_tensor(hn[:, h, :], bank(r, E1), hs[:, h, :], ALU.add).then_inc(round_free[r % 2], 1)
                        wait_full(dve, round_free, r, i, per)
                        link(dve.tensor_tensor_reduce(out=hf[:, h, :], in0=hn[:, h, 0:HD], in1=hn[:, h, 0:HD], scale=1.0,
                                                      scalar=0.0, op0=ALU.mult, op1=ALU.add, accum_out=sm[:, 0, h:h + 1]))
                    if q >= 2:
                        wait_full(dve, round_full, r, i, per)
                        a = q - 2
                        dve.scalar_tensor_tensor(out=cst[:, h, a, :], in0=cst[:, h, a, :], scalar=cur[:, c, 4, h:h + 1],
                                                 in1=bank(r, E1), op0=ALU.mult, op1=ALU.add
                                                 ).then_inc(round_free[r % 2], 1)
                if slot == 20:
                    den = hn[:, :, HD]
                    link(dve.scalar_tensor_tensor(out=sm[:, 1, :], in0=den, scalar=-1.0, in1=den, op0=ALU.mult, op1=ALU.max))
                    link(dve.tensor_tensor(sm[:, 1, :], sm[:, 1, :], cur[:, c, 2, :], ALU.max))
                    link(dve.reciprocal(sm[:, 2, :], sm[:, 1, :]))
                    link(dve.tensor_tensor(sm[:, 3, :], sm[:, 0, :], sm[:, 2, :], ALU.mult))
                    dve.tensor_tensor(sm[:, 3, :], sm[:, 3, :], sm[:, 2, :], ALU.mult).then_inc(msq_ready, 1)
                    dve.wait_ge(hstd_ready, ci + 1)
                    link(dve.reciprocal(sm[:, 5, :], sm[:, 4, :]))
                    link(dve.tensor_tensor(sm[:, 6, :], sm[:, 5, :], sm[:, 2, :], ALU.mult))
                    for h in range(H):
                        ins = dve.tensor_scalar(hf[:, h, :], hn[:, h, 0:HD], sm[:, 6, h:h + 1], None, ALU.mult)
                    ins.then_inc(hf_ready, 1)

            chunk_steps = 2 * (H + 6)
            with dve.Fori(0, NCK // 2) as i:
                enter(i, chunk_steps)
                for j in range(6):
                    for s in range(8):
                        chunk_dve(j // 3, i, (j % 3) * 8 + s)
                        if j and s == 3:
                            split_lo(U_L2 + j + 1, i, 6)
                split_lo(U_L2 + 7, i, 6)
                leave(NCK // 2, chunk_steps)

            wait_full(dve, round_full, R_UT)
            dve.tensor_copy(nT[:, :, :].rearrange("p a r -> p (a r)"), bank(R_UT, 2 * HC)).then_inc(round_free[R_UT % 2], 1)
            wait_full(dve, round_full, R_UT + 1)
            dve.tensor_copy(urows[:, :], bank(R_UT + 1, PW, HIST + SMP)).then_inc(round_free[(R_UT + 1) % 2], 1)
            wait_full(dve, round_free, R_UT)
            with dve.Fori(0, H // 2) as i:
                enter(i, 14)
                for s in range(2):
                    h = i * 2 + s
                    rb, per = R_SMP + RPH * s, 2 * RPH

                    def full(r):
                        wait_full(dve, round_full, rb + r, i, per)

                    def by_head(ap):
                        return ap[:, :, :].rearrange("p a (b h) -> p b a h", h=H)[:, :, :, ds(h, 1)].rearrange(
                            "p b a o -> p b (a o)")

                    dve.wait_ge(head_in[s], i * (11 * 16) + 11 * 16)
                    dve.tensor_copy(cs[:, s, :, :, HD], by_head(nT)).then_inc(n_ready, 1)
                    full(0)
                    dve.wait_ge(weights_exp, h + (NCK + 1))
                    dve.scalar_tensor_tensor(out=pTS[:, :], in0=bank(rb, SMP, SMP), scalar=HD ** -0.5,
                                             in1=wexpS[:, s, :], op0=ALU.mult, op1=ALU.mult
                                             ).then_inc(round_free[rb % 2], 1)
                    full(1)
                    dve.tensor_copy(ks[:, :], bank(rb + 1, HD, SMP)).then_inc(head_keys, 1)
                    dve.tensor_copy(vs[:, 0:HD], bank(rb + 1, 512, SMP)[:, HD:512]).then_inc(round_free[(rb + 1) % 2], 1)
                    wait_full(dve, round_free, rb + 2, i, per)
                    full(3)
                    dve.tensor_tensor(hnS[:, :], bank(rb + 3, E1, SMP), hsS[:, :], ALU.add
                                      ).then_inc(round_free[(rb + 3) % 2], 1)
                    wait_full(dve, round_free, rb + 3, i, per)
                    link(dve.tensor_tensor_reduce(out=hfS[:, :], in0=hnS[:, 0:HD], in1=hnS[:, 0:HD], scale=1.0,
                                                  scalar=0.0, op0=ALU.mult, op1=ALU.add, accum_out=smS[:, 0:1]))
                    den = hnS[:, HD:E1]
                    link(dve.scalar_tensor_tensor(out=smS[:, 1:2], in0=den, scalar=-1.0, in1=den, op0=ALU.mult, op1=ALU.max))
                    link(dve.tensor_tensor(smS[:, 1:2], smS[:, 1:2], curC[:, s, 2:3], ALU.max))
                    link(dve.reciprocal(smS[:, 2:3], smS[:, 1:2]))
                    link(dve.tensor_tensor(smS[:, 3:4], smS[:, 0:1], smS[:, 2:3], ALU.mult))
                    dve.tensor_tensor(smS[:, 3:4], smS[:, 3:4], smS[:, 2:3], ALU.mult).then_inc(msq_ready, 1)
                    for b in range(NB):
                        for a in range(2):
                            r = 4 + 2 * b + a
                            full(r)
                            dve.scalar_tensor_tensor(out=cs[:, s, b, a, :], in0=cs[:, s, b, a, :],
                                                     scalar=curD[:, s, b:b + 1], in1=bank(rb + r, E1),
                                                     op0=ALU.mult, op1=ALU.add).then_inc(round_free[(rb + r) % 2], 1)
                        if b == 1:
                            dve.wait_ge(hstd_ready, h + (NCK + 1))
                            link(dve.reciprocal(smS[:, 5:6], smS[:, 4:5]))
                            link(dve.tensor_tensor(smS[:, 6:7], smS[:, 5:6], smS[:, 2:3], ALU.mult))
                            dve.tensor_scalar(hfS[:, :], hnS[:, 0:HD], smS[:, 6:7], None, ALU.mult).then_inc(hf_ready, 1)
                    for r in (18, 19):
                        wait_full(dve, round_free, rb + r, i, per)
                    dve.tensor_copy(by_head(nO), cs[:, s, :, :, HD]).then_inc(nO_ready, 1)
                leave(H // 2, 14)
            wait_full(dve, round_full, R_NOUT)
            dve.tensor_copy(nout[:, :], bank(R_NOUT, HD, HC)).then_inc(round_free[R_NOUT % 2], 1)

            for g in range(PG):
                k = T_YP + g
                dve.wait_ge(yphi_ready, g + 1)
                dve.tensor_tensor(yp_lo[:, g, :], sq[:, :], yp_hi[:, g, :].bitcast(F32), ALU.subtract
                                  ).then_inc(tile_free[k % 2], 1)
            def gated(k, dst, i, per):
                sg = stage[:, k % 2, :]
                wait_full(dve, tile_full, k, i, per)
                dve.tensor_tensor(wide(dst), tile_wide(k), wide(sg), ALU.mult)
                dve.tensor_tensor(dst[:, 768:T], tile(k, 2), sg[:, 768:T], ALU.mult).then_inc(tile_free[k % 2], 1)

            with dve.Fori(0, 2) as i:
                for j in range(4):
                    kt = i * 4 + j
                    y = row(hmT, kt)
                    dve.wait_ge(osig_ready, kt + 1)
                    dve.scalar_tensor_tensor(out=y, in0=y, scalar=vec[:, ds(kt + V_HEAD, 1)], in1=oin[:, j % 2, :],
                                             op0=ALU.mult, op1=ALU.mult).then_inc(yml32_ready, 1)
                    dve.wait_ge(ymlhi_ready, kt + 1)
                    dve.tensor_tensor(row(act_lo, kt), y, row(act_hi, kt).bitcast(F32), ALU.subtract
                                      ).then_inc(yml_ready, 1)
                    dve.wait_ge(gsig_ready, kt + 1)
                    dve.wait_ge(yml_ready, kt + 1)
                    gated(T_BP + j, y, i, 4)
                    if j % 2:
                        split_lo(U_BP + 2 + j // 2, i, 2)
            with dve.Fori(0, 4) as i:
                for j in range(2):
                    k = T_BM + j
                    kt = i * 2 + j
                    m = row(hmT, kt)
                    dve.wait_ge(gsig_ready, kt + (KT + 1))
                    wait_full(dve, raw_free, U_BM + 1 + j, i, 2)
                    gated(k, sq[:, :], i, 2)
                    wait_full(dve, tile_free, k, i, 2)
                    dve.tensor_tensor(m, m, sq[:, :], ALU.add).then_inc(m32_ready, 1)
                    split_lo(U_BM + 2 + j, i, 2)
            for k in range(KT):
                low_rows(k, hmT[:, k, :], mhi_ready, m_ready)

            link(dve.memset(ssq[:, :], 0.0))
            with dve.Fori(0, 4) as i:
                enter(i, 6)
                for j in range(2):
                    k = T_OUT + j
                    kt = i * 2 + j
                    x1, xin = row(hmT, kt), stage[:, k % 2, :]
                    gt = mod[:, ds(kt + GT1, 1), :].rearrange("p o g -> p (o g)")
                    wait_full(dve, tile_full, k, i, 2)
                    wait_full(dve, gin_in, 16 + j, i, 2, 16)
                    link(dve.tensor_tensor(smp3(gsm[:, 0, :]), smp3(tile(k, 2, 256, 320)), per_batch(gt[:, 1:GRP]), ALU.mult))
                    dve.scalar_tensor_tensor(out=wide(x1), in0=tile_wide(k), scalar=gt[:, 0:1], in1=wide(xin),
                                             op0=ALU.mult, op1=ALU.add)
                    dve.scalar_tensor_tensor(out=x1[:, 768:SEQ], in0=tile(k, 2, 0, 256), scalar=gt[:, 0:1],
                                             in1=xin[:, 768:SEQ], op0=ALU.mult, op1=ALU.add)
                    dve.tensor_tensor(x1[:, SEQ:T], gsm[:, 0, :], xin[:, SEQ:T], ALU.add).then_inc(tile_free[k % 2], 1)
                    wait_full(dve, tile_free, k, i, 2)
                    link(dve.tensor_tensor(sq[:, :], x1, x1, ALU.mult))
                    link(dve.tensor_tensor(ssq[:, :], ssq[:, :], sq[:, :], ALU.add))
                    split_lo(U_OUT + 2 + j, i, 2)
                leave(4, 6)
            dve.sem_inc(xsum_ready, 1)
            link(dve.scalar_tensor_tensor(out=amp2[:, :, :], in0=mod[:, SC2:SC2 + KT, :], scalar=1.0,
                                          in1=vec[:, V_FFN:V_FFN + KT].unsqueeze(2).to_broadcast([P, KT, GRP]),
                                          op0=ALU.add, op1=ALU.mult))
            recip_cols(2)
            diagonals(sq)
            for k in range(KT):
                s = (sil, a32[:, 0, :])[k % 2]
                s = s[:, :]
                dve.wait_ge(x1n_ready, k + 1)
                norm_rows(k, s, amp2, SH2, h2f_ready, h2_ready)
                if k:
                    low_rows(k - 1, h32[:, (k - 1) % 2, :], h2hi_ready, h2_ready)
            low_rows(KT - 1, h32[:, (KT - 1) % 2, :], h2hi_ready, h2_ready)

            dve.wait_ge(h2_ready, KT)

            def silu_taken(k, m):
                dve.wait_ge(sil_ready, m)
                dve.sem_inc(tile_free[k % 2], 1)

            def ffn_dve(i, last=False):
                n, k = U_FFN + 1, T_FFN + 1
                for f in range(2):
                    if f:
                        silu_taken(k + 1, i * 2 + 2)
                        split_lo(n + 3, i, 6)
                    t = k + 2 * f
                    wait_full(dve, tile_full, t, i, 12)
                    dve.tensor_tensor(wide(a32[:, f, :]), tile_wide(t), wide(sil[:, :]), ALU.mult)
                    dve.tensor_tensor(a32[:, f, 768:T], tile(t, 2), sil[:, 768:T], ALU.mult).then_inc(a32_ready, 1)
                    dve.wait_ge(ahi_ready, i * 2 + (f + 1))
                    dve.tensor_tensor(a_lo[:, f, :], a32[:, f, :], a_hi[:, f, :].bitcast(F32), ALU.subtract
                                      ).then_inc(tile_free[t % 2], 1)
                    split_lo(n + 2 * f + 2, i, 6)
                t0 = k + 3
                if not last:
                    silu_taken(k + 3, i * 2 + 3)
                    split_lo(n + 5, i, 6)
                    t0 = k + 4
                for o in range(KT):
                    t = t0 + o
                    x1 = hmT[:, o, :]
                    gt = mod[:, GT2 + o, :]
                    wait_full(dve, tile_full, t, i, 12)
                    dve.scalar_tensor_tensor(out=wide(x1), in0=tile_wide(t), scalar=gt[:, 0:1], in1=wide(x1),
                                             op0=ALU.mult, op1=ALU.add)
                    dve.scalar_tensor_tensor(out=x1[:, 768:SEQ], in0=tile(t, 2, 0, 256), scalar=gt[:, 0:1],
                                             in1=x1[:, 768:SEQ], op0=ALU.mult, op1=ALU.add)
                    g = gsm[:, o % 2, :]
                    dve.tensor_tensor(smp3(g), smp3(tile(t, 2, 256, 320)), per_batch(gt[:, 1:GRP]), ALU.mult
                                      ).then_inc(tile_free[t % 2], 1)
                    wait_full(dve, tile_free, t, i, 12)
                    dve.tensor_tensor(x1[:, SEQ:T], g, x1[:, SEQ:T], ALU.add).then_inc(x2_ready, 1)
                    if o % 4 == 3 and not last:
                        split_lo(n + 6 + o // 4, i, 6)

            silu_taken(T_FFN, 1)
            split_lo(U_FFN + 2)
            with dve.Fori(0, FI - 1) as i:
                ffn_dve(i)
            ffn_dve(FI - 1, last=True)

            recip_cols(3)
            for tt in range(TT):
                k, rows = T_Y + tt, P if tt < 8 else SMP
                wait_full(dve, tile_full, k)
                if tt >= 2:
                    dve.wait_ge(y_out[tt % 2], 16 * (tt // 2))
                dve.tensor_scalar(ytok[0:rows, tt % 2, 512:1024], dense[0:rows, 3 * (k % 2) + 1, :],
                                  rcol[0:rows, tt:tt + 1], None, ALU.mult).then_inc(ytok_dve, 1)

        @block.tensor
        def _(pe):
            def products(k, n, off, kk, last, x_hi, x_lo):
                hi, lo = w_hi[:, n % 2, off:off + P], w_lo[:, n % 2, off:off + P]
                for w, x in ((hi, x_hi), (hi, x_lo), (lo, x_hi)):
                    for c, (t0, t1) in enumerate(CH):
                        ins = pe.matmul(tile(k, c), w, x[:, kk, t0:t1], start=(kk == 0 and x is x_hi and w is hi),
                                        stop=(last and w is lo))
                if last:
                    ins.then_inc(tile_full[k % 2], 1)

            def halves(n, i=0, per=0):
                wait_full(pe, raw_free, n, i, per)

            def free_tile(k, i=0, per=0):
                wait_free(pe, tile_free, k, i, per)

            def take(r, i=0, per=0):
                wait_free(pe, round_free, r, i, per)

            def give(ins, r):
                ins.then_inc(round_full[r % 2], 1)

            def unit(n, k, i=0, per=0, between=None, tper=None):
                halves(n, i, per)
                free_tile(k, i, per if tper is None else tper)
                for kk in range(KT):
                    products(k, n, P * kk, kk, kk == KT - 1, act_hi, act_lo)
                    if between is not None:
                        between(kk)

            def two_units(n, k, ready):
                for j in range(2):
                    halves(n + j)
                    free_tile(k + j)
                for kk in range(KT):
                    pe.wait_ge(ready, kk + 1)
                    for j in range(2):
                        products(k + j, n + j, P * kk, kk, kk == KT - 1, act_hi, act_lo)

            def turn_x(k):
                if k % 4 == 0:
                    pe.wait_ge(x_in[k // 4], 16)
                free_tile(k)
                for j in range(TT):
                    rows = P if j < 8 else SMP
                    c = j // 3
                    ins = pe.transpose(tile(k, c, P * (j - 3 * c), P * (j - 3 * c) + rows),
                                       xtok[0:rows, j, P * k:P * k + P], ident[0:rows, 0:rows])
                ins.then_inc(tile_full[k % 2], 1)

            def sum_partitions(k, src):
                free_tile(k)
                for c, (t0, t1) in enumerate(CH):
                    ins = pe.matmul(tile(k, c), ones[:, :], src[:, t0:t1], start=True, stop=True)
                ins.then_inc(tile_full[k % 2], 1)

            def col_sums(r, src):
                take(r)
                for tt in range(TT):
                    rows = P if tt < 8 else SMP
                    ins = pe.matmul(misc[0:rows, r % 2, tt:tt + 1], src[:, P * tt:P * tt + rows], ones[:, 0:1],
                                    start=True, stop=True)
                give(ins, r)

            pe.wait_ge(consts_ready, 3)
            pe.wait_ge(x_in[2], 16)
            turn_x(0)
            turn_x(1)
            pe.wait_ge(silu_ready, 1)
            for k in range(KT):
                ins = pe.transpose(misc[:, R_CT % 2, GRP * k:GRP * k + GRP], stage[0:GRP, 0, P * k:P * k + P],
                                   ident[0:GRP, 0:GRP])
            give(ins, R_CT)
            pe.wait_ge(small_in, small)
            give(pe.transpose(bank(R_VEC, NV), vrow[:, :], ident[0:NV, 0:NV]), R_VEC)
            for a in range(ADA0 // 2):
                r0, r1 = ada_rounds(a)
                wait_full(pe, ada_in, a, inc=16)
                take(r0)
                for kk in range(KT):
                    ins = pe.matmul(bank(r0, 256, GRP), cT[:, kk, :], ada_w[:, a % 2, kk, :],
                                    start=(kk == 0), stop=(kk == KT - 1))
                give(ins, r0)
                if a + 2 < KT:
                    turn_x(a + 2)
                take(r1)
                wait_full(pe, round_free, r0)
                for col in range(2):
                    ins = pe.transpose(misc[:, r1 % 2, GRP * col:GRP * col + GRP], mod_rows[:, P * col:P * col + P],
                                       ident[0:GRP, 0:GRP])
                give(ins, r1)
                if a == A_NORM - 2:
                    pe.wait_ge(ssq_ready, KT)
                    col_sums(R_SS, xssq)
                if a == A_NORM - 1:
                    pe.wait_ge(diag_ready, 1)
                    sum_partitions(T_SS, xsq[:, 0, :])

            def ada(r, a, col, i=0, per=0, aper=0):
                if col == 0:
                    wait_full(pe, ada_in, a, i, aper, 16)
                take(r, i, per)
                for kk in range(KT):
                    ins = pe.matmul(bank(r, GRP), ada_w[:, a % 2, kk, P * col:P * col + P], cT[:, kk, :],
                                    start=(kk == 0), stop=(kk == KT - 1))
                give(ins, r)

            two_units(0, T_GATE, h_ready)

            def l1_part(part):
                lo, hi = L1_CUTS[part]
                rb = R_SEG[part]

                def body(i, per):
                    for jt in range(4):
                        if jt or per:
                            unit(U_L1 + jt, T_L1 + jt, i, per)
                        ada(rb + jt, ADA0 // 2 + jt // 2, jt % 2, i, per, per // 2)

                if lo == 0:
                    body(0, 0)
                    return
                with pe.Fori(lo // 2, hi // 2) as i:
                    body(i, 4)

            l1_part(0)
            l1_part(1)
            pe.wait_ge(cummax_ready, 2)
            take(R_GATES)
            for a, n in enumerate(("b", "cm")):
                ins = pe.matmul(misc[0:1, R_GATES % 2, HC * a:HC * a + HC], tab[n][:, CK - 1:CK], ident[0:HC, 0:HC],
                                start=True, stop=True)
            give(ins, R_GATES)
            pe.wait_ge(mprow_ready, 1)
            take(R_GATES + 1)
            give(pe.matmul(bank(R_GATES + 1, 1, HC), mprow[0:1, :], ones[0:1, 0:1], start=True, stop=True), R_GATES + 1)
            l1_part(2)
            pe.wait_ge(tables_ready, 1)
            take(R_COLS)
            for q, n in enumerate(("r", "winter", "emt", "wend16")):
                ins = pe.transpose(misc[:, R_COLS % 2, HC * q:HC * q + HC], tab[n][:, 0:CK], ident[0:HC, 0:HC])
            give(ins, R_COLS)
            take(R_COLS + 1)
            rows = NB * HIST
            for g in range(PG):
                ins = pe.transpose(misc[:, (R_COLS + 1) % 2, rows * g:rows * g + rows], hrow[:, P * g:P * g + P],
                                   ident[0:rows, 0:rows])
            give(ins, R_COLS + 1)
            l1_part(3)

            def chunk_pe(c, i, slot):
                rb, per = R_L2 + RPC * c, 2 * RPC
                q, k, v = (qkv[:, c, 8 * g:8 * g + 8, :] for g in range(3))

                def turned(src, r):
                    take(r, i, per)
                    for a in range(4):
                        ins = pe.transpose(bank(r)[:, P * a:P * a + P], src[:, a, :], ident[:, :])
                    give(ins, r)

                if slot == 0:
                    pe.wait_ge(qkv_in[c], i * 32 + 32)
                    take(rb, i, per)
                    for h in range(H):
                        for a in range(2):
                            ins = pe.matmul(bank(rb)[:, CK * h:CK * h + CK], k[:, 2 * h + a, :], q[:, 2 * h + a, :],
                                            start=(a == 0), stop=(a == 1))
                    give(ins, rb)
                    turned(k[:, 0:4, :], rb + 1)
                if slot == 1:
                    turned(k[:, 4:8, :], rb + 2)
                if slot in (2, 3):
                    turned(v[:, 4 * slot - 8:4 * slot - 4, :], rb + 1 + slot)
                if 4 <= slot < 20:
                    h, p = slot // 4 - 1, slot % 4
                    r = rb + 5 + 4 * h + p
                    take(r, i, per)
                    if p == 0:
                        if h == 0:
                            pe.wait_ge(mls_init, 2)
                        for a in range(2):
                            ins = pe.matmul(bank(r, E1), q[:, 2 * h + a, :], cst[:, h, a, :], start=(a == 0), stop=(a == 1))
                    elif p == 1:
                        ins = pe.matmul(bank(r, E1), pT[:, h, :], vext[:, h, :], start=True, stop=True)
                    else:
                        ins = pe.matmul(bank(r, E1), kw[:, h, P * (p - 2):P * (p - 1)], vext[:, h, :], start=True, stop=True)
                    give(ins, r)
                if slot == 23:
                    pe.wait_ge(hf_ready, i * 2 + (c + 1))
                    for a in range(2):
                        turned(hf[:, 2 * a:2 * a + 2, :].rearrange("p h (a t) -> p (h a) t", a=2), rb + 21 + a)

            with pe.Fori(0, NCK // 2) as i:
                for j in range(6):
                    def between(kk, j=j):
                        chunk_pe(j // 3, i, (j % 3) * 8 + kk)
                    unit(U_L2 + j, T_L2 + j, i, 6, between)

            pe.wait_ge(nrow_in, 16)
            take(R_UT)
            for a in range(2):
                ins = pe.transpose(misc[:, R_UT % 2, HC * a:HC * a + HC], nrow[:, P * a:P * a + P], ident[0:HC, 0:HC])
            give(ins, R_UT)
            pe.wait_ge(ulast_in, 16)
            take(R_UT + 1)
            for g in range(PG):
                ins = pe.transpose(misc[0:HIST + SMP, (R_UT + 1) % 2, P * g:P * g + P], ulast[:, g, :], ident[:, :])
            give(ins, R_UT + 1)
            pe.wait_ge(vs_init, 1)
            with pe.Fori(0, H // 2) as i:
                for s in range(2):
                    rb, per = R_SMP + RPH * s, 2 * RPH
                    h = i * 2 + s

                    def take_s(r):
                        take(r, i, per)
                        pe.sem_inc(pe_passed, 1)

                    qs, kks, vvs = (qkvs[:, s, 2 * g:2 * g + 2, :] for g in range(3))
                    pe.wait_ge(head_in[s], i * (11 * 16) + 11 * 16)
                    take_s(rb)
                    for a in range(2):
                        ins = pe.matmul(bank(rb, SMP, SMP), kks[:, a, :], qs[:, a, :], start=(a == 0), stop=(a == 1))
                    give(ins, rb)
                    take_s(rb + 1)
                    for g, src in enumerate((kks, vvs)):
                        for a in range(2):
                            c0 = HD * g + P * a
                            ins = pe.transpose(misc[0:SMP, (rb + 1) % 2, c0:c0 + P], src[:, a, :], ident[:, :])
                    give(ins, rb + 1)
                    pe.wait_ge(n_ready, h + 1)
                    pe.wait_ge(head_prep, h * 11 + 11)
                    take_s(rb + 2)
                    for b in range(NB):
                        for a in range(2):
                            ins = pe.matmul(bank(rb + 2, E1, SMP), qm[:, s, b, a, :], cs[:, s, b, a, :],
                                            start=(b == 0 and a == 0), stop=(b == NB - 1 and a == 1))
                    give(ins, rb + 2)
                    take_s(rb + 3)
                    give(pe.matmul(bank(rb + 3, E1, SMP), pTS[:, :], vs[:, :], start=True, stop=True), rb + 3)
                    for b in range(NB):
                        for a in range(2):
                            r = rb + 4 + 2 * b + a
                            if a == 0:
                                pe.wait_ge(head_kb, h * NB + (b + 1))
                            take_s(r)
                            give(pe.matmul(bank(r, E1), kb[:, b, P * a:P * a + P], vs[:, :], start=True, stop=True), r)
                    pe.wait_ge(hf_ready, h + (NCK + 1))
                    take_s(rb + 20)
                    for a in range(2):
                        ins = pe.transpose(misc[:, (rb + 20) % 2, SMP * a:SMP * a + SMP], hfS[:, P * a:P * a + P],
                                           ident[0:SMP, 0:SMP])
                    give(ins, rb + 20)
            pe.wait_ge(nO_ready, H)
            take(R_NOUT)
            for a in range(2):
                ins = pe.transpose(misc[0:HC, R_NOUT % 2, P * a:P * a + P], nO[:, a, :], ident[:, :])
            give(ins, R_NOUT)

            pe.wait_ge(wpool_in, 16)
            for g in range(PG):
                k = T_YP + g
                free_tile(k)
                wait_full(pe, d_in, g, inc=16)
                for c, (t0, t1) in enumerate(CH):
                    ins = pe.matmul(tile(k, c), wpool[:, g, :], dT[:, g % 2, t0:t1], start=True, stop=True)
                ins.then_inc(tile_full[k % 2], 1)
            for g in (PG - 2, PG - 1):
                wait_full(pe, tile_free, T_YP + g)
            with pe.Fori(0, 2) as i:
                for u in range(2):
                    halves(U_BP + u, i, 2)
                    for o in range(2):
                        k = T_BP + 2 * u + o
                        free_tile(k, i, 4)
                        for kk in range(PG):
                            products(k, U_BP + u, 256 * kk + P * o, kk, kk == PG - 1, yp_hi, yp_lo)
            pe.wait_ge(yml_ready, KT)
            with pe.Fori(0, 4) as i:
                for j in range(2):
                    unit(U_BM + j, T_BM + j, i, 2)
            two_units(U_OUT, T_OUT, m_ready)
            with pe.Fori(1, 4) as i:
                for j in range(2):
                    unit(U_OUT + j, T_OUT + j, i, 2)
            pe.wait_ge(xsum_ready, 1)
            col_sums(R_N2, ssq)
            pe.wait_ge(diag_ready, 2)
            sum_partitions(T_N2, sq)

            def ffn_pe(i, first=False, last=False):
                n, k = U_FFN + 1, T_FFN + 1
                ups = 3 if last else 4
                for j in range(1 if first else 0, ups):
                    unit(n + j, k + j, i, 6, tper=12)
                wait_full(pe, tile_free, k + 2, i, 12)
                for j in range(2):
                    halves(n + ups + j, i, 6)
                    for o in range(4):
                        t = k + ups + 4 * j + o
                        free_tile(t, i, 12)
                        for f in range(2):
                            products(t, n + ups + j, 512 * f + P * o, f, f == 1, a_hi, a_lo)

            two_units(U_FFN, T_FFN, h2_ready)
            ffn_pe(0, first=True)
            with pe.Fori(1, FI - 1) as i:
                ffn_pe(i)
            ffn_pe(FI - 1, last=True)

            pe.wait_ge(x2sum_ready, KT)
            col_sums(R_Y, ssq)
            pe.wait_ge(xg_ready, KT)
            for tt in range(TT):
                k, rows = T_Y + tt, P if tt < 8 else SMP
                if tt < 2:
                    free_tile(k)
                else:
                    pe.wait_ge(ytok_act, tt - 1)
                    pe.wait_ge(ytok_dve, tt - 1)
                for kk in range(KT):
                    ins = pe.transpose(dense[0:rows, 3 * (k % 2) + kk // 4, P * (kk % 4):P * (kk % 4) + P],
                                       hmT[:, kk, P * tt:P * tt + rows], ident[:, :])
                ins.then_inc(tile_full[k % 2], 1)


_INS = ['x_prompt', 'x_sample', 'c_prompt', 'c_sample', 'state_pool', 'state_mlstm_c', 'state_mlstm_n',
        'state_mlstm_m', 'g_mix', 'g_ffn', 'g_final', 'w_ada', 'b_ada', 'w_in', 'b_igate', 'b_fgate', 'w_pool',
        's_pool', 'g_head', 'w_branch_pool', 'w_branch_mlstm', 'w_out', 'w_gate_up', 'w_down']
_OUTS = [(1, SEQ, D), (NB, NT, D),
         (1, 1, HIST, PW), (1, 1, H, HD, HD), (1, 1, H, HD), (1, 1, H),
         (1, NB, HIST, PW), (1, NB, H, HD, HD), (1, NB, H, HD), (1, NB, H)]


def kernel(**inputs):
    import numpy as _np
    import concourse.bacc as _bacc
    from concourse import mybir as _mybir
    from concourse.bass_utils import run_bass_kernel_spmd as _run

    nc = _bacc.Bacc("TRN2", target_bir_lowering=False, num_devices=1)
    arrays, args = {}, []
    for name in _INS:
        a = _np.ascontiguousarray(inputs[name])
        arrays[f"in_{name}_dram"] = a
        args.append(nc.dram_tensor(f"in_{name}_dram", a.shape, _mybir.dt.from_np(a.dtype), kind="ExternalInput").ap())
    for i, shape in enumerate(_OUTS):
        args.append(nc.dram_tensor(f"out_{i}_dram", shape, _mybir.dt.float32, kind="ExternalOutput").ap())
    trunk(nc, *args)
    r = _run(nc, [arrays], core_ids=[0])
    return tuple(r.results[0][f"out_{i}_dram"] for i in range(len(_OUTS)))
```

```python
from contextlib import ExitStack

import concourse.bass as bass
from concourse import mybir

F32 = mybir.dt.float32
F32R = mybir.dt.float32r
ALU = mybir.AluOpType
ACT = mybir.ActivationFunctionType
ds = bass.ds

P = 128
D = 1024
KT = D // P
SEQ = 1024
NB, NT = 8, 8
SMP = NB * NT
T = SEQ + SMP
TT = 9
CH = ((0, 384), (384, 768), (768, T))
GRP = 1 + NB
PW = 512
PG = PW // P
HIST = 15
H = 4
HD = 256
CK = 128
NCK = SEQ // CK
HC = H * NCK
GL = CK + NT
E1 = HD + 1
FF = 2816
FT = FF // P
LEAD = 2
FI = FT // 2
EPS = 1e-6
NEG = -1e30
NA = 6 * KT
V_MIX, V_FFN, V_FIN, V_HEAD, V_POOL, V_ADA = 0, 8, 16, 24, 32, 36
NV = V_ADA + NA
SH1, SC1, GT1, SH2, SC2, GT2 = (KT * j for j in range(6))
Z_U, Z_Q, Z_K, Z_V, Z_O, Z_GP, Z_GM, Z_X, Z_D = 0, 4, 12, 20, 28, 36, 44, 52, 60
GATE_COL = PW + 4 * D
U_L1, U_L2, U_BP, U_BM, U_OUT, U_FFN = 1, 29, 53, 57, 65, 73
T_SS, T_GATE, T_L1, T_L2, T_YP, T_BP, T_BM, T_OUT, T_N2, T_FFN = 8, 9, 10, 38, 62, 66, 74, 82, 90, 91
T_Y = T_FFN + 6 * FT
R_CT, R_VEC, R_ADA = 0, 1, 2
ADA0 = 20
A_NORM = KT
R_SS = R_ADA + 2 * (A_NORM - 1)
R_L1 = R_ADA + ADA0 + 1
L1_CUTS = ((0, 2), (2, 4), (4, 6), (6, 8), (8, 14))
R_SEG = (R_L1, R_L1, R_L1 + 1, R_L1 + 2, R_L1 + 4)
R_GATES = R_L1 + 8
R_STAB = R_L1 + 13
R_COLS = R_L1 + 18
R_L2 = R_L1 + 32
RPC = 23
R_UT = R_L2 + NCK * RPC
R_SMP = R_UT + 2
RPH = 21
R_NOUT = R_SMP + H * RPH
R_N2 = R_NOUT + 1
R_Y = R_N2 + 1


def ada_rounds(a):
    r = R_ADA + 2 * a + (a >= A_NORM - 1)
    return r, r + 1


def last_tile(n):
    if n < U_BP:
        return n + T_GATE
    if n < U_BM:
        return T_BP + 2 * (n - U_BP) + 1
    if n < U_FFN:
        return n - U_BM + T_BM
    if n == U_FFN:
        return T_FFN
    q, r = divmod(n - U_FFN - 1, 6)
    ups = 4 if q < FI - 1 else 3
    return T_FFN + 1 + 12 * q + (r if r < ups else 4 * r - 3 * ups + 3)


def trunk(nc, x_prompt, x_sample, c_prompt, c_sample, state_pool, state_c, state_n, state_m,
          g_mix, g_ffn, g_final, w_ada, b_ada, w_in, b_igate, b_fgate, w_pool, s_pool, g_head,
          w_bp, w_bm, w_out, w_gu, w_down,
          y_prompt, y_sample, pool_p, c_p, n_p, m_p, pool_s, c_s, n_s, m_s):
    z = nc.dram_tensor("z_scratch", (64, P, T), F32).ap()
    gate_rows_p = nc.dram_tensor("gate_rows_p", (8, SEQ), F32).ap()
    gate_rows_s = nc.dram_tensor("gate_rows_s", (8, SMP), F32).ap()
    negg_dram = nc.dram_tensor("negg_rows", (HC, CK), F32).ap()
    tab_s_dram = nc.dram_tensor("tab_s", (5, HC, NT), F32).ap()
    decay_dram = nc.dram_tensor("decay_rows", (2, HC), F32).ap()

    top = ExitStack()
    with top:
        top.enter_context(nc.allow_non_contiguous_dma(reason="single columns of gates, stabilisers and normalisers"))
        def sem(name):
            return top.enter_context(nc.semaphore(name))

        def sb(stack, name, shape, dt=F32):
            return stack.enter_context(nc.sbuf_tensor(name, shape, dt))

        ident = sb(top, "ident", [P, P])
        ones = sb(top, "ones", [P, P])
        vec = sb(top, "vec", [P, NV])
        mod = sb(top, "mod", [P, NA, GRP])
        amp1 = sb(top, "amp1", [P, KT, GRP])
        amp2 = sb(top, "amp2", [P, KT, GRP])
        epsc = sb(top, "epsc", [P, 1])
        raw = sb(top, "raw", [P, 2, 1024])
        w_hi = sb(top, "w_hi", [P, 2, 1024], F32R)
        w_lo = sb(top, "w_lo", [P, 2, 1024], F32R)
        act_hi = sb(top, "act_hi", [P, KT, T], F32R)
        act_lo = sb(top, "act_lo", [P, KT, T], F32R)
        stage = sb(top, "stage", [P, 2, T])
        dec = sb(top, "dec", [P, 2, HC])
        colp = sb(top, "colp", [P, 4, HC])
        scol = sb(top, "scol", [SMP, 4, H])
        negg_s = sb(top, "negg_s", [SMP, H, SMP])
        gbias = sb(top, "gbias", [8, 1])
        mprev = sb(top, "mprev", [HC, 2])
        rcol = sb(top, "rcol", [P, TT])

        early = ExitStack()
        xtok = sb(early, "xtok", [P, TT, D])
        xn = xtok[:, :, :].rearrange("p j d -> p (j d)")[:, 0:KT * T].rearrange("p (k t) -> p k t", t=T)
        xT = sb(early, "xT", [P, KT, T])
        xsq = sb(early, "xsq", [P, 2, T])
        xssq = sb(early, "xssq", [P, T])
        ada_w = sb(early, "ada_w", [P, 2, KT, 256])
        cT = sb(early, "cT", [P, KT, GRP])
        vrow = sb(early, "vrow", [NV, P])
        hrow = sb(early, "hrow", [NB * HIST, PW])
        early.close()
        halved = ExitStack()
        sb(halved, "over_x", [P, TT * D + KT * T + 600])
        wa_hi = sb(halved, "wa_hi", [P, KT, 256], F32R)
        c_hl = sb(halved, "c_hl", [P, KT, 2 * GRP], F32R)
        ada_rows = sb(halved, "ada_rows", [2 * GRP, 256])
        sb(halved, "over_ada_slot0", [P, 3 * T - 600 - KT * 2 * GRP - 256])
        wa_lo = sb(halved, "wa_lo", [P, KT, 256], F32R)
        halved.close()
        h32 = stage
        cc, csig = stage[0:GRP, 0, 0:D], stage[0:GRP, 1, 0:D]
        mod_rows = negg_s[0:GRP, :, :].rearrange("p h t -> p (h t)")
        mixer = ExitStack()
        ext_p = sb(mixer, "ext_p", [P, PG, HIST + SEQ])
        ext_s = sb(mixer, "ext_s", [P, PG, NB, HIST + NT])
        win = sb(mixer, "win", [P, 2, HIST + SEQ])
        mixer.close()
        gtab = ExitStack()
        sb(gtab, "over_xtok", [P, TT * D])
        gates = sb(gtab, "gates", [8, T])
        tab = {n: sb(gtab, "tab_" + n, [HC, GL]) for n in
               ("ig", "fg", "abs", "exp", "ln", "lf", "b", "r", "cm", "g", "negg", "mt", "winter", "emt", "wend", "wend16")}
        zeros = sb(gtab, "zeros", [HC, GL])
        ngend = sb(gtab, "ngend", [HC, 2])
        rows2 = sb(gtab, "rows2", [1, 2, HC])
        mnext = sb(gtab, "mnext", [1, HC])
        mprow = sb(gtab, "mprow", [1, HC])
        invcnt = sb(gtab, "invcnt", [P, PG, 16])
        gtab.close()

        hmT = sb(top, "hmT", [P, KT, T])
        nrow = sb(top, "nrow", [HC, HD])
        ulast = sb(top, "ulast", [P, PG, HIST + SMP])
        warm = sb(top, "warm", [P, 1])
        mls = ExitStack()
        cst = sb(mls, "cst", [P, H, 2, E1])
        qkv = sb(mls, "qkv", [P, 2, 24, CK])
        neggb = sb(mls, "neggb", [P, 2, H, CK])
        mask = sb(mls, "mask", [P, CK])
        cur = sb(mls, "cur", [P, 2, 5, H])
        vext = sb(mls, "vext", [P, H, E1])
        wexp = sb(mls, "wexp", [P, 2, H, CK])
        pT = sb(mls, "pT", [P, H, CK])
        kw = sb(mls, "kw", [P, H, HD])
        hs = sb(mls, "hs", [P, H, E1])
        hn = sb(mls, "hn", [P, H, E1])
        hf = sb(mls, "hf", [P, H, HD])
        sm = sb(mls, "sm", [P, 8, H])
        mls.close()
        smp = ExitStack()
        kb = sb(smp, "kb", [SMP, NB, HD])
        hsS = sb(smp, "hsS", [SMP, E1])
        oin = sb(smp, "oin", [P, 2, T])
        qkvs = sb(smp, "qkvs", [P, 2, 6, SMP])
        qm = sb(smp, "qm", [P, NB, 2, SMP])
        argS = sb(smp, "argS", [SMP, 2, SMP])
        wexpS = sb(smp, "wexpS", [SMP, 2, SMP])
        pTS = sb(smp, "pTS", [SMP, SMP])
        ks = sb(smp, "ks", [SMP, HD])
        vs = sb(smp, "vs", [SMP, E1])
        hnS = sb(smp, "hnS", [SMP, E1])
        hfS = sb(smp, "hfS", [SMP, HD])
        curD = sb(smp, "curD", [P, 2, NB])
        curC = sb(smp, "curC", [SMP, 2, 4])
        wmask = sb(smp, "wmask", [SMP, 2, NB])
        smS = sb(smp, "smS", [SMP, 8])
        maskS = sb(smp, "maskS", [SMP, SMP])
        blk = sb(smp, "blk", [SMP, NB])
        nT = sb(smp, "nT", [P, 2, HC])
        nO = sb(smp, "nO", [P, 2, HC])
        nout = nrow
        urows = sb(smp, "urows", [HIST + SMP, PW])
        cs = [sb(smp, "cs0", [P, NB, 2, E1])]
        grp = ExitStack()
        wpool = sb(grp, "wpool", [P, PG, P])
        dT = sb(grp, "dT", [P, PG - 1, T])
        grp.close()
        cs.append(sb(smp, "cs1", [P, NB, 2, E1]))
        smp.close()
        YP0 = KT - PG
        sq = sb(top, "sq", [P, T])
        ssq = sb(top, "ssq", [P, T])
        ffn = ExitStack()
        a_hi = sb(ffn, "a_hi", [P, 2, T], F32R)
        a_lo = sb(ffn, "a_lo", [P, 2, T], F32R)
        a32 = sb(ffn, "a32", [P, 2, T])
        sil = sb(ffn, "sil", [P, T])
        gsm = sb(ffn, "gsm", [P, 2, SMP])
        ytok = sb(ffn, "ytok", [P, 2, D])
        ffn.close()

        dense = top.enter_context(nc.psum_tensor("dense", [P, 6, 512], F32))
        misc = top.enter_context(nc.psum_tensor("misc", [P, 2, 512], F32))

        def pair(name):
            return [sem(name + "0"), sem(name + "1")]

        consts_ready = sem("consts_ready")
        c_in = sem("c_in")
        small_in, nrow_in, ulast_in, wpool_in = sem("small_in"), sem("nrow_in"), sem("ulast_in"), sem("wpool_in")
        x_in = [sem(f"x_in{j}") for j in range(3)]
        raw_in, raw_free = pair("raw_in"), pair("raw_free")
        ada_in, ada_free = pair("ada_in"), pair("ada_free")
        chi_ready, c_ready = sem("chi_ready"), sem("c_ready")
        adahi_ready, ada_cut, mod_ready = sem("adahi_ready"), sem("ada_cut"), sem("mod_ready")
        hi_ready, table_loaded = sem("hi_ready"), sem("table_loaded")
        tile_full, tile_free = pair("tile_full"), pair("tile_free")
        round_full, round_free = pair("round_full"), pair("round_free")
        stage_out = pair("stage_out")
        csig_ready, silu_ready = sem("csig_ready"), sem("silu_ready")
        xsq_ready, ssq_ready, xn_ready = sem("xsq_ready"), sem("ssq_ready"), sem("xn_ready")
        std_ready, diag_ready, x_spilled = sem("std_ready"), sem("diag_ready"), sem("x_spilled")
        h32_ready, hhi_ready, h_ready = sem("h32_ready"), sem("hhi_ready"), sem("h_ready")
        dve_step, act_step, pool_step = sem("dve_step"), sem("act_step"), sem("pool_step")
        gates_ready, gates_out, gates_in = sem("gates_ready"), sem("gates_out"), sem("gates_in")
        lnterm_ready, cummax_ready, mprow_ready = sem("lnterm_ready"), sem("cummax_ready"), sem("mprow_ready")
        g_ready, gexp_ready, tables_ready = sem("g_ready"), sem("gexp_ready"), sem("tables_ready")
        tables_out, tables_in = sem("tables_out"), sem("tables_in")
        ext_in, d_out = sem("ext_in"), sem("d_out")
        qk_in, v_in, mls_init, chunk_prep = pair("qk_in"), pair("v_in"), sem("mls_init"), sem("chunk_prep")
        weights_exp = sem("weights_exp")
        msq_ready, hstd_ready, hf_ready = sem("msq_ready"), sem("hstd_ready"), sem("hf_ready")
        outs, state_out = sem("outs"), sem("state_out")
        head_rows_in, states_in, cs_out = pair("head_rows_in"), pair("states_in"), pair("cs_out")
        vs_init, head_prep, head_keys, head_kb = sem("vs_init"), sem("head_prep"), sem("head_keys"), sem("head_kb")
        pe_passed, pool_passed = sem("pe_passed"), sem("pool_passed")
        n_ready, nO_ready = sem("n_ready"), sem("nO_ready")
        d_in = [sem(f"d_in{g}") for g in range(PG)]
        yphi_ready = sem("yphi_ready")
        gin_in, oin_in = pair("gin_in"), pair("oin_in")
        yml32_ready, ymlhi_ready, yml_ready = sem("yml32_ready"), sem("ymlhi_ready"), sem("yml_ready")
        m32_ready, mhi_ready, m_ready = sem("m32_ready"), sem("mhi_ready"), sem("m_ready")
        xsum_ready, x1n_ready = sem("xsum_ready"), sem("x1n_ready")
        h2f_ready, h2hi_ready, h2_ready = sem("h2f_ready"), sem("h2hi_ready"), sem("h2_ready")
        sil_ready, a32_ready, ahi_ready = sem("sil_ready"), sem("a32_ready"), sem("ahi_ready")
        x2_ready, x2sq_ready, x2sum_ready = sem("x2_ready"), sem("x2sq_ready"), sem("x2sum_ready")
        rcol_ready, xg_ready = sem("rcol_ready"), sem("xg_ready")
        ytok_act, ytok_dve, y_out = sem("ytok_act"), sem("ytok_dve"), pair("y_out")

        def turn(k, i=0, per=0):
            assert per % 2 == 0
            return k % 2, k // 2 + i * (per // 2)

        def wait_full(eng, sems, k, i=0, per=0, inc=1):
            slot, n = turn(k, i, per)
            eng.wait_ge(sems[slot], n * inc + inc)

        def wait_free(eng, sems, k, i=0, per=0):
            slot, n = turn(k, i, per)
            if per or n:
                eng.wait_ge(sems[slot], n)

        def tile(k, c, lo=0, hi=None):
            return dense[:, 3 * (k % 2) + c, lo:CH[c][1] - CH[c][0] if hi is None else hi]

        def tile_wide(k):
            return dense[:, 3 * (k % 2):3 * (k % 2) + 2, 0:384]

        def wide(ap):
            return ap[:, 0:768].rearrange("p (c t) -> p c t", c=2)

        def bank(r, n=512, rows=P):
            return misc[0:rows, r % 2, 0:n]

        def smp3(ap):
            return ap.rearrange("p (b t) -> p b t", t=NT)

        def per_batch(ap):
            return ap.unsqueeze(2).to_broadcast([P, NB, NT])

        def row(ap3, k):
            return ap3[:, ds(k, 1), :].rearrange("p o t -> p (o t)")

        def zrow(k):
            return z[ds(k, 1)].rearrange("o p t -> (o p) t")

        vecs = ((V_MIX, g_mix[0]), (V_FFN, g_ffn[0]), (V_FIN, g_final), (V_HEAD, g_head[0]), (V_POOL, s_pool[0]),
                (V_ADA, b_ada[0]))
        small = 13 * 16

        block = top.enter_context(nc.Block())

        @block.sync
        def _(sp):
            def w_cols(w, col, n=P):
                return w[:, ds(col, n)].rearrange("(k p) n -> p k n", p=P)

            def load(n, src, i=0, per=0, kt=KT):
                wait_free(sp, raw_free, n, i, per)
                sp.dma_start(raw[:, n % 2, :].rearrange("p (k n) -> p k n", k=kt), src).then_inc(raw_in[n % 2], 16)

            def late_ada_load(j, i=0, per=0):
                a = ADA0 // 2 + j
                if per or j:
                    sp.wait_ge(ada_cut, i * per + j)
                else:
                    wait_free(sp, ada_free, a)
                sp.dma_start(ada_w[:, 0, :, :], w_cols(w_ada[0], i * (256 * per) + 256 * a, 256)
                             ).then_inc(ada_in[a % 2], 16)

            def ada_load(a, i=0, per=0):
                wait_free(sp, ada_free, a, i, per)
                sp.dma_start(ada_w[:, a % 2, :, :], w_cols(w_ada[0], i * (256 * per) + 256 * a, 256)
                             ).then_inc(ada_in[a % 2], 16)

            xp = x_prompt[0].rearrange("(j p) d -> p j d", p=P)
            sp.dma_start(xtok[:, 0:8, 0:512], xp[:, :, 0:512]).then_inc(x_in[0], 16)
            for r, v in vecs:
                n = v.shape[0] // P
                sp.dma_start(vrow[r:r + n, :], v.rearrange("(k p) -> k p", p=P)).then_inc(small_in, 16)
            sp.dma_start(xtok[0:SMP, 8, :], x_sample.rearrange("b t d -> (b t) d")).then_inc(x_in[2], 16)
            ada_load(0)
            sp.dma_start(xtok[:, 0:8, 512:1024], xp[:, :, 512:1024]).then_inc(x_in[1], 16)
            for a in range(1, ADA0 // 2):
                ada_load(a)
                if a in (5, 6):
                    load(a - 5, w_cols(w_in[0], GATE_COL if a == 5 else 0))
            late_ada_load(0)
            for j in range(2):
                load(2 + j, w_cols(w_in[0], P * (1 + j)))
            for s in range(2):
                sp.wait_ge(tile_free[s], KT // 2)
            sp.dma_start(z[Z_X:Z_X + KT].rearrange("k p t -> p k t"), xT[:, :, :]).then_inc(x_spilled, 16)

            late_ada_load(1)
            sp.wait_ge(gates_ready, 2)
            sp.dma_start(gate_rows_p, gates[:, 0:SEQ]).then_inc(gates_out, 16)
            sp.dma_start(gate_rows_s, gates[:, SEQ:T]).then_inc(gates_out, 16)
            sp.wait_ge(gates_out, 32)
            for n, h0 in (("ig", 0), ("fg", H)):
                sp.dma_start(tab[n][:, 0:CK], gate_rows_p[h0:h0 + H].rearrange("h (c t) -> (h c) t", t=CK)
                             ).then_inc(gates_in, 16)
                sp.dma_start(tab[n][:, CK:GL], gate_rows_s[h0:h0 + H].rearrange("h (c t) -> (h c) t", t=NT)
                             ).then_inc(gates_in, 16)

            def l1_loads(lo, hi):
                with sp.Fori(lo, hi) as i:
                    for j in range(2):
                        for n in (4 + 2 * j, 5 + 2 * j):
                            load(n, w_cols(w_in[0], i * (4 * P) + P * (n - U_L1)), i, 4)
                        late_ada_load(2 + j, i, 2)

            l1_loads(0, 4)
            sp.wait_ge(tables_ready, 1)
            sp.dma_start(negg_dram, tab["negg"][:, 0:CK]).then_inc(tables_out, 16)
            for j, n in enumerate(("r", "winter", "emt", "wend16", "negg")):
                sp.dma_start(tab_s_dram[j], tab[n][:, CK:GL]).then_inc(tables_out, 16)
            for j, col in enumerate((CK - 1, GL - 1)):
                sp.dma_start(decay_dram[j].rearrange("(r o) -> r o", o=1), tab["winter"][:, col:col + 1]
                             ).then_inc(tables_out, 16)
            for h in range(H):
                sp.dma_start(m_s[0, :, h:h + 1], tab["mt"][h * NB:(h + 1) * NB, GL - 1:GL]).then_inc(outs, 16)
            sp.dma_start(m_p[0], mnext[:, :].rearrange("p (h c) -> p h c", c=NCK)[:, :, NCK - 1]).then_inc(outs, 16)
            sp.wait_ge(tables_out, 8 * 16)
            sp.dma_start(dec[:, :, :].rearrange("p a r -> p (a r)"),
                         decay_dram.rearrange("a r -> (a r)").partition_broadcast(P)).then_inc(tables_in, 16)
            sp.dma_start(negg_s[:, :, :].rearrange("p h t -> p (h t)"),
                         tab_s_dram[4].rearrange("r t -> (r t)").partition_broadcast(SMP)).then_inc(tables_in, 16)
            for q in range(4):
                for h in range(H):
                    sp.dma_start(scol[:, q, h:h + 1],
                                 tab_s_dram[q, h * NB:(h + 1) * NB].rearrange("b (t o) -> (b t) o", o=1)
                                 ).then_inc(tables_in, 16)
            l1_loads(4, 6)
            load(28, w_cols(w_in[0], 27 * P))

            def l2_load(j, i=0, per=0):
                g = j // 2
                col = PW + 3 * D + g * D + (2 * H if g else 0) + P * (j % 2)
                load(U_L2 + j, w_cols(w_in[0], i * 256 + col), i, per)

            def qk_load(c, ci):
                sp.dma_start(qkv[:, c, 0:16, :], z[Z_Q:Z_V, :, ds(ci * CK, CK)].rearrange("j p t -> p j t")
                             ).then_inc(qk_in[c], 16)
                src = negg_dram.rearrange("(h c) t -> c h t", h=H)[ds(ci, 1)].rearrange("o h t -> (o h) t")
                sp.dma_start(neggb[:, c, :, :], src.partition_broadcast(P)).then_inc(qk_in[c], 16)

            def v_load(c, ci):
                sp.dma_start(qkv[:, c, 16:24, :], z[Z_V:Z_O, :, ds(ci * CK, CK)].rearrange("j p t -> p j t")
                             ).then_inc(v_in[c], 16)

            sp.wait_ge(x_spilled, 16)
            sp.wait_ge(tables_in, 18 * 16)
            sp.wait_ge(outs, 5 * 16)
            sp.wait_ge(d_out, 2 * PG * 16)
            for s in range(2):
                sp.wait_ge(stage_out[s], 10 * 16)
            for c in range(2):
                qk_load(c, c)
            for j in range(2):
                l2_load(j)
            for s in range(2):
                sp.wait_ge(stage_out[s], 14 * 16)
            for c in range(2):
                v_load(c, c)
            for j in range(2, 6):
                l2_load(j)
            sp.dma_start(nrow[:, :], state_n[0].rearrange("b h d -> (b h) d")).then_inc(nrow_in, 16)
            sp.dma_start(ulast[:, :, :], z[Z_U:Z_Q, :, SEQ - HIST:T].rearrange("g p t -> p g t")).then_inc(ulast_in, 16)
            with sp.Fori(1, 4) as i:
                for j in range(6):
                    l2_load(j, i, 6)
                    if j % 3 == 1:
                        wait_full(sp, round_full, R_L2 + RPC * (j // 3) + 17, i - 1, 2 * RPC)
                        qk_load(j // 3, i * 2 + j // 3)
                        v_load(j // 3, i * 2 + j // 3)

            def bp_src(n):
                return w_bp[0][:, 256 * (n - U_BP):256 * (n - U_BP) + 256].rearrange("(k p) n -> p k n", p=P)

            for n in (U_BP, U_BP + 1):
                load(n, bp_src(n), kt=PG)
            for r in (R_UT - 2, R_UT - 1):
                wait_full(sp, round_free, r)
            sp.dma_start(wpool[:, :, :], w_pool[0].rearrange("g c d -> c g d")).then_inc(wpool_in, 16)
            for g in range(PG - 1):
                sp.dma_start(dT[:, g, :], z[Z_D + g]).then_inc(d_in[g], 16)

            def head_rows(s, h):
                for g, zr in enumerate((Z_Q, Z_K, Z_V)):
                    sp.dma_start(qkvs[:, s, 2 * g:2 * g + 2, :],
                                 z[2 * h + zr:2 * h + zr + 2, :, SEQ:T].rearrange("j p t -> p j t")
                                 ).then_inc(head_rows_in[s], 16)

            def head_states(s, h):
                for b in range(NB):
                    sp.dma_start(cs[s][:, b, :, 0:HD], state_c[0, b, h].rearrange("(a p) e -> p a e", p=P)
                                 ).then_inc(states_in[s], 16)

            def head_store(s, h, b):
                for a in range(2):
                    wait_full(sp, round_free, R_SMP + RPH * h + 4 + 2 * b + a)
                sp.dma_start(c_s[0, b, h].rearrange("(a p) e -> p a e", p=P), cs[s][:, b, :, 0:HD]
                             ).then_inc(cs_out[s], 16)

            def gp_in(j):
                sp.wait_ge(stage_out[j % 2], (26 + j // 2) * 16)
                sp.dma_start(stage[:, j % 2, :], z[Z_GP + j]).then_inc(gin_in[j % 2], 16)

            def share_out(j):
                wait_full(sp, tile_free, T_BP + j)
                sp.dma_start(z[Z_GP + j], stage[:, j % 2, :]).then_inc(stage_out[j % 2], 16)

            head_rows(0, 0)
            wait_full(sp, tile_full, T_YP)
            sp.dma_start(dT[:, 0, :], z[Z_D + PG - 1]).then_inc(d_in[PG - 1], 16)
            head_states(0, 0)
            for h in range(H):
                sp.dma_start(c_p[0, 0, h].rearrange("(a p) e -> p a e", p=P), cst[:, h, :, 0:HD]).then_inc(state_out, 16)
                sp.dma_start(n_p[0, 0, h].rearrange("(a p o) -> p a o", p=P, o=1), cst[:, h, :, HD:E1]).then_inc(state_out, 16)
            for j in range(2):
                gp_in(j)
            for g in range(2, PG):
                wait_full(sp, tile_free, T_YP + g)
            head_rows(1, 1)
            head_states(1, 1)
            wait_full(sp, round_free, R_UT + 1)
            sp.dma_start(pool_p[0, 0], urows[0:HIST, :]).then_inc(outs, 16)
            for b in range(NB):
                sp.dma_start(pool_s[0, b, HIST - NT:HIST], urows[HIST + b * NT:HIST + (b + 1) * NT, :]).then_inc(outs, 16)
            sp.dma_start(pool_s[0, :, 0:HIST - NT], state_pool[0, :, NT:HIST]).then_inc(outs, 16)
            for j in range(2):
                sp.dma_start(oin[:, j, :], z[Z_O + j]).then_inc(oin_in[j], 16)
            for h in range(H):
                load(U_BP + 2 + h, *((bp_src(U_BP + 2 + h), 0, 0, PG) if h < 2 else (w_cols(w_bm[0], P * (h - 2)),)))
                for b in range(4):
                    head_store(h % 2, h, b)
                share_out(2 * h)
                if h + 1 < H:
                    gp_in(2 * h + 2)
                for b in range(4, NB):
                    head_store(h % 2, h, b)
                if h + 2 < H:
                    sp.wait_ge(cs_out[h % 2], NB * 16)
                    wait_full(sp, round_full, R_SMP + RPH * h + 20)
                    head_rows(h % 2, h + 2)
                    head_states(h % 2, h + 2)
                share_out(2 * h + 1)
                if h + 1 < H:
                    gp_in(2 * h + 3)
            for j in range(2, KT):
                sp.wait_ge(yml32_ready, j - 1)
                sp.dma_start(oin[:, j % 2, :], z[Z_O + j]).then_inc(oin_in[j % 2], 16)
                if j == 3:
                    wait_full(sp, round_free, R_NOUT)
                    sp.dma_start(n_s[0].rearrange("b h d -> (b h) d"), nout[:, :]).then_inc(outs, 16)

            def rows_in(k, src, i=0, per=0):
                wait_free(sp, tile_free, k, i, per)
                sp.dma_start(stage[:, k % 2, :], src).then_inc(gin_in[k % 2], 16)

            for s in range(2):
                sp.wait_ge(stage_out[s], 30 * 16)
            for j in range(KT):
                rows_in(T_BM + j, z[Z_GM + j])
                if j < 2:
                    sp.wait_ge(yml32_ready, KT - 1 + j)
                else:
                    sp.wait_ge(m32_ready, j - 1)
                sp.dma_start(oin[:, j % 2, :], z[Z_GP + j]).then_inc(oin_in[j % 2], 16)
                load(U_BM + 2 + j, w_cols((w_bm if j < 6 else w_out)[0], P * ((j + 2) % KT)))
            with sp.Fori(0, 3) as i:
                for j in range(2):
                    rows_in(T_OUT + j, zrow(i * 2 + (Z_X + j)), i, 2)
                    load(U_OUT + 2 + j, w_cols(w_out[0], i * 256 + P * (2 + j)), i, 2)
            for j in range(6, KT):
                rows_in(T_OUT + j, z[Z_X + j])

            def up_load(n, f, up, i, i_w, per):
                load(n, w_cols(w_gu[0], i_w * 256 + (P * f + FF * up)), i, per)

            def ffn_loads(i, last=False):
                n = U_FFN + 1
                for f, up in ((0, 1), (1, 0), (1, 1)):
                    up_load(n, f, up, i, i, 6)
                    n += 1
                if not last:
                    up_load(n, 0, 0, i, i + 1, 6)
                    n += 1
                for half in range(2):
                    load(n + half, w_down[0][ds(i * 256, 256), 512 * half:512 * half + 512].rearrange(
                        "(f p) n -> p f n", p=P), i, 6, kt=2)

            up_load(U_FFN, 0, 0, 0, 0, 0)
            with sp.Fori(0, FI - 1) as i:
                ffn_loads(i)
            ffn_loads(FI - 1, last=True)

            for tt in range(TT):
                sp.wait_ge(ytok_act, tt + 1)
                sp.wait_ge(ytok_dve, tt + 1)
                dst = y_prompt[0, tt * P:(tt + 1) * P] if tt < 8 else y_sample.rearrange("b t d -> (b t) d")
                sp.dma_start(dst, ytok[0:P if tt < 8 else SMP, tt % 2, :]).then_inc(y_out[tt % 2], 16)
            sp.wait_ge(y_out[0], 5 * 16)
            sp.wait_ge(y_out[1], 4 * 16)

        @block.gpsimd
        def _(pool):
            step = [0]

            def link(ins):
                step[0] += 1
                ins.then_inc(pool_step, 1)
                pool.wait_ge(pool_step, step[0])

            pool.memset(ones[:, :], 1.0).then_inc(consts_ready, 1)
            pool.memset(epsc[:, :], EPS).then_inc(consts_ready, 1)
            link(pool.memset(ident[:, :], 0.0))
            pool.affine_select(out=ident[:, :], in_=ident[:, :], compare_op=ALU.not_equal, fill=1.0,
                               base=0, pattern=[[-1, P]], channel_multiplier=1).then_inc(consts_ready, 1)

            for k in range(KT):
                pool.wait_ge(xsq_ready, k + 1)
                if k == 0:
                    pool.tensor_copy(xssq[:, :], xsq[:, 0, :]).then_inc(ssq_ready, 1)
                else:
                    pool.wait_ge(ssq_ready, k)
                    pool.tensor_tensor(xssq[:, :], xssq[:, :], xsq[:, k % 2, :], ALU.add).then_inc(ssq_ready, 1)
            wait_full(pool, tile_free, T_SS)
            for k in range(KT):
                pool.tensor_tensor(xn[:, k, :], xT[:, k, :], xssq[:, :], ALU.mult).then_inc(xn_ready, 1)

            pool.wait_ge(h_ready, KT)
            pool.wait_ge(x_spilled, 16)
            pool.memset(zeros[:, :], 0.0).then_inc(consts_ready, 1)
            for g in range(PG):
                for t in range(16):
                    last = pool.memset(invcnt[:, g, t:t + 1], 1.0 / min(t + 1, 2 << g))
            link(last)
            link(pool.memset(ext_p[:, :, 0:HIST], 0.0))
            for s in range(2):
                pool.wait_ge(stage_out[s], 2 * 16)
            for g in range(PG):
                pool.dma_start(ext_p[:, g, HIST:HIST + SEQ], z[Z_U + g, :, 0:SEQ]).then_inc(ext_in, 16)
                pool.dma_start(ext_s[:, g, :, HIST:HIST + NT], smp3(z[Z_U + g, :, SEQ:T])).then_inc(ext_in, 16)
            pool.wait_ge(ext_in, 2 * PG * 16)
            wait_full(pool, round_free, R_COLS + 1)
            for g in range(PG):
                for smp_part in (False, True):
                    n = HIST + (NT if smp_part else SEQ)
                    ext = ext_s[:, g, :, :] if smp_part else ext_p[:, g, :]
                    bufs = [win[:, s, 0:NB * n].rearrange("p (b t) -> p b t", b=NB) if smp_part else win[:, s, :]
                            for s in range(2)]

                    def cut(v, lo, hi):
                        return v[:, :, lo:hi] if smp_part else v[:, lo:hi]

                    src, span, turn_ = ext, 1, 0
                    while span < 2 << g:
                        dst, turn_ = bufs[turn_], 1 - turn_
                        link(pool.tensor_tensor(cut(dst, 2 * span - 1, n), cut(src, 2 * span - 1, n),
                                                cut(src, span - 1, n - span), ALU.add))
                        src, span = dst, 2 * span
                    dst = bufs[turn_]
                    if smp_part:
                        link(pool.tensor_scalar(cut(dst, HIST, n), cut(src, HIST, n), 1.0 / (2 << g), None, ALU.mult))
                    else:
                        pool.tensor_tensor(dst[:, HIST:HIST + 16], src[:, HIST:HIST + 16], invcnt[:, g, :], ALU.mult)
                        link(pool.tensor_scalar(dst[:, HIST + 16:n], src[:, HIST + 16:n], 1.0 / (2 << g), None, ALU.mult))
                    link(pool.tensor_tensor(cut(ext, HIST, n), cut(dst, HIST, n), cut(ext, HIST, n), ALU.subtract))
                pool.dma_start(z[Z_D + g, :, 0:SEQ], ext_p[:, g, HIST:HIST + SEQ]).then_inc(d_out, 16)
                pool.dma_start(smp3(z[Z_D + g, :, SEQ:T]), ext_s[:, g, :, HIST:HIST + NT]).then_inc(d_out, 16)
            pool.wait_ge(d_out, 2 * PG * 16)

            pool.wait_ge(tables_in, 18 * 16)
            pool.wait_ge(outs, 5 * 16)
            wait_full(pool, round_full, R_L2 - 2)
            link(pool.memset(mask[:, :], 0.0))
            link(pool.affine_select(out=mask[:, :], in_=mask[:, :], compare_op=ALU.is_ge, fill=NEG,
                                    base=0, pattern=[[1, CK]], channel_multiplier=-1))
            pool.memset(vext[:, :, HD:E1], 1.0).then_inc(mls_init, 1)
            pool.memset(cst[:, :, :, :], 0.0).then_inc(mls_init, 1)
            with pool.Fori(0, NCK // 2) as i:
                for c in range(2):
                    ci = i * 2 + c
                    for r in (21, 22):
                        wait_full(pool, round_free, R_L2 + RPC * c + r, i - 1, 2 * RPC)
                    pool.wait_ge(qk_in[c], i * 32 + 32)
                    pool.tensor_tensor(neggb[:, c, :, :], neggb[:, c, :, :],
                                       mask[:, :].unsqueeze(1).to_broadcast([P, H, CK]), ALU.add).then_inc(chunk_prep, 1)
                    pool.tensor_copy(cur[:, c, 0:4, :], colp[:, :, :].rearrange("p q (h c) -> p q h c", h=H)
                                     [:, :, :, ds(ci, 1)].rearrange("p q h o -> p q (h o)")).then_inc(chunk_prep, 1)
                    pool.tensor_copy(cur[:, c, 4, :], dec[:, 0, :].rearrange("p (h c) -> p h c", h=H)
                                     [:, :, ds(ci, 1)].rearrange("p h o -> p (h o)")).then_inc(chunk_prep, 1)

            for r in (R_UT - 2, R_UT - 1):
                wait_full(pool, round_free, r)
            pool.memset(vs[:, HD:E1], 1.0).then_inc(vs_init, 1)
            link(pool.memset(maskS[:, :], 0.0))
            m3 = smp3(maskS[:, :])
            link(pool.affine_select(out=m3, in_=m3, compare_op=ALU.is_ge, fill=NEG,
                                    base=0, pattern=[[NT, NB], [1, NT]], channel_multiplier=-1))
            link(pool.affine_select(out=m3, in_=m3, compare_op=ALU.is_ge, fill=NEG,
                                    base=0, pattern=[[-NT, NB], [0, NT]], channel_multiplier=1))
            link(pool.memset(blk[:, :], 1.0))
            link(pool.affine_select(out=blk[:, :], in_=blk[:, :], compare_op=ALU.is_ge, fill=0.0,
                                    base=0, pattern=[[-NT, NB]], channel_multiplier=1))
            link(pool.affine_select(out=blk[:, :], in_=blk[:, :], compare_op=ALU.is_ge, fill=0.0,
                                    base=NT - 1, pattern=[[NT, NB]], channel_multiplier=-1))
            link(pool.memset(qm[:, :, :, :], 0.0))
            base = step[0]
            with pool.Fori(0, H // 2) as i:
                for s in range(2):
                    h = i * 2 + s
                    wait_full(pool, round_full, R_SMP + 2 + (0 if s else RPH), i if s else i - 1, 2 * RPH)
                    pool.tensor_tensor(argS[:, s, :], row(negg_s, h), maskS[:, :], ALU.add).then_inc(head_prep, 1)
                    pool.tensor_copy(curD[:, s, :], dec[:, 1, ds(h * NB, NB)]).then_inc(head_prep, 1)
                    pool.tensor_copy(curC[:, s, :], scol[:, :, ds(h, 1)].rearrange("p q o -> p (q o)")
                                     ).then_inc(pool_step, 1)
                    pool.wait_ge(pool_step, h + (base + 1))
                    pool.sem_inc(pool_passed, 1)
                    pool.tensor_scalar(wmask[:, s, :], blk[:, :], curC[:, s, 3:4], None, ALU.mult
                                       ).then_inc(head_prep, 1)
                    pool.wait_ge(head_rows_in[s], i * (3 * 16) + 3 * 16)
                    pool.sem_inc(pool_passed, 1)
                    for b in range(NB):
                        pool.tensor_copy(qm[:, b, :, NT * b:NT * b + NT], qkvs[:, s, 0:2, NT * b:NT * b + NT]
                                         ).then_inc(head_prep, 1)
                    pool.wait_ge(state_out, 2 * H * 16)
                    pool.wait_ge(head_keys, h + 1)
                    pool.wait_ge(head_prep, h * 11 + 11)
                    pool.sem_inc(pool_passed, 1)
                    for b in range(NB):
                        pool.tensor_scalar(kb[:, b, :], ks[:, :], wmask[:, s, b:b + 1], None, ALU.mult
                                           ).then_inc(head_kb, 1)

            wait_full(pool, tile_free, T_N2)
            for k in range(2, KT):
                pool.wait_ge(h2f_ready, k - 1)
                pool.tensor_tensor((sil[:, :], a32[:, 0, :])[k % 2], hmT[:, k, :], ssq[:, :], ALU.mult
                                   ).then_inc(x1n_ready, 1)

            for k in range(KT):
                pool.wait_ge(x2sq_ready, k + 1)
                s = (sq, sil)[k % 2][:, :]
                if k == 0:
                    pool.tensor_copy(ssq[:, :], s).then_inc(x2sum_ready, 1)
                else:
                    pool.wait_ge(x2sum_ready, k)
                    pool.tensor_tensor(ssq[:, :], ssq[:, :], s, ALU.add).then_inc(x2sum_ready, 1)

        @block.scalar
        def _(act):
            def copy2(k, dst, func=ACT.Copy, scale=1.0, bias=None):
                kw_ = {} if bias is None else {"bias": bias}
                act.activation(wide(dst), tile_wide(k), func, scale=scale, **kw_)
                return act.activation(dst[:, 768:T], tile(k, 2), func, scale=scale, **kw_)

            def split_hi(n, i=0, per=0):
                wait_full(act, raw_in, n, i, per, inc=16)
                act.activation(w_hi[:, n % 2, :], raw[:, n % 2, :], ACT.Copy).then_inc(hi_ready, 1)

            def ada_high(j, i=0):
                wait_full(act, ada_in, ADA0 // 2 + j, i, 2, 16)
                act.activation(wa_hi[:, :, :], ada_w[:, 0, :, :], ACT.Copy).then_inc(adahi_ready, 1)

            def col_std(r):
                wait_full(act, round_full, r)
                act.activation(rcol[:, 0:8], bank(r, 8), ACT.Sqrt, scale=1.0 / D, bias=epsc[:, 0:1]).then_inc(std_ready, 1)
                act.activation(rcol[0:SMP, 8:9], bank(r, 9, SMP)[:, 8:9], ACT.Sqrt, scale=1.0 / D,
                               bias=epsc[0:SMP, 0:1]).then_inc(std_ready, 1)
                act.wait_ge(std_ready, 2 * (1 + (R_SS, R_N2, R_Y).index(r)))
                act.sem_inc(round_free[r % 2], 1)

            act.dma_start(cc[0:1, :], c_prompt).then_inc(c_in, 16)
            act.dma_start(cc[1:GRP, :], c_sample).then_inc(c_in, 16)
            act.dma_start(hrow[:, :], state_pool[0].rearrange("b t c -> (b t) c")).then_inc(small_in, 16)
            act.dma_start(gbias[0:H, :], b_igate[0].rearrange("(h o) -> h o", o=1)).then_inc(small_in, 16)
            act.dma_start(gbias[H:2 * H, :], b_fgate[0].rearrange("(h o) -> h o", o=1)).then_inc(small_in, 16)
            for h in range(H):
                act.dma_start(mprev[h * NB:(h + 1) * NB, 1:2], state_m[0, :, h:h + 1]).then_inc(small_in, 16)
            act.wait_ge(c_in, 2 * 16)
            act.activation(csig, cc, ACT.Sigmoid).then_inc(csig_ready, 1)

            def squares(k):
                wait_full(act, tile_full, k)
                if k >= 2:
                    act.wait_ge(ssq_ready, k - 1)
                copy2(k, xsq[:, k % 2, :], ACT.Square).then_inc(xsq_ready, 1)

            def h_high(k):
                act.wait_ge(h32_ready, k + 1)
                act.activation(act_hi[:, k, :], h32[:, k % 2, :], ACT.Copy).then_inc(hhi_ready, 1)

            squares(0)
            squares(1)
            act.wait_ge(consts_ready, 3)
            for a in range(ADA0 // 2):
                r0, r1 = ada_rounds(a)
                wait_full(act, round_full, r0)
                act.sem_inc(ada_free[a % 2], 1)
                if a == 0:
                    act.wait_ge(silu_ready, 1)
                act.activation(mod_rows, bank(r0, 256, GRP), ACT.Copy).then_inc(round_free[r0 % 2], 1)
                if a + 2 < KT:
                    squares(a + 2)
                if a == 0:
                    wait_full(act, round_free, R_VEC)
                wait_full(act, round_full, r1)
                for m in (2 * a, 2 * a + 1):
                    ins = act.activation(mod[:, m, :], bank(r1, 2 * GRP)[:, GRP * (m % 2):GRP * (m % 2) + GRP],
                                         ACT.Identity, bias=vec[:, V_ADA + m:V_ADA + m + 1])
                ins.then_inc(round_free[r1 % 2], 1)
                if a == A_NORM - 2:
                    col_std(R_SS)
                if a == A_NORM - 1:
                    wait_full(act, tile_full, T_SS)
                    copy2(T_SS, xssq[:, :]).then_inc(tile_free[T_SS % 2], 1)
                    split_hi(0)
                    split_hi(1)
                if a == A_NORM:
                    h_high(0)
            for k in range(1, KT):
                h_high(k)
            act.wait_ge(h_ready, KT)
            wait_full(act, round_free, R_CT)
            act.activation(c_hl[:, :, 0:GRP], cT[:, :, :], ACT.Copy).then_inc(chi_ready, 1)
            ada_high(0)
            act.wait_ge(small_in, small)
            wait_full(act, tile_full, T_GATE)
            act.wait_ge(x_spilled, 16)
            s = 3 * (T_GATE % 2)
            act.activation(wide(gates[:, :]), dense[0:8, s:s + 2, 0:384], ACT.Identity, bias=gbias[:, 0:1]
                           ).then_inc(gates_ready, 1)
            act.activation(gates[:, 768:T], dense[0:8, s + 2, 0:320], ACT.Identity, bias=gbias[:, 0:1]
                           ).then_inc(gates_ready, 1)
            act.wait_ge(gates_ready, 2)
            act.sem_inc(tile_free[T_GATE % 2], 1)
            split_hi(2)

            def evac(k, part, i=0, per=0, func=ACT.Copy):
                if part == 0:
                    wait_full(act, tile_full, k, i, per)
                    slot, m = turn(k - T_L1, i, per)
                    if per or m:
                        act.wait_ge(stage_out[slot], m * 16)
                    act.activation(wide(stage[:, k % 2, :]), tile_wide(k), func)
                else:
                    act.activation(stage[:, k % 2, 768:T], tile(k, 2), func).then_inc(tile_free[k % 2], 1)

            def store(k, dst, i=0, per=0):
                wait_full(act, tile_free, k, i, per)
                act.dma_start(dst, stage[:, k % 2, :]).then_inc(stage_out[k % 2], 16)

            def l1_part(part):
                lo, hi = L1_CUTS[part]
                rb = R_SEG[part]

                def body(j, i, per, last=False):
                    k = T_L1 + j
                    evac(k, 0, i, per)
                    evac(k, 1, i, per)
                    split_hi(U_L1 + j + 2, i, per)
                    store(k, zrow(i * 4 + j) if per else z[j], i, per)
                    if j % 2 == 0:
                        r = rb + j
                        wait_full(act, round_full, r, i, per)
                        act.activation(ada_rows[:, :], bank(r, 256, 2 * GRP), ACT.Copy).then_inc(round_free[r % 2], 1)
                        if not last or j == 0:
                            ada_high(1 + j // 2, i)

                if lo == 0:
                    for j in range(4):
                        body(j, 0, 0)
                    return
                end = part == len(L1_CUTS) - 1
                with act.Fori(lo // 2, hi // 2 - end) as i:
                    for j in range(4):
                        body(j, i, 4)
                if end:
                    for j in range(4):
                        body(j, hi // 2 - 1, 4, last=True)

            l1_part(0)
            act.wait_ge(gates_in, 4 * 16)
            act.activation(tab["abs"][:, :], tab["fg"][:, :], ACT.Abs).then_inc(act_step, 1)
            act.wait_ge(act_step, 1)
            act.activation(tab["exp"][:, :], tab["abs"][:, :], ACT.Exp, scale=-1.0).then_inc(act_step, 1)
            act.wait_ge(act_step, 2)
            act.activation(tab["ln"][:, :], tab["exp"][:, :], ACT.Ln, bias=1.0).then_inc(lnterm_ready, 1)
            l1_part(1)
            l1_part(2)
            act.wait_ge(g_ready, 1)
            for a, cols in enumerate((slice(0, CK), slice(CK, GL))):
                act.activation(tab["winter"][:, cols], tab["g"][:, cols], ACT.Exp, scale=-1.0, bias=mprev[:, a:a + 1]
                               ).then_inc(gexp_ready, 1)
                act.activation(tab["wend"][:, cols], tab["r"][:, cols], ACT.Exp, bias=ngend[:, a:a + 1]
                               ).then_inc(gexp_ready, 1)
            act.activation(tab["emt"][:, :], tab["mt"][:, :], ACT.Exp, scale=-1.0).then_inc(gexp_ready, 1)
            l1_part(3)
            l1_part(4)

            def l2_step(j, i, part):
                k = T_L2 + j
                if part < 2:
                    evac(k, part, i, 6, ACT.Sigmoid)
                if part == 2:
                    split_hi(U_L2 + j + 2, i, 6)
                if part == 3:
                    store(k, zrow(i * 2 + (Z_O + KT * (j // 2) + j % 2)), i, 6)

            def weights(c, i):
                ci = i * 2 + c
                act.wait_ge(chunk_prep, ci * 3 + 3)
                for h in range(H):
                    ins = act.activation(wexp[:, c, h, :], neggb[:, c, h, :], ACT.Exp, bias=cur[:, c, 0, h:h + 1])
                ins.then_inc(weights_exp, 1)

            def chunk_act(c, i, slot):
                ci = i * 2 + c
                rb = R_L2 + RPC * c
                if slot in (0, 1):
                    r = rb + 1 + slot
                    wait_full(act, round_full, r, i, 2 * RPC)
                    for a in range(2):
                        h = 2 * slot + a
                        ins = act.activation(kw[:, h, :], bank(r)[:, HD * a:HD * a + HD], ACT.Copy,
                                             scale=cur[:, c, 3, h:h + 1])
                    ins.then_inc(round_free[r % 2], 1)
                if 4 <= slot < 20 and slot % 4 == 0:
                    h = slot // 4 - 1
                    r = rb + 5 + 4 * h
                    wait_full(act, round_full, r, i, 2 * RPC)
                    act.activation(hs[:, h, :], bank(r, E1), ACT.Copy, scale=cur[:, c, 1, h:h + 1]
                                   ).then_inc(round_free[r % 2], 1)
                if slot in (18, 22):
                    act.activation(warm[:, :], epsc[:, :], ACT.Sqrt if slot == 18 else ACT.Exp).then_inc(table_loaded, 1)
                    act.wait_ge(table_loaded, ci * 2 + (1 if slot == 18 else 2))
                if slot == 20:
                    act.wait_ge(msq_ready, ci + 1)
                    act.activation(sm[:, 4, :], sm[:, 3, :], ACT.Sqrt, scale=1.0 / HD, bias=epsc[:, 0:1]
                                   ).then_inc(hstd_ready, 1)
                if slot == 23:
                    for a in range(2):
                        r = rb + 21 + a
                        wait_full(act, round_full, r, i, 2 * RPC)
                        act.activation(hmT[:, 4 * a:4 * a + 4, ds(ci * CK, CK)],
                                       bank(r).rearrange("p (j t) -> p j t", t=CK), ACT.Copy
                                       ).then_inc(round_free[r % 2], 1)

            def l2_act(i, last=False):
                for j in range(6):
                    if j == 3:
                        weights(1, i)
                    for s in range(8):
                        chunk_act(j // 3, i, (j % 3) * 8 + s)
                        if j:
                            l2_step(j - 1, i, s)
                if not last:
                    weights(0, i + 1)
                for s in range(4):
                    l2_step(5, i, s)

            weights(0, 0)
            with act.Fori(0, NCK // 2 - 1) as i:
                l2_act(i)
            l2_act(NCK // 2 - 1, last=True)

            for g in range(PG):
                k = T_YP + g
                sc = vec[:, V_POOL + g:V_POOL + g + 1]
                wait_full(act, tile_full, k)
                copy2(k, act_hi[:, YP0 + g, :], scale=sc).then_inc(yphi_ready, 1)

            with act.Fori(0, H // 2) as i:
                for s in range(2):
                    h = i * 2 + s
                    rb = R_SMP + RPH * s
                    act.wait_ge(head_prep, h * 11 + 11)
                    act.activation(wexpS[:, s, :], argS[:, s, :], ACT.Exp, bias=curC[:, s, 0:1]).then_inc(weights_exp, 1)
                    act.wait_ge(state_out, 2 * H * 16)
                    wait_full(act, round_full, rb + 2, i, 2 * RPH)
                    act.activation(hsS[:, :], bank(rb + 2, E1, SMP), ACT.Copy, scale=curC[:, s, 1:2]
                                   ).then_inc(round_free[(rb + 2) % 2], 1)
                    act.wait_ge(msq_ready, h + (NCK + 1))
                    act.activation(smS[:, 4:5], smS[:, 3:4], ACT.Sqrt, scale=1.0 / HD, bias=epsc[0:SMP, 0:1]
                                   ).then_inc(hstd_ready, 1)
                    wait_full(act, round_full, rb + 20, i, 2 * RPH)
                    act.activation(hmT[:, ds(h * 2, 2), SEQ:T], bank(rb + 20, 128).rearrange("p (j t) -> p j t", t=SMP),
                                   ACT.Copy).then_inc(round_free[(rb + 20) % 2], 1)
                    split_hi(U_BP + 2 + s, i, 2)

            with act.Fori(0, KT // 2) as i:
                for j in range(2):
                    kt = i * 2 + j
                    act.wait_ge(yml32_ready, kt + 1)
                    act.activation(row(act_hi, kt), row(hmT, kt), ACT.Copy).then_inc(ymlhi_ready, 1)
            with act.Fori(0, 3) as i:
                for j in range(2):
                    wait_full(act, tile_full, T_BM + j, i, 2)
                    split_hi(U_BM + 2 + j, i, 2)
            wait_full(act, tile_full, T_BM + 6)
            split_hi(U_OUT)
            wait_full(act, tile_full, T_BM + 7)
            for k in range(KT):
                act.wait_ge(m32_ready, k + 1)
                act.activation(act_hi[:, k, :], hmT[:, k, :], ACT.Copy).then_inc(mhi_ready, 1)
                if k == 1:
                    split_hi(U_OUT + 1)
            with act.Fori(0, 4) as i:
                for j in range(2):
                    wait_full(act, tile_full, T_OUT + j, i, 2)
                    split_hi(U_OUT + 2 + j, i, 2)
            col_std(R_N2)
            for k in range(KT):
                act.wait_ge(h2f_ready, k + 1)
                act.activation(act_hi[:, k, :], h32[:, k % 2, :], ACT.Copy).then_inc(h2hi_ready, 1)
                if k == 0:
                    act.wait_ge(x1n_ready, 2)
                    wait_full(act, tile_full, T_N2)
                    copy2(T_N2, ssq[:, :]).then_inc(tile_free[T_N2 % 2], 1)

            def silu(k, f, i, per=12):
                wait_full(act, tile_full, k, i, per)
                act.wait_ge(a32_ready, i * 2 + (f + 1))
                copy2(k, sil[:, :], ACT.Silu).then_inc(sil_ready, 1)

            def ffn_act(i, last=False):
                n, k = U_FFN + 1, T_FFN + 1
                for f in range(2):
                    if f:
                        silu(k + 1, 1, i)
                        split_hi(n + 3, i, 6)
                    wait_full(act, tile_full, k + 2 * f, i, 12)
                    act.wait_ge(a32_ready, i * 2 + (f + 2))
                    act.activation(a_hi[:, f, :], a32[:, f, :], ACT.Copy).then_inc(ahi_ready, 1)
                    split_hi(n + 2 * f + 2, i, 6)
                if last:
                    return
                wait_full(act, tile_full, k + 3, i, 12)
                act.wait_ge(a32_ready, i * 2 + 3)
                copy2(k + 3, sil[:, :], ACT.Silu).then_inc(sil_ready, 1)
                split_hi(n + 5, i, 6)
                for j in (4, 5):
                    wait_full(act, tile_full, last_tile(n + j), i, 12)
                    split_hi(n + j + 2, i, 6)

            silu(T_FFN, 0, 0, 0)
            split_hi(U_FFN + 2)
            with act.Fori(0, FI - 1) as i:
                ffn_act(i)
            ffn_act(FI - 1, last=True)

            for k in range(KT):
                act.wait_ge(x2_ready, KT * (FI - 1) + k + 1)
                if k >= 2:
                    act.wait_ge(x2sum_ready, k - 1)
                act.activation((sq, sil)[k % 2][:, :], hmT[:, k, :], ACT.Square).then_inc(x2sq_ready, 1)
                act.wait_ge(x2sq_ready, k + 1)
                act.activation(hmT[:, k, :], hmT[:, k, :], ACT.Copy, scale=vec[:, V_FIN + k:V_FIN + k + 1]
                               ).then_inc(xg_ready, 1)
            col_std(R_Y)
            act.wait_ge(rcol_ready, 3 * 2)
            for tt in range(TT):
                k, rows = T_Y + tt, P if tt < 8 else SMP
                wait_full(act, tile_full, k)
                if tt >= 2:
                    act.wait_ge(y_out[tt % 2], 16 * (tt // 2))
                act.activation(ytok[0:rows, tt % 2, 0:512], dense[0:rows, 3 * (k % 2), :], ACT.Copy,
                               scale=rcol[0:rows, tt:tt + 1]).then_inc(ytok_act, 1)

        @block.vector
        def _(dve):
            steps = [0, 0, None]

            def now():
                return steps[0] if steps[2] is None else steps[2] + steps[0]

            def link(ins):
                steps[0] += 1
                ins.then_inc(dve_step, 1)
                dve.wait_ge(dve_step, now())

            def enter(i, per):
                steps[1], steps[2] = steps[0], i * per

            def leave(n, per):
                assert steps[0] - steps[1] == per, (steps[0] - steps[1], per)
                steps[0], steps[2] = steps[1] + n * per, None

            def split_lo(n, i=0, per=0):
                dve.wait_ge(hi_ready, i * per + (n + 1))
                dve.tensor_tensor(w_lo[:, n % 2, :], raw[:, n % 2, :], w_hi[:, n % 2, :].bitcast(F32), ALU.subtract
                                  ).then_inc(raw_free[n % 2], 1)

            def norm_rows(k, xrows, amp, sh, done, used):
                o = h32[:, k % 2, :]
                if k >= 2:
                    dve.wait_ge(used, k - 1)
                link(dve.tensor_tensor(smp3(o[:, SEQ:T]), smp3(xrows[:, SEQ:T]), per_batch(amp[:, k, 1:GRP]), ALU.mult))
                dve.tensor_scalar(o[:, 0:SEQ], xrows[:, 0:SEQ], amp[:, k, 0:1], mod[:, sh + k, 0:1], ALU.mult, ALU.add)
                dve.tensor_tensor(smp3(o[:, SEQ:T]), smp3(o[:, SEQ:T]), per_batch(mod[:, sh + k, 1:GRP]), ALU.add
                                  ).then_inc(done, 1)

            def low_rows(k, src, hi_sem, out_sem):
                dve.wait_ge(hi_sem, k + 1)
                dve.tensor_tensor(act_lo[:, k, :], src, act_hi[:, k, :].bitcast(F32), ALU.subtract).then_inc(out_sem, 1)

            dve.sem_inc(a32_ready, 1)
            dve.wait_ge(csig_ready, 1)
            dve.tensor_tensor(cc, cc, csig, ALU.mult).then_inc(silu_ready, 1)

            def recip_cols(use):
                dve.wait_ge(std_ready, 2 * use)
                dve.reciprocal(rcol[:, 0:8], rcol[:, 0:8]).then_inc(rcol_ready, 1)
                dve.reciprocal(rcol[0:SMP, 8:9], rcol[0:SMP, 8:9]).then_inc(rcol_ready, 1)
                dve.wait_ge(rcol_ready, 2 * use)

            def diagonals(dst):
                for tt in range(TT):
                    n = P if tt < 8 else SMP
                    ins = dve.tensor_scalar(dst[:, P * tt:P * tt + n], ident[:, 0:n], rcol[:, tt:tt + 1], None, ALU.mult)
                ins.then_inc(diag_ready, 1)

            def take_x(k):
                wait_full(dve, tile_full, k)
                dve.wait_ge(xsq_ready, k + 1)
                dve.tensor_copy(wide(xT[:, k, :]), tile_wide(k))
                dve.tensor_copy(xT[:, k, 768:T], tile(k, 2)).then_inc(tile_free[k % 2], 1)

            link(dve.memset(rcol[:, :], 0.0))
            take_x(0)
            take_x(1)
            wait_full(dve, round_full, R_CT)
            dve.tensor_copy(cT[:, :, :].rearrange("p k g -> p (k g)"), bank(R_CT, KT * GRP)).then_inc(round_free[R_CT % 2], 1)
            wait_full(dve, round_full, R_VEC)
            dve.tensor_copy(vec[:, :], bank(R_VEC, NV)).then_inc(round_free[R_VEC % 2], 1)
            for k in range(2, KT):
                take_x(k)
            dve.wait_ge(consts_ready, 3)
            recip_cols(1)
            dve.wait_ge(ssq_ready, KT)
            diagonals(xsq[:, 0, :])
            for r in ada_rounds(A_NORM - 1):
                wait_full(dve, round_free, r)
            wait_full(dve, round_free, R_VEC)
            link(dve.scalar_tensor_tensor(out=amp1[:, :, :], in0=mod[:, SC1:SC1 + KT, :], scalar=1.0,
                                          in1=vec[:, V_MIX:V_MIX + KT].unsqueeze(2).to_broadcast([P, KT, GRP]),
                                          op0=ALU.add, op1=ALU.mult))
            split_lo(0)
            split_lo(1)
            for k in range(KT):
                dve.wait_ge(xn_ready, k + 1)
                norm_rows(k, xn[:, k, :], amp1, SH1, h32_ready, h_ready)
                if k:
                    low_rows(k - 1, h32[:, (k - 1) % 2, :], hhi_ready, h_ready)
            low_rows(KT - 1, h32[:, (KT - 1) % 2, :], hhi_ready, h_ready)
            def ada_low(j, i=0):
                dve.wait_ge(adahi_ready, i + (j + 1))
                dve.tensor_tensor(wa_lo[:, :, :], ada_w[:, 0, :, :], wa_hi[:, :, :].bitcast(F32), ALU.subtract
                                  ).then_inc(ada_cut, 1)

            dve.wait_ge(chi_ready, 1)
            dve.tensor_tensor(c_hl[:, :, GRP:2 * GRP], cT[:, :, :], c_hl[:, :, 0:GRP].bitcast(F32), ALU.subtract
                              ).then_inc(c_ready, 1)
            ada_low(0)
            split_lo(2)

            def l1_part(part):
                lo, hi = L1_CUTS[part]
                r = R_SEG[part] + 1

                def body(i, last=False):
                    split_lo(U_L1 + 2, i, 2)
                    if not last:
                        ada_low(1, i)
                        split_lo(U_L1 + 3, i, 2)
                    wait_full(dve, round_full, r, i, 2)
                    for col in range(2):
                        m = i * 2 + (ADA0 + col)
                        c0 = 2 * GRP * col
                        t = misc[:, r % 2, c0:c0 + 2 * GRP]
                        out = mod[:, ds(m, 1), :].rearrange("p o g -> p (o g)")
                        ins = dve.tensor_scalar(out, t[:, 0:GRP], vec[:, ds(m + V_ADA, 1)], None, ALU.add)
                        ins.then_inc(mod_ready, 1)
                        dve.wait_ge(mod_ready, i * 4 + (2 * col + 1))
                        ins = dve.tensor_tensor(out, out, t[:, GRP:2 * GRP], ALU.add)
                        ins.then_inc(mod_ready, 1)
                        dve.wait_ge(mod_ready, i * 4 + (2 * col + 2))
                    dve.sem_inc(round_free[r % 2], 1)

                end = part == len(L1_CUTS) - 1
                with dve.Fori(lo, hi - end) as i:
                    body(i)
                if end:
                    body(hi - 1, last=True)

            l1_part(0)
            parts = (slice(0, CK), slice(CK, GL))
            dve.wait_ge(lnterm_ready, 1)
            link(dve.scalar_tensor_tensor(out=tab["lf"][:, :], in0=tab["fg"][:, :], scalar=0.0, in1=tab["ln"][:, :],
                                          op0=ALU.min, op1=ALU.subtract))
            for cols in parts:
                link(dve.tensor_tensor_scan(tab["b"][:, cols], ones[0:HC, 0:cols.stop - cols.start], tab["lf"][:, cols],
                                            0.0, ALU.mult, ALU.add))
            link(dve.tensor_tensor(tab["r"][:, :], tab["ig"][:, :], tab["b"][:, :], ALU.subtract))
            dve.wait_ge(consts_ready, 4)
            for cols in parts:
                dve.tensor_tensor_scan(tab["cm"][:, cols], tab["r"][:, cols], zeros[:, cols], -3e38, ALU.max, ALU.add
                                       ).then_inc(cummax_ready, 1)
            l1_part(1)
            wait_full(dve, round_full, R_GATES)
            dve.tensor_copy(rows2[:, :, :].rearrange("p a r -> p (a r)"), bank(R_GATES, 2 * HC, 1)
                            ).then_inc(round_free[R_GATES % 2], 1)
            wait_full(dve, round_free, R_GATES)
            link(dve.memset(mprow[:, :], NEG))
            for h in range(H):
                c = slice(h * NCK, (h + 1) * NCK)
                link(dve.tensor_tensor_scan(mnext[:, c], rows2[:, 1, c], rows2[:, 0, c], NEG, ALU.max, ALU.add))
            dve.tensor_copy(mprow[:, :].rearrange("p (h c) -> p h c", h=H)[:, :, 1:NCK],
                            mnext[:, :].rearrange("p (h c) -> p h c", h=H)[:, :, 0:NCK - 1]).then_inc(mprow_ready, 1)
            l1_part(2)
            wait_full(dve, round_full, R_STAB)
            dve.tensor_copy(mprev[:, 0:1], bank(R_STAB, 1, HC)).then_inc(round_free[R_STAB % 2], 1)
            wait_full(dve, round_free, R_STAB)
            dve.wait_ge(small_in, small)
            dve.wait_ge(cummax_ready, 2)
            for a, cols in enumerate(parts):
                link(dve.tensor_scalar(tab["g"][:, cols], tab["cm"][:, cols], mprev[:, a:a + 1], None, ALU.max))
            link(dve.tensor_scalar(tab["negg"][:, :], tab["g"][:, :], -1.0, None, ALU.mult))
            for a, cols in enumerate(parts):
                link(dve.tensor_copy(ngend[:, a:a + 1], tab["negg"][:, cols.stop - 1:cols.stop]))
            dve.tensor_tensor(tab["mt"][:, :], tab["b"][:, :], tab["g"][:, :], ALU.add).then_inc(g_ready, 1)
            dve.wait_ge(gexp_ready, 5)
            dve.tensor_scalar(tab["wend16"][:, :], tab["wend"][:, :], HD ** -0.5, None, ALU.mult).then_inc(tables_ready, 1)
            l1_part(3)
            wait_full(dve, round_full, R_COLS)
            dve.tensor_copy(colp[:, :, :].rearrange("p q r -> p (q r)"), bank(R_COLS, 4 * HC)
                            ).then_inc(round_free[R_COLS % 2], 1)
            wait_full(dve, round_full, R_COLS + 1)
            dve.tensor_copy(ext_s[:, :, :, 0:HIST], bank(R_COLS + 1, PG * NB * HIST).rearrange(
                "p (g b t) -> p g b t", g=PG, b=NB)).then_inc(round_free[(R_COLS + 1) % 2], 1)
            l1_part(4)

            def chunk_dve(c, i, slot):
                ci = i * 2 + c
                rb = R_L2 + RPC * c
                per = 2 * RPC
                if slot == 0:
                    dve.wait_ge(weights_exp, ci + 1)
                    wait_full(dve, round_full, rb, i, per)
                    dve.scalar_tensor_tensor(out=pT[:, :, :].rearrange("p h t -> p (h t)"), in0=bank(rb),
                                             scalar=HD ** -0.5,
                                             in1=wexp[:, c, :, :].rearrange("p h t -> p (h t)"),
                                             op0=ALU.mult, op1=ALU.mult).then_inc(round_free[rb % 2], 1)
                if slot in (2, 3):
                    r = rb + 1 + slot
                    wait_full(dve, round_full, r, i, per)
                    dve.tensor_copy(vext[:, 2 * slot - 4:2 * slot - 2, 0:HD], bank(r).rearrange("p (h e) -> p h e", e=HD)
                                    ).then_inc(round_free[r % 2], 1)
                if 4 <= slot < 20:
                    h, q = slot // 4 - 1, slot % 4
                    r = rb + 5 + 4 * h + q
                    if q == 1:
                        wait_full(dve, round_free, r - 1, i, per)
                        wait_full(dve, round_full, r, i, per)
                        dve.tensor_tensor(hn[:, h, :], bank(r, E1), hs[:, h, :], ALU.add).then_inc(round_free[r % 2], 1)
                        wait_full(dve, round_free, r, i, per)
                        link(dve.tensor_tensor_reduce(out=hf[:, h, :], in0=hn[:, h, 0:HD], in1=hn[:, h, 0:HD], scale=1.0,
                                                      scalar=0.0, op0=ALU.mult, op1=ALU.add, accum_out=sm[:, 0, h:h + 1]))
                    if q >= 2:
                        wait_full(dve, round_full, r, i, per)
                        a = q - 2
                        dve.scalar_tensor_tensor(out=cst[:, h, a, :], in0=cst[:, h, a, :], scalar=cur[:, c, 4, h:h + 1],
                                                 in1=bank(r, E1), op0=ALU.mult, op1=ALU.add
                                                 ).then_inc(round_free[r % 2], 1)
                if slot == 20:
                    den = hn[:, :, HD]
                    link(dve.scalar_tensor_tensor(out=sm[:, 1, :], in0=den, scalar=-1.0, in1=den, op0=ALU.mult, op1=ALU.max))
                    link(dve.tensor_tensor(sm[:, 1, :], sm[:, 1, :], cur[:, c, 2, :], ALU.max))
                    link(dve.reciprocal(sm[:, 2, :], sm[:, 1, :]))
                    link(dve.tensor_tensor(sm[:, 3, :], sm[:, 0, :], sm[:, 2, :], ALU.mult))
                    dve.tensor_tensor(sm[:, 3, :], sm[:, 3, :], sm[:, 2, :], ALU.mult).then_inc(msq_ready, 1)
                    dve.wait_ge(hstd_ready, ci + 1)
                    link(dve.reciprocal(sm[:, 5, :], sm[:, 4, :]))
                    link(dve.tensor_tensor(sm[:, 6, :], sm[:, 5, :], sm[:, 2, :], ALU.mult))
                    for h in range(H):
                        ins = dve.tensor_scalar(hf[:, h, :], hn[:, h, 0:HD], sm[:, 6, h:h + 1], None, ALU.mult)
                    ins.then_inc(hf_ready, 1)

            chunk_steps = 2 * (H + 6)
            with dve.Fori(0, NCK // 2) as i:
                enter(i, chunk_steps)
                for j in range(6):
                    for s in range(8):
                        chunk_dve(j // 3, i, (j % 3) * 8 + s)
                        if s == 3:
                            split_lo(U_L2 + j + 1, i, 6)
                leave(NCK // 2, chunk_steps)

            wait_full(dve, round_full, R_UT)
            dve.tensor_copy(nT[:, :, :].rearrange("p a r -> p (a r)"), bank(R_UT, 2 * HC)).then_inc(round_free[R_UT % 2], 1)
            wait_full(dve, round_full, R_UT + 1)
            dve.tensor_copy(urows[:, :], bank(R_UT + 1, PW, HIST + SMP)).then_inc(round_free[(R_UT + 1) % 2], 1)
            wait_full(dve, round_free, R_UT)
            for g in range(PG):
                k = T_YP + g
                dve.wait_ge(yphi_ready, g + 1)
                sc = vec[:, V_POOL + g:V_POOL + g + 1]
                hi, lo = act_hi[:, YP0 + g, :].bitcast(F32), act_lo[:, YP0 + g, :]
                dve.scalar_tensor_tensor(out=wide(lo), in0=tile_wide(k), scalar=sc, in1=wide(hi),
                                         op0=ALU.mult, op1=ALU.subtract)
                dve.scalar_tensor_tensor(out=lo[:, 768:T], in0=tile(k, 2), scalar=sc, in1=hi[:, 768:T],
                                         op0=ALU.mult, op1=ALU.subtract).then_inc(tile_free[k % 2], 1)

            split_lo(U_BP + 1)

            def gated(k, dst, i, per):
                sg = stage[:, k % 2, :]
                wait_full(dve, tile_full, k, i, per)
                dve.tensor_tensor(wide(dst), tile_wide(k), wide(sg), ALU.mult)
                dve.tensor_tensor(dst[:, 768:T], tile(k, 2), sg[:, 768:T], ALU.mult).then_inc(tile_free[k % 2], 1)

            with dve.Fori(0, H // 2) as i:
                enter(i, 14)
                for s in range(2):
                    h = i * 2 + s
                    rb, per = R_SMP + RPH * s, 2 * RPH

                    def full(r):
                        wait_full(dve, round_full, rb + r, i, per)

                    def share(o):
                        wait_full(dve, gin_in, 2 * s + o, i, 4, 16)
                        gated(T_BP + 2 * s + o, stage[:, o, :], i, 4)

                    def by_head(ap):
                        return ap[:, :, :].rearrange("p a (b h) -> p b a h", h=H)[:, :, :, ds(h, 1)].rearrange(
                            "p b a o -> p b (a o)")

                    dve.wait_ge(states_in[s], i * (NB * 16) + NB * 16)
                    dve.tensor_copy(cs[s][:, :, :, HD], by_head(nT)).then_inc(n_ready, 1)
                    full(0)
                    dve.wait_ge(weights_exp, h + (NCK + 1))
                    dve.scalar_tensor_tensor(out=pTS[:, :], in0=bank(rb, SMP, SMP), scalar=HD ** -0.5,
                                             in1=wexpS[:, s, :], op0=ALU.mult, op1=ALU.mult
                                             ).then_inc(round_free[rb % 2], 1)
                    full(1)
                    dve.tensor_copy(ks[:, :], bank(rb + 1, HD, SMP)).then_inc(head_keys, 1)
                    dve.tensor_copy(vs[:, 0:HD], bank(rb + 1, 512, SMP)[:, HD:512]).then_inc(round_free[(rb + 1) % 2], 1)
                    wait_full(dve, round_free, rb + 2, i, per)
                    full(3)
                    dve.tensor_tensor(hnS[:, :], bank(rb + 3, E1, SMP), hsS[:, :], ALU.add
                                      ).then_inc(round_free[(rb + 3) % 2], 1)
                    wait_full(dve, round_free, rb + 3, i, per)
                    link(dve.tensor_tensor_reduce(out=hfS[:, :], in0=hnS[:, 0:HD], in1=hnS[:, 0:HD], scale=1.0,
                                                  scalar=0.0, op0=ALU.mult, op1=ALU.add, accum_out=smS[:, 0:1]))
                    den = hnS[:, HD:E1]
                    link(dve.scalar_tensor_tensor(out=smS[:, 1:2], in0=den, scalar=-1.0, in1=den, op0=ALU.mult, op1=ALU.max))
                    link(dve.tensor_tensor(smS[:, 1:2], smS[:, 1:2], curC[:, s, 2:3], ALU.max))
                    link(dve.reciprocal(smS[:, 2:3], smS[:, 1:2]))
                    link(dve.tensor_tensor(smS[:, 3:4], smS[:, 0:1], smS[:, 2:3], ALU.mult))
                    dve.tensor_tensor(smS[:, 3:4], smS[:, 3:4], smS[:, 2:3], ALU.mult).then_inc(msq_ready, 1)
                    for b in range(NB):
                        for a in range(2):
                            r = 4 + 2 * b + a
                            full(r)
                            dve.scalar_tensor_tensor(out=cs[s][:, b, a, :], in0=cs[s][:, b, a, :],
                                                     scalar=curD[:, s, b:b + 1], in1=bank(rb + r, E1),
                                                     op0=ALU.mult, op1=ALU.add).then_inc(round_free[(rb + r) % 2], 1)
                        if b == 4:
                            share(0)
                        if b == 1:
                            dve.wait_ge(hstd_ready, h + (NCK + 1))
                            link(dve.reciprocal(smS[:, 5:6], smS[:, 4:5]))
                            link(dve.tensor_tensor(smS[:, 6:7], smS[:, 5:6], smS[:, 2:3], ALU.mult))
                            dve.tensor_scalar(hfS[:, :], hnS[:, 0:HD], smS[:, 6:7], None, ALU.mult).then_inc(hf_ready, 1)
                    for r in (18, 19):
                        wait_full(dve, round_free, rb + r, i, per)
                    dve.tensor_copy(by_head(nO), cs[s][:, :, :, HD]).then_inc(nO_ready, 1)
                    share(1)
                    split_lo(U_BP + 2 + s, i, 2)
                leave(H // 2, 14)
            wait_full(dve, round_full, R_NOUT)
            dve.tensor_copy(nout[:, :], bank(R_NOUT, HD, HC)).then_inc(round_free[R_NOUT % 2], 1)

            for kt in range(KT):
                y = hmT[:, kt, :]
                wait_full(dve, oin_in, kt, inc=16)
                dve.scalar_tensor_tensor(out=y, in0=y, scalar=vec[:, V_HEAD + kt:V_HEAD + kt + 1], in1=oin[:, kt % 2, :],
                                         op0=ALU.mult, op1=ALU.mult).then_inc(yml32_ready, 1)
                if kt:
                    dve.wait_ge(yml32_ready, kt)
                    low_rows(kt - 1, hmT[:, kt - 1, :], ymlhi_ready, yml_ready)
            dve.wait_ge(yml32_ready, KT)
            low_rows(KT - 1, hmT[:, KT - 1, :], ymlhi_ready, yml_ready)
            def merged(i, j, between=None):
                k = T_BM + j
                kt = i * 2 + j
                m = row(hmT, kt)
                wait_full(dve, gin_in, KT + j, i, 2, 16)
                if between is None:
                    wait_full(dve, raw_free, U_BM + 1 + j, i, 2)
                gated(k, sq[:, :], i, 2)
                wait_full(dve, tile_free, k, i, 2)
                if between is not None:
                    between()
                wait_full(dve, oin_in, KT + j, i, 2, 16)
                dve.tensor_tensor(m, oin[:, j, :], sq[:, :], ALU.add).then_inc(m32_ready, 1)
                if between is None:
                    split_lo(U_BM + 2 + j, i, 2)

            def first_blocks():
                low_rows(0, hmT[:, 0, :], mhi_ready, m_ready)
                low_rows(1, hmT[:, 1, :], mhi_ready, m_ready)
                split_lo(U_OUT + 1)

            with dve.Fori(0, 3) as i:
                for j in range(2):
                    merged(i, j)
            merged(3, 0)
            dve.wait_ge(raw_free[U_OUT % 2], U_OUT // 2 + 1)
            merged(3, 1, first_blocks)
            for k in range(2, KT):
                low_rows(k, hmT[:, k, :], mhi_ready, m_ready)

            dve.wait_ge(outs, 16 * 16)
            for s in range(2):
                dve.wait_ge(cs_out[s], 2 * NB * 16)
            link(dve.memset(ssq[:, :], 0.0))
            def residual(i, j, first=False):
                k = T_OUT + j
                kt = i * 2 + j
                x1, xin = row(hmT, kt), stage[:, k % 2, :]
                gt = mod[:, ds(kt + GT1, 1), :].rearrange("p o g -> p (o g)")
                wait_full(dve, tile_full, k, i, 2)
                if first:
                    split_lo(U_OUT + 2 + j)
                wait_full(dve, gin_in, 16 + j, i, 2, 16)
                link(dve.tensor_tensor(smp3(gsm[:, 0, :]), smp3(tile(k, 2, 256, 320)), per_batch(gt[:, 1:GRP]), ALU.mult))
                dve.scalar_tensor_tensor(out=wide(x1), in0=tile_wide(k), scalar=gt[:, 0:1], in1=wide(xin),
                                         op0=ALU.mult, op1=ALU.add)
                dve.scalar_tensor_tensor(out=x1[:, 768:SEQ], in0=tile(k, 2, 0, 256), scalar=gt[:, 0:1],
                                         in1=xin[:, 768:SEQ], op0=ALU.mult, op1=ALU.add)
                dve.tensor_tensor(x1[:, SEQ:T], gsm[:, 0, :], xin[:, SEQ:T], ALU.add).then_inc(tile_free[k % 2], 1)
                wait_full(dve, tile_free, k, i, 2)
                link(dve.tensor_tensor(sq[:, :], x1, x1, ALU.mult))
                link(dve.tensor_tensor(ssq[:, :], ssq[:, :], sq[:, :], ALU.add))
                if not first:
                    split_lo(U_OUT + 2 + j, i, 2)

            for j in range(2):
                residual(0, j, first=True)
            with dve.Fori(0, 3) as i:
                enter(i, 6)
                for j in range(2):
                    residual(i + 1, j)
                leave(3, 6)
            dve.sem_inc(xsum_ready, 1)
            link(dve.scalar_tensor_tensor(out=amp2[:, :, :], in0=mod[:, SC2:SC2 + KT, :], scalar=1.0,
                                          in1=vec[:, V_FFN:V_FFN + KT].unsqueeze(2).to_broadcast([P, KT, GRP]),
                                          op0=ALU.add, op1=ALU.mult))
            recip_cols(2)
            diagonals(sq)
            for k in range(KT):
                s = (sil, a32[:, 0, :])[k % 2]
                s = s[:, :]
                if k < 2:
                    if k == 0:
                        wait_full(dve, tile_full, T_N2)
                    dve.tensor_tensor(wide(s), wide(hmT[:, k, :]), tile_wide(T_N2), ALU.mult)
                    dve.tensor_tensor(s[:, 768:T], hmT[:, k, 768:T], tile(T_N2, 2), ALU.mult).then_inc(x1n_ready, 1)
                dve.wait_ge(x1n_ready, k + 1)
                if k == 1:
                    low_rows(0, h32[:, 0, :], h2hi_ready, h2_ready)
                norm_rows(k, s, amp2, SH2, h2f_ready, h2_ready)
                if k > 1:
                    low_rows(k - 1, h32[:, (k - 1) % 2, :], h2hi_ready, h2_ready)
            low_rows(KT - 1, h32[:, (KT - 1) % 2, :], h2hi_ready, h2_ready)

            dve.wait_ge(h2_ready, KT)

            def silu_taken(k, m):
                dve.wait_ge(sil_ready, m)
                dve.sem_inc(tile_free[k % 2], 1)

            def ffn_dve(i, last=False):
                n, k = U_FFN + 1, T_FFN + 1
                for f in range(2):
                    if f:
                        silu_taken(k + 1, i * 2 + 2)
                        split_lo(n + 3, i, 6)
                    t = k + 2 * f
                    wait_full(dve, tile_full, t, i, 12)
                    dve.tensor_tensor(wide(a32[:, f, :]), tile_wide(t), wide(sil[:, :]), ALU.mult)
                    dve.tensor_tensor(a32[:, f, 768:T], tile(t, 2), sil[:, 768:T], ALU.mult).then_inc(a32_ready, 1)
                    dve.wait_ge(ahi_ready, i * 2 + (f + 1))
                    dve.tensor_tensor(a_lo[:, f, :], a32[:, f, :], a_hi[:, f, :].bitcast(F32), ALU.subtract
                                      ).then_inc(tile_free[t % 2], 1)
                    split_lo(n + 2 * f + 2, i, 6)
                t0 = k + 3
                if not last:
                    silu_taken(k + 3, i * 2 + 3)
                    split_lo(n + 5, i, 6)
                    t0 = k + 4
                for o in range(KT):
                    t = t0 + o
                    x1 = hmT[:, o, :]
                    gt = mod[:, GT2 + o, :]
                    wait_full(dve, tile_full, t, i, 12)
                    dve.scalar_tensor_tensor(out=wide(x1), in0=tile_wide(t), scalar=gt[:, 0:1], in1=wide(x1),
                                             op0=ALU.mult, op1=ALU.add)
                    dve.scalar_tensor_tensor(out=x1[:, 768:SEQ], in0=tile(t, 2, 0, 256), scalar=gt[:, 0:1],
                                             in1=x1[:, 768:SEQ], op0=ALU.mult, op1=ALU.add)
                    g = gsm[:, o % 2, :]
                    dve.tensor_tensor(smp3(g), smp3(tile(t, 2, 256, 320)), per_batch(gt[:, 1:GRP]), ALU.mult
                                      ).then_inc(tile_free[t % 2], 1)
                    wait_full(dve, tile_free, t, i, 12)
                    dve.tensor_tensor(x1[:, SEQ:T], g, x1[:, SEQ:T], ALU.add).then_inc(x2_ready, 1)
                    if o % 4 == 3 and not last:
                        split_lo(n + 6 + o // 4, i, 6)

            silu_taken(T_FFN, 1)
            split_lo(U_FFN + 2)
            with dve.Fori(0, FI - 1) as i:
                ffn_dve(i)
            ffn_dve(FI - 1, last=True)

            recip_cols(3)
            for tt in range(TT):
                k, rows = T_Y + tt, P if tt < 8 else SMP
                wait_full(dve, tile_full, k)
                if tt >= 2:
                    dve.wait_ge(y_out[tt % 2], 16 * (tt // 2))
                dve.tensor_scalar(ytok[0:rows, tt % 2, 512:1024], dense[0:rows, 3 * (k % 2) + 1, :],
                                  rcol[0:rows, tt:tt + 1], None, ALU.mult).then_inc(ytok_dve, 1)

        @block.tensor
        def _(pe):
            def one_pass(k, n, off, xr, p, first, last, x_hi, x_lo):
                w, x = ((w_hi, x_hi), (w_hi, x_lo), (w_lo, x_hi))[p]
                for c, (t0, t1) in enumerate(CH):
                    ins = pe.matmul(tile(k, c), w[:, n % 2, off:off + P], x[:, xr, t0:t1],
                                    start=(first and p == 0), stop=(last and p == 2))
                if last and p == 2:
                    ins.then_inc(tile_full[k % 2], 1)

            def products(k, n, off, kk, last, x_hi, x_lo):
                for p in range(3):
                    one_pass(k, n, off, kk, p, kk == 0, last, x_hi, x_lo)

            def halves(n, i=0, per=0):
                wait_full(pe, raw_free, n, i, per)

            def free_tile(k, i=0, per=0):
                wait_free(pe, tile_free, k, i, per)

            def take(r, i=0, per=0):
                wait_free(pe, round_free, r, i, per)

            def give(ins, r):
                ins.then_inc(round_full[r % 2], 1)

            def unit(n, k, i=0, per=0, between=None, tper=None):
                halves(n, i, per)
                free_tile(k, i, per if tper is None else tper)
                for kk in range(KT):
                    products(k, n, P * kk, kk, kk == KT - 1, act_hi, act_lo)
                    if between is not None:
                        between(kk)

            def two_units(n, k, ready):
                for kk in range(KT + LEAD):
                    for j, b in enumerate((kk, kk - LEAD)):
                        if not 0 <= b < KT:
                            continue
                        if b == 0:
                            halves(n + j)
                            free_tile(k + j)
                        if j == 0:
                            pe.wait_ge(ready, kk + 1)
                        products(k + j, n + j, P * b, b, b == KT - 1, act_hi, act_lo)

            def turn_x(k):
                if k % 4 == 0:
                    pe.wait_ge(x_in[k // 4], 16)
                free_tile(k)
                for j in range(TT):
                    rows = P if j < 8 else SMP
                    c = j // 3
                    ins = pe.transpose(tile(k, c, P * (j - 3 * c), P * (j - 3 * c) + rows),
                                       xtok[0:rows, j, P * k:P * k + P], ident[0:rows, 0:rows])
                ins.then_inc(tile_full[k % 2], 1)

            def sum_partitions(k, src):
                free_tile(k)
                for c, (t0, t1) in enumerate(CH):
                    ins = pe.matmul(tile(k, c), ones[:, :], src[:, t0:t1], start=True, stop=True)
                ins.then_inc(tile_full[k % 2], 1)

            def col_sums(r, src):
                take(r)
                for tt in range(TT):
                    rows = P if tt < 8 else SMP
                    ins = pe.matmul(misc[0:rows, r % 2, tt:tt + 1], src[:, P * tt:P * tt + rows], ones[:, 0:1],
                                    start=True, stop=True)
                give(ins, r)

            pe.wait_ge(consts_ready, 3)
            pe.wait_ge(x_in[2], 16)
            turn_x(0)
            turn_x(1)
            pe.wait_ge(silu_ready, 1)
            for k in range(KT):
                ins = pe.transpose(misc[:, R_CT % 2, GRP * k:GRP * k + GRP], stage[0:GRP, 0, P * k:P * k + P],
                                   ident[0:GRP, 0:GRP])
            give(ins, R_CT)
            pe.wait_ge(small_in, small)
            give(pe.transpose(bank(R_VEC, NV), vrow[:, :], ident[0:NV, 0:NV]), R_VEC)
            for a in range(ADA0 // 2):
                r0, r1 = ada_rounds(a)
                wait_full(pe, ada_in, a, inc=16)
                take(r0)
                for kk in range(KT):
                    ins = pe.matmul(bank(r0, 256, GRP), cT[:, kk, :], ada_w[:, a % 2, kk, :],
                                    start=(kk == 0), stop=(kk == KT - 1))
                give(ins, r0)
                if a + 2 < KT:
                    turn_x(a + 2)
                take(r1)
                wait_full(pe, round_free, r0)
                for col in range(2):
                    ins = pe.transpose(misc[:, r1 % 2, GRP * col:GRP * col + GRP], mod_rows[:, P * col:P * col + P],
                                       ident[0:GRP, 0:GRP])
                give(ins, r1)
                if a == A_NORM - 2:
                    pe.wait_ge(ssq_ready, KT)
                    col_sums(R_SS, xssq)
                if a == A_NORM - 1:
                    pe.wait_ge(diag_ready, 1)
                    sum_partitions(T_SS, xsq[:, 0, :])

            def ada_product(r, jt, i, per):
                pe.wait_ge(ada_cut, i * (per // 2) + (jt // 2 + 1))
                take(r, i, per)
                pe.sem_inc(pe_passed, 1)
                for kk in range(KT):
                    pe.matmul(bank(r, 256, 2 * GRP), c_hl[:, kk, :], wa_hi[:, kk, :], start=(kk == 0), stop=False)
                    ins = pe.matmul(bank(r, 256, GRP), c_hl[:, kk, 0:GRP], wa_lo[:, kk, :], start=False,
                                    stop=(kk == KT - 1))
                give(ins, r)

            def ada_turn(r, jt, i, per):
                take(r, i, per)
                wait_full(pe, round_free, r - 1, i, per)
                pe.sem_inc(pe_passed, 1)
                for col in range(2):
                    ins = pe.transpose(misc[:, r % 2, 2 * GRP * col:2 * GRP * (col + 1)],
                                       ada_rows[:, P * col:P * col + P], ident[0:2 * GRP, 0:2 * GRP])
                give(ins, r)

            two_units(0, T_GATE, h_ready)

            def l1_part(part):
                lo, hi = L1_CUTS[part]
                rb = R_SEG[part]

                def body(i, per):
                    for jt in range(4):
                        if jt or per:
                            unit(U_L1 + jt, T_L1 + jt, i, per)
                        (ada_turn if jt % 2 else ada_product)(rb + jt, jt, i, per)

                if lo == 0:
                    pe.wait_ge(c_ready, 1)
                    body(0, 0)
                    return
                with pe.Fori(lo // 2, hi // 2) as i:
                    body(i, 4)

            l1_part(0)
            l1_part(1)
            pe.wait_ge(cummax_ready, 2)
            take(R_GATES)
            for a, n in enumerate(("b", "cm")):
                ins = pe.matmul(misc[0:1, R_GATES % 2, HC * a:HC * a + HC], tab[n][:, CK - 1:CK], ident[0:HC, 0:HC],
                                start=True, stop=True)
            give(ins, R_GATES)
            l1_part(2)
            pe.wait_ge(mprow_ready, 1)
            take(R_STAB)
            give(pe.matmul(bank(R_STAB, 1, HC), mprow[0:1, :], ones[0:1, 0:1], start=True, stop=True), R_STAB)
            l1_part(3)
            pe.wait_ge(tables_ready, 1)
            take(R_COLS)
            for q, n in enumerate(("r", "winter", "emt", "wend16")):
                ins = pe.transpose(misc[:, R_COLS % 2, HC * q:HC * q + HC], tab[n][:, 0:CK], ident[0:HC, 0:HC])
            give(ins, R_COLS)
            take(R_COLS + 1)
            rows = NB * HIST
            for g in range(PG):
                ins = pe.transpose(misc[:, (R_COLS + 1) % 2, rows * g:rows * g + rows], hrow[:, P * g:P * g + P],
                                   ident[0:rows, 0:rows])
            give(ins, R_COLS + 1)
            l1_part(4)

            def chunk_pe(c, i, slot):
                rb, per = R_L2 + RPC * c, 2 * RPC
                q, k, v = (qkv[:, c, 8 * g:8 * g + 8, :] for g in range(3))

                def turned(src, r):
                    take(r, i, per)
                    for a in range(4):
                        ins = pe.transpose(bank(r)[:, P * a:P * a + P], src[:, a, :], ident[:, :])
                    give(ins, r)

                if slot == 0:
                    pe.wait_ge(qk_in[c], i * 32 + 32)
                    take(rb, i, per)
                    for h in range(H):
                        for a in range(2):
                            ins = pe.matmul(bank(rb)[:, CK * h:CK * h + CK], k[:, 2 * h + a, :], q[:, 2 * h + a, :],
                                            start=(a == 0), stop=(a == 1))
                    give(ins, rb)
                    turned(k[:, 0:4, :], rb + 1)
                if slot == 1:
                    turned(k[:, 4:8, :], rb + 2)
                if slot == 2:
                    pe.wait_ge(v_in[c], i * 16 + 16)
                if slot in (2, 3):
                    turned(v[:, 4 * slot - 8:4 * slot - 4, :], rb + 1 + slot)
                if 4 <= slot < 20:
                    h, p = slot // 4 - 1, slot % 4
                    r = rb + 5 + 4 * h + p
                    take(r, i, per)
                    if p == 0:
                        if h == 0:
                            pe.wait_ge(mls_init, 2)
                        for a in range(2):
                            ins = pe.matmul(bank(r, E1), q[:, 2 * h + a, :], cst[:, h, a, :], start=(a == 0), stop=(a == 1))
                    elif p == 1:
                        ins = pe.matmul(bank(r, E1), pT[:, h, :], vext[:, h, :], start=True, stop=True)
                    else:
                        ins = pe.matmul(bank(r, E1), kw[:, h, P * (p - 2):P * (p - 1)], vext[:, h, :], start=True, stop=True)
                    give(ins, r)
                if slot == 23:
                    pe.wait_ge(hf_ready, i * 2 + (c + 1))
                    for a in range(2):
                        turned(hf[:, 2 * a:2 * a + 2, :].rearrange("p h (a t) -> p (h a) t", a=2), rb + 21 + a)

            with pe.Fori(0, NCK // 2) as i:
                for j in range(6):
                    def between(kk, j=j):
                        chunk_pe(j // 3, i, (j % 3) * 8 + kk)
                    unit(U_L2 + j, T_L2 + j, i, 6, between)

            pe.wait_ge(nrow_in, 16)
            take(R_UT)
            for a in range(2):
                ins = pe.transpose(misc[:, R_UT % 2, HC * a:HC * a + HC], nrow[:, P * a:P * a + P], ident[0:HC, 0:HC])
            give(ins, R_UT)
            pe.wait_ge(ulast_in, 16)
            take(R_UT + 1)
            for g in range(PG):
                ins = pe.transpose(misc[0:HIST + SMP, (R_UT + 1) % 2, P * g:P * g + P], ulast[:, g, :], ident[:, :])
            give(ins, R_UT + 1)
            pe.wait_ge(wpool_in, 16)
            for g in range(PG):
                k = T_YP + g
                free_tile(k)
                pe.wait_ge(d_in[g], 16)
                for c, (t0, t1) in enumerate(CH):
                    ins = pe.matmul(tile(k, c), wpool[:, g, :], dT[:, g % (PG - 1), t0:t1], start=True, stop=True)
                ins.then_inc(tile_full[k % 2], 1)
            pe.wait_ge(vs_init, 1)
            with pe.Fori(0, H // 2) as i:
                for s in range(2):
                    rb, per = R_SMP + RPH * s, 2 * RPH
                    h = i * 2 + s

                    def take_s(r):
                        take(r, i, per)
                        pe.sem_inc(pe_passed, 1)

                    def branch(lo, hi):
                        n = U_BP + s
                        if lo == 0:
                            halves(n, i, 2)
                            if s == 0:
                                for g in (PG - 2, PG - 1):
                                    wait_full(pe, tile_free, T_YP + g)
                        for m in range(lo, hi):
                            o, kk, p = m // (3 * PG), m // 3 % PG, m % 3
                            if m % (3 * PG) == 0:
                                free_tile(T_BP + 2 * s + o, i, 4)
                            one_pass(T_BP + 2 * s + o, n, 256 * kk + P * o, YP0 + kk, p, kk == 0, kk == PG - 1,
                                     act_hi, act_lo)

                    qs, kks, vvs = (qkvs[:, s, 2 * g:2 * g + 2, :] for g in range(3))
                    pe.wait_ge(head_rows_in[s], i * (3 * 16) + 3 * 16)
                    take_s(rb)
                    for a in range(2):
                        ins = pe.matmul(bank(rb, SMP, SMP), kks[:, a, :], qs[:, a, :], start=(a == 0), stop=(a == 1))
                    give(ins, rb)
                    take_s(rb + 1)
                    for g, src in enumerate((kks, vvs)):
                        for a in range(2):
                            c0 = HD * g + P * a
                            ins = pe.transpose(misc[0:SMP, (rb + 1) % 2, c0:c0 + P], src[:, a, :], ident[:, :])
                    give(ins, rb + 1)
                    branch(0, 3)
                    pe.wait_ge(states_in[s], i * (NB * 16) + NB * 16)
                    pe.wait_ge(n_ready, h + 1)
                    pe.wait_ge(head_prep, h * 11 + 11)
                    take_s(rb + 2)
                    for b in range(NB):
                        for a in range(2):
                            ins = pe.matmul(bank(rb + 2, E1, SMP), qm[:, b, a, :], cs[s][:, b, a, :],
                                            start=(b == 0 and a == 0), stop=(b == NB - 1 and a == 1))
                    give(ins, rb + 2)
                    branch(3, 6)
                    take_s(rb + 3)
                    give(pe.matmul(bank(rb + 3, E1, SMP), pTS[:, :], vs[:, :], start=True, stop=True), rb + 3)
                    branch(6, 8)
                    for b in range(NB):
                        for a in range(2):
                            r = rb + 4 + 2 * b + a
                            if a == 0:
                                pe.wait_ge(head_kb, h * NB + (b + 1))
                            take_s(r)
                            give(pe.matmul(bank(r, E1), kb[:, b, P * a:P * a + P], vs[:, :], start=True, stop=True), r)
                            branch(8 + 2 * b + a, 9 + 2 * b + a)
                    pe.wait_ge(hf_ready, h + (NCK + 1))
                    take_s(rb + 20)
                    for a in range(2):
                        ins = pe.transpose(misc[:, (rb + 20) % 2, SMP * a:SMP * a + SMP], hfS[:, P * a:P * a + P],
                                           ident[0:SMP, 0:SMP])
                    give(ins, rb + 20)
            pe.wait_ge(nO_ready, H)
            take(R_NOUT)
            for a in range(2):
                ins = pe.transpose(misc[0:HC, R_NOUT % 2, P * a:P * a + P], nO[:, a, :], ident[:, :])
            give(ins, R_NOUT)

            two_units(U_BM, T_BM, yml_ready)
            with pe.Fori(1, 4) as i:
                for j in range(2):
                    unit(U_BM + j, T_BM + j, i, 2)
            two_units(U_OUT, T_OUT, m_ready)
            with pe.Fori(1, 4) as i:
                for j in range(2):
                    unit(U_OUT + j, T_OUT + j, i, 2)
            pe.wait_ge(xsum_ready, 1)
            col_sums(R_N2, ssq)
            pe.wait_ge(diag_ready, 2)
            sum_partitions(T_N2, sq)

            def ffn_pe(i, first=False, last=False):
                n, k = U_FFN + 1, T_FFN + 1
                ups = 3 if last else 4
                for j in range(1 if first else 0, ups):
                    unit(n + j, k + j, i, 6, tper=12)
                for j in range(2):
                    halves(n + ups + j, i, 6)
                    for o in range(4):
                        t = k + ups + 4 * j + o
                        free_tile(t, i, 12)
                        for f in range(2):
                            if j == 0 and o == 0 and f == 1:
                                wait_full(pe, tile_free, k + 2, i, 12)
                            products(t, n + ups + j, 512 * f + P * o, f, f == 1, a_hi, a_lo)

            two_units(U_FFN, T_FFN, h2_ready)
            ffn_pe(0, first=True)
            with pe.Fori(1, FI - 1) as i:
                ffn_pe(i)
            ffn_pe(FI - 1, last=True)

            pe.wait_ge(xg_ready, KT)
            for tt in range(TT):
                if tt == 2:
                    pe.wait_ge(x2sum_ready, KT)
                    col_sums(R_Y, ssq)
                k, rows = T_Y + tt, P if tt < 8 else SMP
                if tt < 2:
                    free_tile(k)
                else:
                    pe.wait_ge(ytok_act, tt - 1)
                    pe.wait_ge(ytok_dve, tt - 1)
                for kk in range(KT):
                    ins = pe.transpose(dense[0:rows, 3 * (k % 2) + kk // 4, P * (kk % 4):P * (kk % 4) + P],
                                       hmT[:, kk, P * tt:P * tt + rows], ident[:, :])
                ins.then_inc(tile_full[k % 2], 1)


_INS = ['x_prompt', 'x_sample', 'c_prompt', 'c_sample', 'state_pool', 'state_mlstm_c', 'state_mlstm_n',
        'state_mlstm_m', 'g_mix', 'g_ffn', 'g_final', 'w_ada', 'b_ada', 'w_in', 'b_igate', 'b_fgate', 'w_pool',
        's_pool', 'g_head', 'w_branch_pool', 'w_branch_mlstm', 'w_out', 'w_gate_up', 'w_down']
_OUTS = [(1, SEQ, D), (NB, NT, D),
         (1, 1, HIST, PW), (1, 1, H, HD, HD), (1, 1, H, HD), (1, 1, H),
         (1, NB, HIST, PW), (1, NB, H, HD, HD), (1, NB, H, HD), (1, NB, H)]


def kernel(**inputs):
    import numpy as _np
    import concourse.bacc as _bacc
    from concourse import mybir as _mybir
    from concourse.bass_utils import run_bass_kernel_spmd as _run

    nc = _bacc.Bacc("TRN2", target_bir_lowering=False, num_devices=1)
    arrays, args = {}, []
    for name in _INS:
        a = _np.ascontiguousarray(inputs[name])
        arrays[f"in_{name}_dram"] = a
        args.append(nc.dram_tensor(f"in_{name}_dram", a.shape, _mybir.dt.from_np(a.dtype), kind="ExternalInput").ap())
    for i, shape in enumerate(_OUTS):
        args.append(nc.dram_tensor(f"out_{i}_dram", shape, _mybir.dt.float32, kind="ExternalOutput").ap())
    trunk(nc, *args)
    r = _run(nc, [arrays], core_ids=[0])
    return tuple(r.results[0][f"out_{i}_dram"] for i in range(len(_OUTS)))
```
